# Optimizing a Trainium2 kernel written in Bass

```python
import math
import jax, jax.numpy as jnp
from jax import lax
import numpy as np

D_MODEL = 1024
BATCH = 1
SEQ = 512
DEPTH = 1

CHUNK = 64
Q_BLOCK = 128
MEM_LEN = 256
EPS = 1e-6
SSM_WIDTH = D_MODEL
SSM_GROUP = 16
SSM_GROUPS = SSM_WIDTH // SSM_GROUP
SSM_STATE = 64
DT_MIN = 1e-3
DT_MAX = 1e-1
DA_HEADS = 8
DA_HEAD_DIM = D_MODEL // (2 * DA_HEADS)
DA_V_DIM = 2 * DA_HEAD_DIM
DA_QK_WIDTH = DA_HEADS * 2 * DA_HEAD_DIM
DA_WIDTH = DA_HEADS * DA_V_DIM
ROPE_THETA = 10000.0
XA_HEADS = 4
XA_HEAD_DIM = D_MODEL // XA_HEADS
D_FF = 4 * D_MODEL
COL_SSM = SSM_WIDTH
COL_Q = COL_SSM + DA_QK_WIDTH
COL_K = COL_Q + DA_QK_WIDTH
COL_V = COL_K + DA_WIDTH
IN_COLS = COL_V + 2 * D_MODEL


F32 = jnp.float32

def rms_norm(x, g):
    xf = x.astype(F32)
    y = xf * lax.rsqrt(jnp.mean(xf * xf, axis=-1, keepdims=True) + EPS)
    return (y * g.astype(F32)).astype(x.dtype)

def rope_tables(seqlen, dim):
    inv = ROPE_THETA ** (-jnp.arange(0, dim, 2, dtype=F32) / dim)
    ang = jnp.arange(seqlen, dtype=F32)[:, None] * inv[None, :]
    return jnp.cos(ang), jnp.sin(ang)

def apply_rope(t, cos, sin):
    half = t.shape[-1] // 2
    c = cos[:, None, None, :]
    s = sin[:, None, None, :]
    t1, t2 = t[..., :half], t[..., half:]
    return jnp.concatenate([t1 * c - t2 * s, t2 * c + t1 * s], axis=-1)

def s5_branch(u, lam_re, lam_im, log_dt, b_re, b_im, c_re, c_im, d_skip):
    bsz, seqlen, _ = u.shape
    ug = u.astype(F32).reshape(bsz, seqlen, SSM_GROUPS, SSM_GROUP).astype(jnp.complex64)
    lam = lax.complex(lam_re.astype(F32), lam_im.astype(F32))
    dt = jnp.exp(log_dt.astype(F32))[:, None]
    lam_bar = jnp.exp(lam * dt)
    b = lax.complex(b_re.astype(F32), b_im.astype(F32))
    c = lax.complex(c_re.astype(F32), c_im.astype(F32))
    b_bar = ((lam_bar - 1.0) / lam)[..., None] * b
    bu = jnp.einsum('gph,blgh->lbgp', b_bar, ug)
    a = jnp.broadcast_to(lam_bar, (seqlen,) + lam_bar.shape)

    def combine(e_i, e_j):
        a_i, s_i = e_i
        a_j, s_j = e_j
        return a_j * a_i, a_j[:, None] * s_i + s_j

    _, states = lax.associative_scan(combine, (a, bu), axis=0)
    y = jnp.einsum('ghp,lbgp->blgh', c, states).real
    y = y.reshape(bsz, seqlen, SSM_WIDTH) + d_skip.astype(F32) * u.astype(F32)
    return y.astype(u.dtype)

def diff_attention(q, k, v, lq1, lk1, lq2, lk2, head_norm, lam_init):
    bsz, seqlen, _ = q.shape
    nb = seqlen // Q_BLOCK
    cos, sin = rope_tables(seqlen, DA_HEAD_DIM)
    q = apply_rope(q.astype(F32).reshape(bsz, seqlen, DA_HEADS, 2, DA_HEAD_DIM), cos, sin)
    k = apply_rope(k.astype(F32).reshape(bsz, seqlen, DA_HEADS, 2, DA_HEAD_DIM), cos, sin)
    q = jnp.transpose(q, (0, 2, 3, 1, 4))
    k = jnp.transpose(k, (0, 2, 3, 1, 4))
    vv = jnp.transpose(v.astype(F32).reshape(bsz, seqlen, DA_HEADS, DA_V_DIM), (0, 2, 1, 3))
    qblocks = jnp.moveaxis(q.reshape(bsz, DA_HEADS, 2, nb, Q_BLOCK, DA_HEAD_DIM), 3, 0)
    lam = (jnp.exp(jnp.sum(lq1.astype(F32) * lk1.astype(F32)))
           - jnp.exp(jnp.sum(lq2.astype(F32) * lk2.astype(F32))) + lam_init)
    scale = DA_HEAD_DIM ** -0.5
    k_chunk = jnp.arange(seqlen) // CHUNK

    def one_block(args):
        qb, bi = args
        s = jnp.einsum('bhcqd,bhckd->bhcqk', qb, k) * scale
        q_chunk = (bi * Q_BLOCK + jnp.arange(Q_BLOCK)) // CHUNK
        mask = k_chunk[None, :] <= q_chunk[:, None]
        s = jnp.where(mask, s, -jnp.inf)
        p = jax.nn.softmax(s, axis=-1)
        w = p[:, :, 0] - lam * p[:, :, 1]
        return jnp.einsum('bhqk,bhke->bhqe', w, vv)

    o = lax.map(one_block, (qblocks, jnp.arange(nb, dtype=jnp.int32)))
    o = jnp.transpose(o, (1, 0, 3, 2, 4)).reshape(bsz, seqlen, DA_HEADS, DA_V_DIM)
    o = o * lax.rsqrt(jnp.mean(o * o, axis=-1, keepdims=True) + EPS) * head_norm.astype(F32)
    o = o * (1.0 - lam_init)
    return o.reshape(bsz, seqlen, DA_WIDTH).astype(v.dtype)

def memory_cross_attention(h, mem_n, w_xq, w_xkv, w_xo):
    bsz, seqlen, _ = h.shape
    q = (h @ w_xq).reshape(bsz, seqlen, XA_HEADS, XA_HEAD_DIM)
    kv = mem_n @ w_xkv
    k, v = jnp.split(kv, 2, axis=-1)
    k = k.reshape(bsz, -1, XA_HEADS, XA_HEAD_DIM)
    v = v.reshape(bsz, -1, XA_HEADS, XA_HEAD_DIM)
    s = jnp.einsum('blhd,bmhd->bhlm', q, k).astype(F32) * (XA_HEAD_DIM ** -0.5)
    p = jax.nn.softmax(s, axis=-1)
    o = jnp.einsum('bhlm,bmhd->blhd', p, v.astype(F32)).astype(h.dtype)
    return o.reshape(bsz, seqlen, D_MODEL) @ w_xo

def first_inputs(seed: int = 0) -> dict:
    key = jax.random.key(seed)
    ks = iter(jax.random.split(key, 64))
    L = DEPTH

    def nrm(shape, scale):
        return scale * jax.random.normal(next(ks), shape, F32)

    def gain(width=D_MODEL):
        return 1.0 + nrm((L, width), 0.05)

    G, P, Hg = SSM_GROUPS, SSM_STATE, SSM_GROUP
    lam_im = jnp.broadcast_to(jnp.pi * jnp.arange(P, dtype=F32), (L, G, P))
    lam_re = -0.5 + jnp.clip(nrm((L, G, P), 0.01), -0.05, 0.05)
    log_dt = jax.random.uniform(next(ks), (L, G), F32, math.log(DT_MIN), math.log(DT_MAX))
    return {
        "x": nrm((BATCH, SEQ, D_MODEL), 1.0),
        "mem": nrm((BATCH, MEM_LEN, D_MODEL), 1.0),
        "norm_mix_pre": gain(),
        "w_in": nrm((L, D_MODEL, IN_COLS), D_MODEL ** -0.5),
        "b_gate": nrm((L, 2 * D_MODEL), 0.02),
        "ssm_lambda_re": lam_re,
        "ssm_lambda_im": lam_im,
        "ssm_log_dt": log_dt,
        "ssm_b_re": nrm((L, G, P, Hg), (2.0 * Hg) ** -0.5),
        "ssm_b_im": nrm((L, G, P, Hg), (2.0 * Hg) ** -0.5),
        "ssm_c_re": nrm((L, G, Hg, P), (2.0 * P) ** -0.5),
        "ssm_c_im": nrm((L, G, Hg, P), (2.0 * P) ** -0.5),
        "ssm_d": nrm((L, SSM_WIDTH), 1.0),
        "w_glu": nrm((L, SSM_WIDTH, SSM_WIDTH), SSM_WIDTH ** -0.5),
        "b_glu": nrm((L, SSM_WIDTH), 0.02),
        "w_ssm_proj": nrm((L, SSM_WIDTH, D_MODEL), SSM_WIDTH ** -0.5),
        "da_lambda_q1": nrm((L, DA_HEAD_DIM), 0.1),
        "da_lambda_k1": nrm((L, DA_HEAD_DIM), 0.1),
        "da_lambda_q2": nrm((L, DA_HEAD_DIM), 0.1),
        "da_lambda_k2": nrm((L, DA_HEAD_DIM), 0.1),
        "da_head_norm": gain(DA_V_DIM),
        "w_da_proj": nrm((L, DA_WIDTH, D_MODEL), DA_WIDTH ** -0.5),
        "w_mix_out": nrm((L, D_MODEL, D_MODEL), D_MODEL ** -0.5),
        "norm_mix_post": gain(),
        "norm_x_pre": gain(),
        "norm_mem": gain(),
        "w_xq": nrm((L, D_MODEL, D_MODEL), D_MODEL ** -0.5),
        "w_xkv": nrm((L, D_MODEL, 2 * D_MODEL), D_MODEL ** -0.5),
        "w_xo": nrm((L, D_MODEL, D_MODEL), D_MODEL ** -0.5),
        "norm_x_post": gain(),
        "norm_ff_pre": gain(),
        "w_ff1": nrm((L, D_MODEL, D_FF), D_MODEL ** -0.5),
        "w_ff2": nrm((L, D_FF, D_MODEL), D_FF ** -0.5),
        "norm_ff_post": gain(),
    }

def first_block(x, mem, norm_mix_pre, w_in, b_gate, ssm_lambda_re, ssm_lambda_im, ssm_log_dt,
              ssm_b_re, ssm_b_im, ssm_c_re, ssm_c_im, ssm_d, w_glu, b_glu, w_ssm_proj,
              da_lambda_q1, da_lambda_k1, da_lambda_q2, da_lambda_k2, da_head_norm, w_da_proj,
              w_mix_out, norm_mix_post, norm_x_pre, norm_mem, w_xq, w_xkv, w_xo, norm_x_post,
              norm_ff_pre, w_ff1, w_ff2, norm_ff_post):
    for l in range(DEPTH):
        lam_init = 0.8 - 0.6 * math.exp(-0.3 * l)
        h = rms_norm(x, norm_mix_pre[l])
        z = h @ w_in[l]
        u_s, q, k, v, g = jnp.split(z, [COL_SSM, COL_Q, COL_K, COL_V], axis=-1)
        ys = s5_branch(u_s, ssm_lambda_re[l], ssm_lambda_im[l], ssm_log_dt[l],
                       ssm_b_re[l], ssm_b_im[l], ssm_c_re[l], ssm_c_im[l], ssm_d[l])
        ys = jax.nn.gelu(ys)
        ys = ys * jax.nn.sigmoid(ys @ w_glu[l] + b_glu[l])
        branch_a = ys @ w_ssm_proj[l]
        ya = diff_attention(q, k, v, da_lambda_q1[l], da_lambda_k1[l], da_lambda_q2[l],
                            da_lambda_k2[l], da_head_norm[l], lam_init)
        branch_b = ya @ w_da_proj[l]
        gates = jax.nn.sigmoid((g + b_gate[l]).astype(F32))
        g_a, g_b = jnp.split(gates, 2, axis=-1)
        merged = (g_a * branch_a.astype(F32) + g_b * branch_b.astype(F32)).astype(x.dtype)
        x = x + rms_norm(merged @ w_mix_out[l], norm_mix_post[l])
        h = rms_norm(x, norm_x_pre[l])
        mem_n = rms_norm(mem, norm_mem[l])
        x = x + rms_norm(memory_cross_attention(h, mem_n, w_xq[l], w_xkv[l], w_xo[l]), norm_x_post[l])
        h = rms_norm(x, norm_ff_pre[l])
        f = jnp.square(jax.nn.relu(h @ w_ff1[l])) @ w_ff2[l]
        x = x + rms_norm(f, norm_ff_post[l])
    return x


DEPTH_2 = 2

N_BRANCH = 4
BRANCH_WIDTH = D_MODEL // N_BRANCH
HEAD_DIM = 64
NSA_HEADS = BRANCH_WIDTH // HEAD_DIM
NSA_CMP_LEN = 32
NSA_CMP_STRIDE = 16
NSA_CMP_HIDDEN = 2 * HEAD_DIM
NSA_SEL_LEN = 64
NSA_N_SEL = 16
NSA_WINDOW = 512
NSA_FORCE_BONUS = 1.0e4
POOL_WINDOWS = (2, 4, 8, 16)
POOL_GROUP = BRANCH_WIDTH // len(POOL_WINDOWS)
CONV_WIDTH = 3
FOX_HEADS = BRANCH_WIDTH // HEAD_DIM
ROPE_THETA_2 = 500000.0
ROPE_DIM = HEAD_DIM // 4
NORM_EPS = 1e-6
MASK_VALUE = -1e30

IN_SPLITS = (
    NSA_HEADS * HEAD_DIM,
    6 * HEAD_DIM,
    3 * NSA_HEADS,
    BRANCH_WIDTH,
    3 * BRANCH_WIDTH,
    3 * BRANCH_WIDTH,
    FOX_HEADS,
    N_BRANCH * BRANCH_WIDTH,
    N_BRANCH * D_MODEL,
)
D_IN = sum(IN_SPLITS)


def rmsnorm(x, g):
    xf = x.astype(jnp.float32)
    y = xf * lax.rsqrt(jnp.mean(xf * xf, axis=-1, keepdims=True) + NORM_EPS)
    return (y * g.astype(jnp.float32)).astype(x.dtype)

def rope(x, pos):
    half = ROPE_DIM // 2
    inv = ROPE_THETA_2 ** (-jnp.arange(half, dtype=jnp.float32) / half)
    ang = pos.astype(jnp.float32)[:, None] * inv[None, :]
    cos = jnp.cos(ang)[None, :, None, :].astype(x.dtype)
    sin = jnp.sin(ang)[None, :, None, :].astype(x.dtype)
    x1, x2, rest = x[..., :half], x[..., half:ROPE_DIM], x[..., ROPE_DIM:]
    return jnp.concatenate([x1 * cos - x2 * sin, x2 * cos + x1 * sin, rest], axis=-1)

def masked_softmax(s, mask):
    s = jnp.where(mask, s.astype(jnp.float32), MASK_VALUE)
    p = jax.nn.softmax(s, axis=-1)
    return jnp.where(mask, p, 0.0)

def to_blocks(a):
    B, T = a.shape[:2]
    a = a.reshape((B, T // Q_BLOCK, Q_BLOCK) + a.shape[2:])
    return jnp.moveaxis(a, 1, 0)

def from_blocks(a):
    a = jnp.moveaxis(a, 0, 1)
    return a.reshape((a.shape[0], a.shape[1] * a.shape[2]) + a.shape[3:])

def nsa_compress(k, pos_emb, w1, b1, w2, b2):
    B, T, hd = k.shape
    nc = (T - NSA_CMP_LEN) // NSA_CMP_STRIDE + 1
    idx = np.arange(nc)[:, None] * NSA_CMP_STRIDE + np.arange(NSA_CMP_LEN)[None, :]
    blocks = k[:, idx] + pos_emb
    flat = blocks.reshape(B, nc, NSA_CMP_LEN * hd)
    return jax.nn.silu(flat @ w1 + b1) @ w2 + b2

def nsa_mixer(q, kv, gate_logits, cmp_pos, cmp_w1, cmp_b1, cmp_w2, cmp_b2):
    B, T = q.shape[:2]
    pos = jnp.arange(T)
    q = rope(q.reshape(B, T, NSA_HEADS, HEAD_DIM), pos) * (HEAD_DIM ** -0.5)
    k_c, v_c, k_s, v_s, k_w, v_w = jnp.split(kv, 6, axis=-1)
    k_s = rope(k_s[:, :, None], pos)[:, :, 0]
    k_w = rope(k_w[:, :, None], pos)[:, :, 0]
    kc = nsa_compress(k_c, cmp_pos[0], cmp_w1[0], cmp_b1[0], cmp_w2[0], cmp_b2[0])
    vc = nsa_compress(v_c, cmp_pos[1], cmp_w1[1], cmp_b1[1], cmp_w2[1], cmp_b2[1])
    nc = kc.shape[1]
    cmp_end_np = np.arange(nc) * NSA_CMP_STRIDE + NSA_CMP_LEN - 1
    cmp_end = jnp.asarray(cmp_end_np)
    kc = rope(kc[:, :, None], cmp_end)[:, :, 0]
    n_blk = T // NSA_SEL_LEN
    n_sel = min(NSA_N_SEL, n_blk)
    ci = np.arange(nc)[:, None] * NSA_CMP_STRIDE
    sj = np.arange(n_blk)[None, :] * NSA_SEL_LEN
    overlap = jnp.asarray((ci < sj + NSA_SEL_LEN) & (ci + NSA_CMP_LEN > sj), jnp.float32)
    k_blk = k_s.reshape(B, n_blk, NSA_SEL_LEN, HEAD_DIM)
    v_blk = v_s.reshape(B, n_blk, NSA_SEL_LEN, HEAD_DIM)
    pad = ((0, 0), (NSA_WINDOW, 0), (0, 0))
    k_wp, v_wp = jnp.pad(k_w, pad), jnp.pad(v_w, pad)
    blk_ids = jnp.arange(n_blk)

    def one_block(args):
        qi, q_blk = args
        t = qi * Q_BLOCK + jnp.arange(Q_BLOCK)
        s = jnp.einsum('bqhd,bnd->bhqn', q_blk, kc)
        p_c = masked_softmax(s, (cmp_end[None, :] <= t[:, None])[None, None])
        o_cmp = jnp.einsum('bhqn,bnd->bqhd', p_c.astype(vc.dtype), vc)
        imp = jnp.einsum('bhqn,nj->bqj', p_c, overlap)
        jt = (t // NSA_SEL_LEN)[:, None]
        j = blk_ids[None, :]
        forced = (j == 0) | (j == jt) | (j == jt - 1)
        valid = j * NSA_SEL_LEN <= t[:, None]
        imp = jnp.where(valid, jnp.where(forced, imp + NSA_FORCE_BONUS, imp), MASK_VALUE)
        _, sel = lax.top_k(imp, n_sel)
        ks = jax.vmap(lambda kb, ib: kb[ib])(k_blk, sel)
        vs = jax.vmap(lambda vb, ib: vb[ib])(v_blk, sel)
        kpos = sel[..., None] * NSA_SEL_LEN + jnp.arange(NSA_SEL_LEN)
        m_s = (kpos <= t[None, :, None, None]).reshape(B, 1, Q_BLOCK, n_sel * NSA_SEL_LEN)
        s = jnp.einsum('bqhd,bqnkd->bhqnk', q_blk, ks).reshape(B, NSA_HEADS, Q_BLOCK, n_sel * NSA_SEL_LEN)
        p_s = masked_softmax(s, m_s).reshape(B, NSA_HEADS, Q_BLOCK, n_sel, NSA_SEL_LEN)
        o_slc = jnp.einsum('bhqnk,bqnkd->bqhd', p_s.astype(vs.dtype), vs)
        kw = lax.dynamic_slice_in_dim(k_wp, qi * Q_BLOCK, Q_BLOCK + NSA_WINDOW, axis=1)
        vw = lax.dynamic_slice_in_dim(v_wp, qi * Q_BLOCK, Q_BLOCK + NSA_WINDOW, axis=1)
        wpos = qi * Q_BLOCK - NSA_WINDOW + jnp.arange(Q_BLOCK + NSA_WINDOW)
        m_w = (wpos[None, :] <= t[:, None]) & (wpos[None, :] > t[:, None] - NSA_WINDOW) & (wpos[None, :] >= 0)
        s = jnp.einsum('bqhd,bkd->bhqk', q_blk, kw)
        p_w = masked_softmax(s, m_w[None, None])
        o_win = jnp.einsum('bhqk,bkd->bqhd', p_w.astype(vw.dtype), vw)
        return o_cmp, o_slc, o_win

    o_cmp, o_slc, o_win = lax.map(one_block, (jnp.arange(T // Q_BLOCK), to_blocks(q)))
    g = jax.nn.sigmoid(gate_logits.reshape(B, T, 3, NSA_HEADS))[..., None]
    o = (g[:, :, 0] * from_blocks(o_cmp) + g[:, :, 1] * from_blocks(o_slc)
         + g[:, :, 2] * from_blocks(o_win))
    return o.reshape(B, T, NSA_HEADS * HEAD_DIM)

def pool_mixer(u, pool_w, pool_scale):
    B, T, C = u.shape
    cs = jnp.concatenate([jnp.zeros((B, 1, C), jnp.float32),
                          jnp.cumsum(u.astype(jnp.float32), axis=1)], axis=1)
    outs = []
    for gi, w in enumerate(POOL_WINDOWS):
        sl = slice(gi * POOL_GROUP, (gi + 1) * POOL_GROUP)
        csg = cs[..., sl]
        lag = jnp.concatenate([jnp.zeros((B, w - 1, POOL_GROUP), jnp.float32),
                               csg[:, :T + 1 - w]], axis=1)
        cnt = jnp.minimum(jnp.arange(1, T + 1), w).astype(jnp.float32)[None, :, None]
        outs.append(((csg[:, 1:] - lag) / cnt).astype(u.dtype) - u[..., sl])
    pooled = jnp.stack(outs, axis=2)
    mixed = jnp.einsum('btgc,gcd->btgd', pooled, pool_w).reshape(B, T, C)
    return mixed * pool_scale

def conv_mixer(xin, b_gate, c_gate, conv_w):
    T = xin.shape[1]
    u = jnp.pad(c_gate * xin, ((0, 0), (CONV_WIDTH - 1, 0), (0, 0)))
    y = sum(u[:, k:k + T] * conv_w[k] for k in range(CONV_WIDTH))
    return b_gate * y

def fox_mixer(q, k, v, f_logit, f_bias):
    B, T = q.shape[:2]
    q = q.reshape(B, T, FOX_HEADS, HEAD_DIM) * (HEAD_DIM ** -0.5)
    k = k.reshape(B, T, FOX_HEADS, HEAD_DIM)
    v = v.reshape(B, T, FOX_HEADS, HEAD_DIM)
    logf = jax.nn.log_sigmoid(f_logit.astype(jnp.float32) + f_bias.astype(jnp.float32))
    c = jnp.cumsum(logf, axis=1)
    c_keys = jnp.transpose(c, (0, 2, 1))
    kpos = jnp.arange(T)

    def one_block(args):
        qi, q_blk, c_blk = args
        t = qi * Q_BLOCK + jnp.arange(Q_BLOCK)
        s = jnp.einsum('bqhd,bkhd->bhqk', q_blk, k).astype(jnp.float32)
        s = s + jnp.transpose(c_blk, (0, 2, 1))[..., None] - c_keys[:, :, None, :]
        p = masked_softmax(s, (kpos[None, :] <= t[:, None])[None, None])
        return jnp.einsum('bhqk,bkhd->bqhd', p.astype(v.dtype), v)

    o = lax.map(one_block, (jnp.arange(T // Q_BLOCK), to_blocks(q), to_blocks(c)))
    return from_blocks(o).reshape(B, T, FOX_HEADS * HEAD_DIM)

def hybrid_layer(x, norm_g, w_in, fox_f_bias, cmp_pos, cmp_w1, cmp_b1, cmp_w2, cmp_b2,
                 pool_w, pool_scale, conv_w, w_branch, w_out):
    B, T, _ = x.shape
    h = rmsnorm(x, norm_g)
    proj = h @ w_in
    split_at = np.cumsum(IN_SPLITS)[:-1].tolist()
    (nsa_q, nsa_kv, nsa_g, pool_in, conv_in, fox_qkv, fox_f,
     gate_in, merge_in) = jnp.split(proj, split_at, axis=-1)
    o_nsa = nsa_mixer(nsa_q, nsa_kv, nsa_g, cmp_pos, cmp_w1, cmp_b1, cmp_w2, cmp_b2)
    o_pool = pool_mixer(pool_in, pool_w, pool_scale)
    c_x, c_b, c_c = jnp.split(conv_in, 3, axis=-1)
    o_conv = conv_mixer(c_x, c_b, c_c, conv_w)
    f_q, f_k, f_v = jnp.split(fox_qkv, 3, axis=-1)
    o_fox = fox_mixer(f_q, f_k, f_v, fox_f, fox_f_bias)
    gates = gate_in.reshape(B, T, N_BRANCH, BRANCH_WIDTH)
    merge = merge_in.reshape(B, T, N_BRANCH, D_MODEL)
    acc = None
    for i, o in enumerate((o_nsa, o_pool, o_conv, o_fox)):
        branch = (o * jax.nn.silu(gates[:, :, i])) @ w_branch[i]
        term = jax.nn.sigmoid(merge[:, :, i]) * branch
        acc = term if acc is None else acc + term
    return x + acc @ w_out

def second_inputs(seed: int = 0) -> dict:
    key = jax.random.key(seed)
    ks = jax.random.split(key, 20)
    f32 = jnp.float32
    nrm = lambda k, shape, scale: jax.random.normal(k, shape, f32) * scale
    cmp_in = NSA_CMP_LEN * HEAD_DIM
    return {
        "x": nrm(ks[0], (BATCH, SEQ, D_MODEL), 1.0),
        "norm_g": 1.0 + nrm(ks[1], (DEPTH_2, D_MODEL), 0.05),
        "w_in": nrm(ks[2], (DEPTH_2, D_MODEL, D_IN), D_MODEL ** -0.5),
        "fox_f_bias": 3.0 + nrm(ks[3], (DEPTH_2, FOX_HEADS), 0.5),
        "cmp_pos": nrm(ks[4], (DEPTH_2, 2, NSA_CMP_LEN, HEAD_DIM), 0.1),
        "cmp_w1": nrm(ks[5], (DEPTH_2, 2, cmp_in, NSA_CMP_HIDDEN), cmp_in ** -0.5),
        "cmp_b1": nrm(ks[6], (DEPTH_2, 2, NSA_CMP_HIDDEN), 0.02),
        "cmp_w2": nrm(ks[7], (DEPTH_2, 2, NSA_CMP_HIDDEN, HEAD_DIM), NSA_CMP_HIDDEN ** -0.5),
        "cmp_b2": nrm(ks[8], (DEPTH_2, 2, HEAD_DIM), 0.02),
        "pool_w": nrm(ks[9], (DEPTH_2, len(POOL_WINDOWS), POOL_GROUP, POOL_GROUP), POOL_GROUP ** -0.5),
        "pool_scale": 1.0 + nrm(ks[10], (DEPTH_2, BRANCH_WIDTH), 0.1),
        "conv_w": nrm(ks[11], (DEPTH_2, CONV_WIDTH, BRANCH_WIDTH), CONV_WIDTH ** -0.5),
        "w_branch": nrm(ks[12], (DEPTH_2, N_BRANCH, BRANCH_WIDTH, D_MODEL), BRANCH_WIDTH ** -0.5),
        "w_out": nrm(ks[13], (DEPTH_2, D_MODEL, D_MODEL), D_MODEL ** -0.5),
        "final_norm_g": 1.0 + nrm(ks[14], (D_MODEL,), 0.05),
    }

def second_block(x, norm_g, w_in, fox_f_bias, cmp_pos, cmp_w1, cmp_b1, cmp_w2, cmp_b2,
              pool_w, pool_scale, conv_w, w_branch, w_out, final_norm_g):
    for l in range(DEPTH_2):
        x = hybrid_layer(x, norm_g[l], w_in[l], fox_f_bias[l], cmp_pos[l], cmp_w1[l],
                         cmp_b1[l], cmp_w2[l], cmp_b2[l], pool_w[l], pool_scale[l],
                         conv_w[l], w_branch[l], w_out[l])
    return rmsnorm(x, final_norm_g)


def setup_inputs(seed=0):
    out = dict(first_inputs(seed))
    for name, value in second_inputs(seed + 1).items():
        if name != "x":
            out[name + "_2"] = value
    return out


def reference(
    x, mem, norm_mix_pre, w_in, b_gate, ssm_lambda_re, ssm_lambda_im, ssm_log_dt, ssm_b_re,
    ssm_b_im, ssm_c_re, ssm_c_im, ssm_d, w_glu, b_glu, w_ssm_proj, da_lambda_q1, da_lambda_k1,
    da_lambda_q2, da_lambda_k2, da_head_norm, w_da_proj, w_mix_out, norm_mix_post, norm_x_pre,
    norm_mem, w_xq, w_xkv, w_xo, norm_x_post, norm_ff_pre, w_ff1, w_ff2, norm_ff_post, norm_g_2,
    w_in_2, fox_f_bias_2, cmp_pos_2, cmp_w1_2, cmp_b1_2, cmp_w2_2, cmp_b2_2, pool_w_2,
    pool_scale_2, conv_w_2, w_branch_2, w_out_2, final_norm_g_2,
):
    x = first_block(
        x, mem, norm_mix_pre, w_in, b_gate, ssm_lambda_re, ssm_lambda_im, ssm_log_dt, ssm_b_re,
        ssm_b_im, ssm_c_re, ssm_c_im, ssm_d, w_glu, b_glu, w_ssm_proj, da_lambda_q1,
        da_lambda_k1, da_lambda_q2, da_lambda_k2, da_head_norm, w_da_proj, w_mix_out,
        norm_mix_post, norm_x_pre, norm_mem, w_xq, w_xkv, w_xo, norm_x_post, norm_ff_pre, w_ff1,
        w_ff2, norm_ff_post,
    )
    return second_block(
        x, norm_g_2, w_in_2, fox_f_bias_2, cmp_pos_2, cmp_w1_2, cmp_b1_2, cmp_w2_2, cmp_b2_2,
        pool_w_2, pool_scale_2, conv_w_2, w_branch_2, w_out_2, final_norm_g_2,
    )


_drawn_inputs = setup_inputs


def setup_inputs(seed=0):
    import zlib

    import numpy as np

    out = dict(_drawn_inputs(seed))
    spreads = {}
    factors = {'b_gate': 8.0,
     'ssm_lambda_re': 64.0,
     'ssm_lambda_im': 26.776,
     'ssm_log_dt': 27.16,
     'ssm_b_re': 38.184,
     'ssm_b_im': 37.8,
     'ssm_c_re': 37.68,
     'ssm_c_im': 37.496,
     'b_glu': 8.0,
     'da_lambda_k2': 2.72,
     'fox_f_bias_2': 34.28,
     'cmp_pos_2': 7.67,
     'cmp_b1_2': 43.005,
     'cmp_b2_2': 25.975,
     'pool_scale_2': 2.956}
    for name, (base, spread) in spreads.items():
        noise = np.random.default_rng([zlib.crc32(name.encode()), seed]).standard_normal(out[name].shape)
        drawn = base * np.exp(spread * noise) if base else spread * noise
        out[name] = __import__('jax').numpy.asarray(drawn.astype(out[name].dtype))
    for name, factor in factors.items():
        out[name] = (out[name] * factor).astype(out[name].dtype)
    return out
```

```python
from contextlib import ExitStack

import numpy as np

import concourse.bass as bass
from concourse import mybir

F32 = mybir.dt.float32
ALU = mybir.AluOpType
ACT = mybir.ActivationFunctionType
AX = mybir.AxisListType

P = 128
D = 1024
T = 512
KT = D // P
TT = T // P
MEM = 256
EPS = 1e-6
MASKED = -1e30

HEADS = 8
DH = 64
GROUPS, STATE, GW = 64, 64, 16
PAIRS = GROUPS // 2
PPB = 4
LO, HI = 16, 32
LAM_INIT = 0.8 - 0.6
XH = 4
XD = D // XH

LAYERS = 2
NH = 4
CMP_LEN, CMP_STRIDE = 32, 16
NC = (T - CMP_LEN) // CMP_STRIDE + 1
NBR = 4

Q_U, Q_GB, Q_HEAD = 0, 2, 4
Q_GLU, Q_SSM, Q_DA, Q_MIX = 12, 14, 16, 18
Q_KX, Q_VX, Q_XQ, Q_XO = 20, 22, 24, 26
Q_FF1, Q_FF2, Q_L2 = 28, 36, 44
QL = 19
Q_END = Q_L2 + LAYERS * QL

V_MIX_PRE, V_BGATE, V_SSMD, V_BGLU, V_MIX_POST = 0, 8, 24, 32, 40
V_X_PRE, V_MEM, V_X_POST, V_FF_PRE, V_FF_POST = 48, 56, 64, 72, 80
V_HEADNORM, V_LQ1, V_LK1, V_LQ2, V_LK2, V_FINAL = 88, 89, 90, 91, 92, 93
V_LRE, V_LIM, V_LDT = 101, 133, 165
V_END = 197
L_NORM, L_POOL, L_CONV, L_FBIAS, L_B1, L_B2K = 0, 8, 10, 16, 17, 19
L_END = 20
C_ID, C_CAUSAL, C_CHUNK, C_SWAP = 0, 128, 256, 384
C_CMP = 512
C_VALID = 640
C_FQ, C_FK, C_NFK = 644, 645, 646
C_INV = 648
C_W = 680
C_END = 682


def build(nc, x_in, mem_in, weights, vecs, lvecs, consts, rope1, rope2, b_pad, c_pad,
          cmp_w1, cmp_pos, cmp_w2k, cmp_w2v, cmp_b2v, pool_w, out):
    ctx = ExitStack()
    with ctx:
        def sb(name, cols, rows=P):
            return ctx.enter_context(nc.sbuf_tensor(name, [rows, cols], F32))

        def sem(name):
            return ctx.enter_context(nc.semaphore(name))

        def sems(name, n):
            return [sem(f"{name}{i}") for i in range(n)]

        def blocks(ap, n, width=T):
            return ap.rearrange("p (k t) -> p k t", k=n, t=width)

        X = blocks(sb("residual", KT * T)[:, :], KT)
        H_ = sb("normed", KT * T)
        H = blocks(H_[:, :], KT)
        SLOTS = sb("weight_slots", 4 * KT * P)
        slot = [blocks(SLOTS[:, s * KT * P:(s + 1) * KT * P], KT, P) for s in range(4)]
        U_ = sb("u_region", KT * T)
        U = blocks(U_[:, :], KT)
        R = sb("wide_region", 32 * T)
        RB = blocks(R[:, :], 32)
        R3 = sb("work_region", 16 * T)
        WB = blocks(R3[:, :], 16)
        V_ = sb("v_region", KT * T)
        VB = blocks(V_[:, :], KT)
        TAB = sb("rope_tables", 2 * T)
        COS, SIN = TAB[:, 0:T], TAB[:, T:2 * T]
        EX = blocks(sb("attention_work", 11 * T)[:, :], 11)
        VEC = sb("vectors", V_END)
        LVEC = sb("layer_vectors", L_END)
        CON = sb("constants", C_END)
        SMALL = sb("small", 240)

        ident = CON[:, C_ID:C_ID + P]
        ones = SMALL[:, 0:1]
        VAR, R0, RT, RSTD = SMALL[:, 4:8], SMALL[:, 8:12], SMALL[:, 12:16], SMALL[:, 16:20]
        HALF = SMALL[:, 20:52]
        HVAR, HR0, HRT, HRS = (SMALL[:, 52 + 32 * i:84 + 32 * i] for i in range(4))
        NMAX, RSUM, RINV = SMALL[:, 180:184], SMALL[:, 184:188], SMALL[:, 188:192]
        LAMP, LAME, NLAM, HN08 = SMALL[:, 192:194], SMALL[:, 194:196], SMALL[:, 196:197], SMALL[:, 197:198]
        ONE_ROW = SMALL[0:1, 200:232]

        bank = [ctx.enter_context(nc.psum_tensor(f"bank{i}", [P, T], F32)) for i in range(8)]

        TMP = [WB[:, i, :] for i in range(4)]
        ROT = [[WB[:, 6 + 2 * d + c, :] for c in range(2)] for d in range(2)]
        SS = [[WB[:, 10 + 2 * d + c, :] for c in range(2)] for d in range(2)]
        PTMP = [WB[:, 14 + c, :] for c in range(2)]
        S5C = R[:, 24 * T:32 * T]
        CT = S5C[:, 0:2048].rearrange("p (n c m) -> p n c m", n=PAIRS, c=2)
        BL = [S5C[:, 2048 + 256 * q:2304 + 256 * q].rearrange("p (c m) -> p c m", c=2) for q in range(PPB)]
        CL = [S5C[:, 3072 + 256 * q:3328 + 256 * q].rearrange("p (c m) -> p c m", c=2) for q in range(PPB)]
        LOT = V_[:, 0:1024].rearrange("p (n c i) -> p n c i", n=PAIRS, c=2)
        HIT = V_[:, 1024:3072].rearrange("p (n c j) -> p n c j", n=PAIRS, c=2)
        PREP = V_[:, 3072:4096].rearrange("p (a n) -> p a n", a=32)
        RADIUS = PREP[:, 0, :]

        QRAW, QSW, KRAW, KSW, QH, KH, VH = (EX[:, i, :] for i in range(7))
        PR = [EX[:, 7, :], EX[:, 8, :]]
        PC = WB[:, 4, :]
        PTB = [EX[:, 9, :], EX[:, 10, :]]
        YA = RB[:, 16:24, :]
        YS2 = RB[:, 24:32, :]
        MG = WB[:, 0:8, :]
        SQ = WB[:, 8:16, :]
        MEMRAW, MEMN = blocks(H_[:, 0:2048], KT, MEM), blocks(H_[:, 2048:4096], KT, MEM)
        KX, VX = blocks(U_[:, 0:2048], KT, MEM), blocks(U_[:, 2048:4096], 2, D)
        HX, QX, OX = RB[:, 0:8, :], RB[:, 8:16, :], RB[:, 16:24, :]

        NQ, KS, KW, VSW = WB[:, 0:2, :], WB[:, 2, :], WB[:, 3, :], WB[:, 4, :]
        FQ, FK, FV = WB[:, 5:7, :], WB[:, 7:9, :], WB[:, 9:11, :]
        FCQ, FCK, KCVC = WB[:, 11, :], WB[:, 12, :], WB[:, 13, :]
        CW = R3[:, 14 * T:15 * T]
        G12 = CW[:, 0:64].rearrange("p (t g) -> p t g", t=TT)
        HID, KCR, KC, VC, KCT = CW[:, 64:128], CW[:, 128:128 + NC], CW[:, 160:160 + NC], CW[:, 192:256], CW[:, 256:320]
        RAW, RTMP = RB[:, 8:11, :], RB[:, 11:14, :]
        FZ, FL = RB[:, 14, :], RB[:, 15, :]
        FLAT = R[:, 16 * T:16 * T + CMP_LEN * NC].rearrange("p (l n) -> p l n", l=CMP_LEN)
        LW = R[:, 18 * T:20 * T]
        W2K, W2V, B2V, POS = LW[:, 0:128], LW[:, 128:192], LW[0:1, 192:256], LW[:, 256:288]
        PW = LW[:, 288:544].rearrange("p (b n) -> p b n", b=2)
        PA, PB = R[:, 20 * T:20 * T + 528], R[:, 20 * T + 528:20 * T + 1056]
        CP = R[:, 20 * T + 1056:20 * T + 1570]
        W1 = R[:, 24 * T:32 * T].rearrange("p (l n) -> p l n", l=CMP_LEN)
        PIN, CX, CB, CC = RB[:, 0:2, :], RB[:, 2:4, :], RB[:, 4:6, :], RB[:, 6:8, :]
        OBR = VB

        w_full, mm_done, evac_done = sems("w_full", 4), sems("mm_done", 4), sems("evac_done", 4)
        x_loaded, consts_in, mem_loaded, rope2_in, out_stored = (
            sem("x_loaded"), sem("consts_in"), sem("mem_loaded"), sem("rope2_in"), sem("out_stored"))
        const_ready = sem("const_ready")
        sq_ready, ms_ready, var_ready = sem("sq_ready"), sem("ms_ready"), sem("var_ready")
        rstd_ready, bc_ready, bc_used = sem("rstd_ready"), sem("bc_ready"), sem("bc_used")
        x_ready = sem("x_ready")
        cl_zero, prep_dt, prep_exp, prep_arg, prep_sin, prep_done = (
            sem("cl_zero"), sem("prep_dt"), sem("prep_exp"), sem("prep_arg"), sem("prep_sin"), sem("prep_done"))
        ct_in = sem("ct_in")
        bl_full = sems("bl_full", PPB)
        bu_ready, bu_used, tab_ready, ss_ready = sem("bu_ready"), sem("bu_used"), sem("tab_ready"), sem("ss_ready")
        cl_ready, y_done, y_used = sem("cl_ready"), sem("y_done"), sem("y_used")
        lam_prod, lam_sum, lam_exp = sem("lam_prod"), sem("lam_sum"), sem("lam_exp")
        rope_done, da_scores, da_max, da_exp = sem("rope_done"), sem("da_scores"), sem("da_max"), sem("da_exp")
        da_probs, da_turned, da_copied, da_pv, da_out = (
            sem("da_probs"), sem("da_turned"), sem("da_copied"), sem("da_pv"), sem("da_out"))
        hsq_ready, hms_ready, hvar_ready, hrs_ready, hbc_ready, ya_ready = (
            sem("hsq_ready"), sem("hms_ready"), sem("hvar_ready"), sem("hrs_ready"), sem("hbc_ready"), sem("ya_ready"))
        gelu_done, gates_done, glu_sig, ys_ready, mg_part, mg_ready = (
            sem("gelu_done"), sem("gates_done"), sem("glu_sig"), sem("ys_ready"), sem("mg_part"), sem("mg_ready"))
        xa_scores, xa_max, xa_exp, xa_probs, xa_turned, xa_copied, xa_pv, xa_out = (
            sem("xa_scores"), sem("xa_max"), sem("xa_exp"), sem("xa_probs"), sem("xa_turned"),
            sem("xa_copied"), sem("xa_pv"), sem("xa_out"))
        ff_relu, ff_ready = sem("ff_relu"), sem("ff_ready")
        lw_in, w1_in, lvec_in = sem("lw_in"), sem("w1_in"), sem("lvec_in")
        sw_ready, sw_used, nq_ready, f_log, f_ready = (
            sem("sw_ready"), sem("sw_used"), sem("nq_ready"), sem("f_log"), sem("f_ready"))
        flat_ready, hid_mm, hid_ready, kv2_mm, kcr_ready, kcs_mm, kc_ready = (
            sem("flat_ready"), sem("hid_mm"), sem("hid_ready"), sem("kv2_mm"), sem("kcr_ready"),
            sem("kcs_mm"), sem("kc_ready"))
        pooled_ready, pool_mm, pool_out, conv_out = sem("pooled_ready"), sem("pool_mm"), sem("pool_out"), sem("conv_out")
        at_scores, at_max, at_exp, at_probs, at_turned, at_copied, at_pv, at_out = (
            sem("at_scores"), sem("at_max"), sem("at_exp"), sem("at_probs"), sem("at_turned"),
            sem("at_copied"), sem("at_pv"), sem("at_out"))
        obr_ready, sig_ready, acc_ready = sem("obr_ready"), sem("sig_ready"), sem("acc_ready")

        def bank_free(pe, quad, s):
            if s >= 2:
                pe.wait_ge(evac_done[s - 2], quad + 1)
            elif not (isinstance(quad, int) and quad == 0):
                pe.wait_ge(evac_done[s + 2], quad)

        def gemm(pe, quad, s, rhs, width=T):
            pe.wait_ge(w_full[s], 16 * quad + 16)
            bank_free(pe, quad, s)
            for k in range(KT):
                mm = pe.matmul(bank[s % 2][:, 0:width], slot[s][:, k, :], rhs[:, k, 0:width],
                               start=(k == 0), stop=(k == KT - 1))
            mm.then_inc(mm_done[s], 1)

        def gemm_tokens(pe, quad, s, lhs, tiles=TT):
            pe.wait_ge(w_full[s], 16 * quad + 16)
            bank_free(pe, quad, s)
            for t in range(tiles):
                for k in range(KT):
                    mm = pe.matmul(bank[s % 2][:, t * P:(t + 1) * P], lhs[:, k, t * P:(t + 1) * P],
                                   slot[s][:, k, :], start=(k == 0), stop=(k == KT - 1))
            mm.then_inc(mm_done[s], 1)

        def squares(act, src, width=T):
            for k in range(KT):
                op = act.activation(SQ[:, k, 0:width], src[:, k, 0:width], ACT.Square)
            op.then_inc(sq_ready, 1)

        def norm_sums(pe, n, tiles=TT):
            pe.wait_ge(sq_ready, n + 1)
            if not (isinstance(n, int) and n == 0):
                pe.wait_ge(var_ready, n)
            for t in range(tiles):
                for k in range(KT):
                    mm = pe.matmul(bank[6][:, t:t + 1], SQ[:, k, t * P:(t + 1) * P], ones,
                                   start=(k == 0), stop=(k == KT - 1))
            mm.then_inc(ms_ready, 1)

        def norm_mean(dve, n, tiles=TT):
            dve.wait_ge(ms_ready, n + 1)
            if not (isinstance(n, int) and n == 0):
                dve.wait_ge(rstd_ready, n)
            dve.tensor_scalar(VAR[:, 0:tiles], bank[6][:, 0:tiles], 1.0 / D, EPS, ALU.mult,
                              ALU.add).then_inc(var_ready, 1)

        def root(pool, v, r0, rt, rs):
            pool.tensor_tensor(r0, v, HALF[:, 0:v.shape[-1]], ALU.pow)
            pool.drain()
            pool.tensor_tensor(rt, r0, r0, ALU.mult)
            pool.drain()
            pool.tensor_tensor(rt, rt, v, ALU.mult)
            pool.drain()
            pool.tensor_scalar(rt, rt, -0.5, 1.5, ALU.mult, ALU.add)
            pool.drain()
            return pool.tensor_tensor(rs, rt, r0, ALU.mult)

        def norm_root(pool, n, tiles=TT):
            pool.wait_ge(var_ready, n + 1)
            if not (isinstance(n, int) and n == 0):
                pool.wait_ge(bc_ready, n)
            root(pool, VAR[:, 0:tiles], R0[:, 0:tiles], RT[:, 0:tiles],
                 RSTD[:, 0:tiles]).then_inc(rstd_ready, 1)

        def norm_spread(pe, n, tiles=TT):
            pe.wait_ge(rstd_ready, n + 1)
            if not (isinstance(n, int) and n == 0):
                pe.wait_ge(bc_used, n)
            for t in range(tiles):
                mm = pe.matmul(bank[7][:, t * P:(t + 1) * P],
                               RSTD[:, t:t + 1].to_broadcast([P, P]), ident, start=True, stop=True)
            mm.then_inc(bc_ready, 1)

        def norm_apply(dve, n, dst, src, gain, width=T):
            dve.wait_ge(bc_ready, n + 1)
            for k in range(KT):
                op = dve.scalar_tensor_tensor(dst[:, k, 0:width], src[:, k, 0:width], gain[:, k:k + 1],
                                              bank[7][:, 0:width], ALU.mult, ALU.mult)
            op.then_inc(bc_used, 1)
            return op

        def residual_add(dve, n, y, gain):
            norm_apply(dve, n, y, y, gain)
            dve.drain()
            for k in range(KT):
                op = dve.tensor_tensor(X[:, k, :], X[:, k, :], y[:, k, :], ALU.add)
            op.then_inc(x_ready, 1)

        def copy_out(act, quad, s, dst, scale=1.0):
            act.wait_ge(mm_done[s], quad + 1)
            act.activation(dst, bank[s % 2][:, 0:dst.shape[-1]], ACT.Copy, scale=scale).then_inc(evac_done[s], 1)

        def one(ap, i):
            if isinstance(i, int):
                return ap[:, i, :]
            return ap[:, bass.ds(i, 1), :].rearrange("p a t -> p (a t)")

        def column(i):
            return VEC[:, i:i + 1] if isinstance(i, int) else VEC[:, bass.ds(i, 1)]

        def vec(col, n=KT):
            return VEC[:, col:col + n]

        def heads(eng, body):
            with eng.Fori(0, HEADS - 1) as b:
                body(b, False)
            body(HEADS - 1, True)

        STEPS = [(h, j, kind) for h in range(NH) for j in range(TT) for kind in ("cmp", "slc", "win", "fox")]
        NS = len(STEPS)

        block = ctx.enter_context(nc.Block())

        @block.sync
        def _(sp):
            for s in range(4):
                sp.dma_start(slot[s], weights[s]).then_inc(w_full[s], 16)
            with sp.Fori(1, Q_END) as quad:
                for s in range(4):
                    src = sp.snap(quad * 4 + s)
                    need = sp.snap(quad + 0)
                    sp.wait_ge(mm_done[s], need)
                    sp.dma_start(slot[s], weights[bass.ds(src, 1)].rearrange("a p k n -> (a p) k n")).then_inc(w_full[s], 16)
            sp.wait_ge(bc_used, 10)
            sp.dma_start(out, H).then_inc(out_stored, 16)
            sp.wait_ge(out_stored, 16)

        @block.tensor
        def _(pe):
            pe.wait_ge(const_ready, 1)
            norm_sums(pe, 0)
            pe.wait_ge(lam_prod, 1)
            for c in range(2):
                mm = pe.matmul(bank[5][:, c:c + 1], LAMP[:, c:c + 1].to_broadcast([P, P]), ones, start=True, stop=True)
            mm.then_inc(lam_sum, 1)
            norm_spread(pe, 0)
            pe.wait_ge(bc_used, 1)
            for quad in range(Q_U, Q_HEAD + 1):
                for s in range(4):
                    if quad == Q_HEAD and s == 3:
                        gemm_tokens(pe, quad, s, H)
                    else:
                        gemm(pe, quad, s, H)
            for s in range(4):
                pe.wait_ge(evac_done[s], 2)
            pe.wait_ge(prep_done, 1)

            def da_score(b, j, c):
                m = 8 * b + 2 * j + c
                if j == 0 and c == 0:
                    pe.wait_ge(rope_done, b + 1)
                pe.wait_ge(da_exp, m + 1)
                rows = slice(DH * c, DH * c + DH)
                pe.matmul(bank[5][:, 0:(j + 1) * P], QH[rows, j * P:(j + 1) * P], KH[rows, 0:(j + 1) * P],
                          start=True, stop=False)
                pe.matmul(bank[5][:, j * P:(j + 1) * P], ident, CON[:, C_CHUNK:C_CHUNK + P],
                          start=False, stop=True).then_inc(da_scores, 1)

            def da_turn(b, j):
                pe.wait_ge(da_probs, 4 * b + j + 1)
                pe.wait_ge(da_copied, 4 * b + j + 1)
                for t in range(j + 1):
                    mm = pe.transpose(bank[6][:, t * P:(t + 1) * P], PC[:, t * P:(t + 1) * P], ident)
                mm.then_inc(da_turned, 1)

            def da_values(b, j):
                if j == 0:
                    pe.wait_ge(da_out, b + 1)
                    pe.wait_ge(evac_done[3], b + (Q_HEAD + 1))
                pe.wait_ge(da_copied, 4 * b + j + 2)
                for t in range(j + 1):
                    mm = pe.matmul(bank[7][:, j * P:(j + 1) * P], VH[:, t * P:(t + 1) * P],
                                   PTB[j % 2][:, t * P:(t + 1) * P], start=(t == 0), stop=(t == j))
                mm.then_inc(da_pv, 1)

            def s5_in(b, q):
                pe.wait_ge(bl_full[q], 16 * b + 16)
                pe.wait_ge(bu_used, 4 * b + q + 1)
                for c in range(2):
                    mm = pe.matmul(bank[2 + c][:, :], BL[q][:, c, :], one(U, b), start=True, stop=True)
                mm.then_inc(bu_ready, 1)

            def s5_out(b, q):
                pe.wait_ge(ss_ready, 4 * b + q + 3)
                pe.wait_ge(cl_ready, 4 * b + q + 1)
                if q == 0:
                    pe.wait_ge(y_used, b + 1)
                for c in range(2):
                    mm = pe.matmul(bank[4][:, :], CL[q][:, c, :], SS[q % 2][c], start=(q == 0 and c == 0),
                                   stop=(q == PPB - 1 and c == 1))
                mm.then_inc(y_done, 1)

            def head_body(b, last):
                for q in range(PPB):
                    s5_in(b, q)
                    da_score(b, q, 0)
                    if not last:
                        if q == 3:
                            gemm_tokens(pe, b + (Q_HEAD + 1), q, H)
                        else:
                            gemm(pe, b + (Q_HEAD + 1), q, H)
                    da_score(b, q, 1)
                    if q:
                        da_turn(b, q - 1)
                        s5_out(b, q - 1)
                        da_values(b, q - 1)
                da_turn(b, 3)
                s5_out(b, 3)
                da_values(b, 3)

            heads(pe, head_body)

            pe.wait_ge(hsq_ready, 1)
            for h in range(HEADS):
                for t in range(TT):
                    mm = pe.matmul(bank[6][:, TT * h + t:TT * h + t + 1], SQ[:, h, t * P:(t + 1) * P], ones,
                                   start=True, stop=True)
            mm.then_inc(hms_ready, 1)
            pe.wait_ge(gelu_done, 1)
            for s in range(4):
                gemm(pe, Q_GLU, s, U)
            norm_sums_mem = lambda: norm_sums(pe, 1, 2)
            pe.wait_ge(hvar_ready, 1)
            norm_sums_mem()
            for s in range(4):
                gemm(pe, Q_GLU + 1, s, U)
            norm_spread(pe, 1, 2)
            pe.wait_ge(hrs_ready, 1)
            for h in range(HEADS):
                if h >= 2:
                    pe.wait_ge(ya_ready, h - 1)
                for t in range(TT):
                    mm = pe.matmul(bank[2 + h % 2][:, t * P:(t + 1) * P],
                                   HRS[:, TT * h + t:TT * h + t + 1].to_broadcast([P, P]), ident,
                                   start=True, stop=True)
                mm.then_inc(hbc_ready, 1)
            pe.wait_ge(ys_ready, KT)
            for i in range(2):
                for s in range(4):
                    gemm(pe, Q_SSM + i, s, YS2)
            pe.wait_ge(ya_ready, HEADS)
            for i in range(2):
                for s in range(4):
                    gemm(pe, Q_DA + i, s, YA)
            pe.wait_ge(mg_ready, KT)
            for i in range(2):
                for s in range(4):
                    gemm(pe, Q_MIX + i, s, MG)
            pe.wait_ge(bc_used, 2)
            norm_sums(pe, 2)
            for s in range(4):
                gemm(pe, Q_KX, s, MEMN, MEM)
            norm_spread(pe, 2)
            for s in range(4):
                gemm(pe, Q_KX + 1, s, MEMN, MEM)
            for s in range(4):
                gemm_tokens(pe, Q_VX, s, MEMN, 2)
            norm_sums(pe, 3)
            for s in range(4):
                gemm_tokens(pe, Q_VX + 1, s, MEMN, 2)
            norm_spread(pe, 3)
            pe.wait_ge(bc_used, 4)
            for i in range(2):
                for s in range(4):
                    gemm(pe, Q_XQ + i, s, HX)
            for s in range(4):
                pe.wait_ge(evac_done[s], Q_XQ + 2)

            def xa_score(i):
                h, j = divmod(i, TT)
                if i >= 2:
                    pe.wait_ge(xa_exp, i - 1)
                for k in range(2):
                    mm = pe.matmul(bank[2 + i % 2][:, 0:MEM], QX[:, 2 * h + k, j * P:(j + 1) * P],
                                   KX[:, 2 * h + k, :], start=(k == 0), stop=(k == 1))
                mm.then_inc(xa_scores, 1)

            def xa_turn(i):
                pe.wait_ge(xa_probs, i + 1)
                if i >= 2:
                    pe.wait_ge(xa_copied, i - 1)
                for k in range(2):
                    mm = pe.transpose(bank[4 + i % 2][:, k * P:(k + 1) * P], PR[i % 2][:, k * P:(k + 1) * P], ident)
                mm.then_inc(xa_turned, 1)

            def xa_values(i):
                h, j = divmod(i, TT)
                if j == 0 and h >= 1:
                    pe.wait_ge(xa_out, h)
                pe.wait_ge(xa_copied, i + 1)
                for e in range(2):
                    for k in range(2):
                        mm = pe.matmul(bank[6 + e][:, j * P:(j + 1) * P],
                                       VX[:, k, h * XD + e * P:h * XD + (e + 1) * P],
                                       PTB[i % 2][:, k * P:(k + 1) * P], start=(k == 0), stop=(k == 1))
                mm.then_inc(xa_pv, 1)

            for i in range(XH * TT + 2):
                if i < XH * TT:
                    xa_score(i)
                if 1 <= i <= XH * TT:
                    xa_turn(i - 1)
                if i >= 2:
                    xa_values(i - 2)
            pe.wait_ge(xa_out, XH)
            for i in range(2):
                for s in range(4):
                    gemm(pe, Q_XO + i, s, OX)
            norm_sums(pe, 4)
            norm_spread(pe, 4)
            norm_sums(pe, 5)
            norm_spread(pe, 5)
            pe.wait_ge(bc_used, 6)
            with pe.Fori(0, Q_FF2 - Q_FF1) as f:
                for s in range(4):
                    gemm(pe, f + Q_FF1, s, H)
            pe.wait_ge(ff_ready, 32)
            for s in range(4):
                pe.wait_ge(evac_done[s], Q_FF2)
            with pe.Fori(0, KT // 2) as f:
                for o in range(2):
                    quad = 2 * f + (Q_FF2 + o)
                    pe.wait_ge(evac_done[2], quad - 1)
                    for s in range(4):
                        pe.wait_ge(w_full[s], 16 * quad + 16)
                        for k in range(KT):
                            mm = pe.matmul(bank[o][:, :], slot[s][:, k, :], RB[:, KT * s + k, :],
                                           start=(s == 0 and k == 0), stop=(s == 3 and k == KT - 1))
                        mm.then_inc(mm_done[s], 1)
            norm_sums(pe, 6)
            norm_spread(pe, 6)

            with pe.Fori(0, LAYERS) as L:
                q0 = pe.snap(QL * L + Q_L2)
                norm_sums(pe, L + 7)
                norm_spread(pe, L + 7)
                pe.wait_ge(bc_used, L + 8)
                for s in range(4):
                    gemm(pe, q0, s, H)
                gemm_tokens(pe, q0 + 1, 0, H)
                pe.wait_ge(w_full[1], 16 * (q0 + 1) + 16)
                bank_free(pe, q0 + 1, 1)
                for k in range(KT):
                    pe.matmul(bank[1][:, :], slot[1][:, k, :], H[:, k, :], start=(k == 0), stop=(k == KT - 1))
                for t in range(TT):
                    for k in range(KT):
                        mm = pe.matmul(bank[4][:, 16 * t:16 * t + 12], H[:, k, t * P:(t + 1) * P],
                                       slot[1][:, k, 2:14], start=(k == 0), stop=(k == KT - 1))
                mm.then_inc(mm_done[1], 1)
                for s in (0, 1, 2):
                    pe.wait_ge(evac_done[s], q0 + 1)
                for i in range(3):
                    mm = pe.matmul(bank[(2, 3, 5)[i]][:, :], CON[:, C_SWAP:C_SWAP + P], RAW[:, i, :],
                                   start=True, stop=True)
                mm.then_inc(sw_ready, 1)
                for s in (2, 3):
                    gemm(pe, q0 + 1, s, H)
                for s in (0, 1):
                    gemm(pe, q0 + 2, s, H)
                for s in (2, 3):
                    gemm_tokens(pe, q0 + 2, s, H)
                for s in range(4):
                    gemm(pe, q0 + 3, s, H)
                pe.wait_ge(flat_ready, L + 1)
                pe.wait_ge(w1_in, 16 * L + 16)
                for c in range(2):
                    rows = slice(64 * c, 64 * c + 64)
                    for l in range(CMP_LEN):
                        mm = pe.matmul(bank[6 + c][:, 32 * c:32 * c + NC], W1[rows, l, :], FLAT[rows, l, :],
                                       start=(l == 0), stop=(l == CMP_LEN - 1))
                mm.then_inc(hid_mm, 1)
                for s in range(4):
                    gemm(pe, q0 + 4, s, H)
                pe.wait_ge(hid_ready, L + 1)
                pe.matmul(bank[6][:, 64:64 + NC], W2K, HID[:, 0:NC], start=True, stop=True)
                pe.matmul(bank[6][0:NC, 128:192], HID[:, 32:32 + NC], W2V, start=True, stop=False)
                pe.matmul(bank[6][0:NC, 128:192], ONE_ROW[:, 0:NC], B2V, start=False, stop=True).then_inc(kv2_mm, 1)
                for s in range(4):
                    gemm(pe, q0 + 5, s, H)
                pe.wait_ge(kcr_ready, L + 1)
                pe.matmul(bank[6][:, 96:96 + NC], CON[:, C_SWAP:C_SWAP + P], KCR, start=True, stop=True).then_inc(kcs_mm, 1)
                pe.wait_ge(pooled_ready, L + 1)
                pe.wait_ge(sw_used, L + 1)
                for i in range(2):
                    mm = pe.matmul(bank[2 + i][:, :], PW[:, i, :], RB[:, 16 + i, :], start=True, stop=True)
                mm.then_inc(pool_mm, 1)
                for s in range(4):
                    gemm(pe, q0 + 6, s, H)
                pe.wait_ge(nq_ready, L + 1)
                pe.wait_ge(f_ready, L + 1)
                pe.wait_ge(kc_ready, L + 1)
                pe.wait_ge(pool_out, L + 1)

                def score(i):
                    h, j, kind = STEPS[i]
                    rows = slice(64 * (h % 2), 64 * (h % 2) + 64)
                    to = bank[2 + i % 2]
                    pe.wait_ge(at_exp, L * NS + (i + 1))
                    if kind == "cmp":
                        pe.matmul(to[:, 0:NC], NQ[rows, h // 2, j * P:(j + 1) * P], KC[rows, :], start=True, stop=False)
                        mm = pe.matmul(to[:, 0:NC], ident, CON[:, C_CMP + 32 * j:C_CMP + 32 * j + NC],
                                       start=False, stop=True)
                    else:
                        keys = {"slc": KS, "win": KW, "fox": FK[:, h // 2, :]}[kind]
                        q = FQ if kind == "fox" else NQ
                        width = (j + 1) * P
                        pe.matmul(to[:, 0:width], q[rows, h // 2, j * P:(j + 1) * P], keys[rows, 0:width],
                                  start=True, stop=False)
                        if kind == "fox":
                            pair = slice(32 * h, 32 * h + 2)
                            pe.matmul(to[:, 0:width], FCQ[pair, j * P:(j + 1) * P], FCK[pair, 0:width],
                                      start=False, stop=False)
                        mm = pe.matmul(to[:, j * P:width], ident, CON[:, C_CAUSAL:C_CAUSAL + P],
                                       start=False, stop=True)
                    mm.then_inc(at_scores, 1)

                def turn(i):
                    h, j, kind = STEPS[i]
                    pe.wait_ge(at_probs, L * NS + (i + 1))
                    pe.wait_ge(at_copied, L * NS + (i + 1))
                    to = bank[4 + i % 2]
                    if kind == "cmp":
                        mm = pe.transpose(to[0:NC, 0:P], PR[i % 2][:, 0:NC], ident)
                    else:
                        for t in range(j + 1):
                            mm = pe.transpose(to[:, t * P:(t + 1) * P], PR[i % 2][:, t * P:(t + 1) * P], ident)
                    mm.then_inc(at_turned, 1)

                def values(i):
                    h, j, kind = STEPS[i]
                    rows = slice(64 * (h % 2), 64 * (h % 2) + 64)
                    if j == 0 and kind in ("cmp", "fox"):
                        pe.wait_ge(at_out, L * 8 + (2 * h + (kind == "fox") + 1))
                    pe.wait_ge(at_copied, L * NS + (i + 3))
                    pt = PTB[i % 2]
                    to = bank[7 if kind == "fox" else 6][rows, j * P:(j + 1) * P]
                    if kind == "cmp":
                        mm = pe.matmul(to, VC[0:NC, :], pt[0:NC, 0:P], start=True, stop=False)
                    else:
                        for t in range(j + 1):
                            if kind == "fox":
                                v = FV[:, h // 2, t * P + 64 * (h % 2):t * P + 64 * (h % 2) + 64]
                            else:
                                o = t * P + (64 if kind == "win" else 0)
                                v = VSW[:, o:o + 64]
                            mm = pe.matmul(to, v, pt[:, t * P:(t + 1) * P], start=(kind == "fox" and t == 0),
                                           stop=(kind != "slc" and t == j))
                    mm.then_inc(at_pv, 1)

                for i in range(NS + 2):
                    if i < NS:
                        score(i)
                    if i < NS and i % 2 == 1:
                        gemm(pe, q0 + (7 + i // 8), (i // 2) % 4, H)
                    if 1 <= i <= NS:
                        turn(i - 1)
                    if i >= 2:
                        values(i - 2)

                pe.wait_ge(obr_ready, L + 1)
                for ob in range(KT):
                    s, quad = ob % 4, q0 + (15 + ob // 4)
                    pe.wait_ge(w_full[s], 16 * quad + 16)
                    bank_free(pe, quad, s)
                    for i in range(NBR):
                        for k in range(2):
                            mm = pe.matmul(bank[4 * (ob % 2) + i][:, :], slot[s][:, 2 * i + k, :], OBR[:, 2 * i + k, :],
                                           start=(k == 0), stop=(k == 1))
                    mm.then_inc(mm_done[s], 1)
                pe.wait_ge(acc_ready, L * KT + KT)
                for i in range(2):
                    for s in range(4):
                        gemm(pe, q0 + (17 + i), s, H)
            norm_sums(pe, 9)
            norm_spread(pe, 9)

        @block.scalar
        def _(act):
            act.dma_start(X, x_in).then_inc(x_loaded, 16)
            act.dma_start(VEC[:, :], vecs).then_inc(consts_in, 16)
            act.dma_start(CON[:, :], consts).then_inc(consts_in, 16)
            act.dma_start(TAB[:, :], rope1).then_inc(consts_in, 16)
            act.sem_inc(da_exp, 1)
            act.sem_inc(da_copied, 1)
            act.sem_inc(da_out, 1)
            act.sem_inc(at_exp, 2)
            act.sem_inc(at_copied, 2)
            act.sem_inc(at_out, 2)
            act.wait_ge(x_loaded, 16)
            squares(act, X)
            act.wait_ge(consts_in, 48)
            act.activation(PREP[:, 1, :], vec(V_LDT, PAIRS), ACT.Exp).then_inc(prep_dt, 1)
            act.wait_ge(lam_sum, 1)
            act.activation(LAME, bank[5][:, 0:2], ACT.Exp).then_inc(lam_exp, 1)
            act.wait_ge(prep_arg, 1)
            act.activation(RADIUS, PREP[:, 2, :], ACT.Exp).then_inc(prep_exp, 1)
            act.wait_ge(prep_arg, 2)
            act.activation(PREP[:, 5, :], PREP[:, 3, :], ACT.Sin)
            act.activation(PREP[:, 6, :], PREP[:, 4, :], ACT.Sin).then_inc(prep_sin, 1)
            for blk in range(KT):
                copy_out(act, Q_U + blk // 4, blk % 4, U[:, blk, :])
            for blk in range(KT):
                s = blk % 4
                act.wait_ge(mm_done[s], Q_GB + blk // 4 + 1)
                act.activation(RB[:, 8 + blk, :], bank[s % 2][:, :], ACT.Identity,
                               bias=column(V_BGATE + 8 + blk)).then_inc(evac_done[s], 1)

            def head_evac(hd, s):
                act.wait_ge(mm_done[s], hd + (Q_HEAD + 1))
                if s < 2:
                    raw, swapped = ((QRAW, QSW), (KRAW, KSW))[s]
                    scale = DH ** -0.5 if s == 0 else 1.0
                    if not isinstance(hd, int):
                        act.wait_ge(rope_done, hd)
                    for quarter in range(4):
                        other = quarter ^ 1
                        act.activation(swapped[32 * quarter:32 * quarter + 32, :],
                                       bank[s][32 * other:32 * other + 32, :], ACT.Copy, scale=scale)
                    act.activation(raw, bank[s][:, :], ACT.Copy, scale=scale).then_inc(evac_done[s], 1)
                elif s == 2:
                    act.activation(one(RB, hd), bank[0][:, :], ACT.Identity,
                                   bias=column(hd + V_BGATE)).then_inc(evac_done[s], 1)
                else:
                    act.activation(VH, bank[1][:, :], ACT.Copy).then_inc(evac_done[s], 1)

            for s in range(4):
                head_evac(0, s)
            act.wait_ge(prep_done, 1)
            act.wait_ge(cl_zero, 1)

            def da_exponent(b, j, c):
                act.wait_ge(da_max, 8 * b + 2 * j + c + 1)
                at = 2 * (j % 2) + c
                act.activation(PR[c][:, 0:(j + 1) * P], bank[5][:, 0:(j + 1) * P], ACT.Exp,
                               bias=NMAX[:, at:at + 1], accum_out=RSUM[:, at:at + 1]).then_inc(da_exp, 1)

            def da_copy(b, j):
                act.wait_ge(da_turned, 4 * b + j + 2)
                act.wait_ge(da_pv, 4 * b + j + 1)
                act.activation(PTB[j % 2][:, 0:(j + 1) * P], bank[6][:, 0:(j + 1) * P], ACT.Copy).then_inc(da_copied, 1)

            def head_body(b, last):
                for q in range(PPB):
                    act.wait_ge(y_done, 4 * b + q + 1)
                    act.activation(CL[q][:, :, 32 * q:32 * q + 32],
                                   CT[:, 4 * b + q, :, :] if isinstance(b, int) else
                                   CT[:, bass.ds(4 * b + q, 1), :, :].rearrange("p a c m -> p (a c) m"),
                                   ACT.Copy).then_inc(cl_ready, 1)
                    da_exponent(b, q, 0)
                    if not last and q < 3:
                        head_evac(b + 1, q)
                    da_exponent(b, q, 1)
                    if q:
                        da_copy(b, q - 1)
                da_copy(b, 3)
                act.wait_ge(da_pv, 4 * b + 6)
                act.activation(one(YA, b), bank[7][:, :], ACT.Copy).then_inc(da_out, 1)
                if not last:
                    head_evac(b + 1, 3)

            act.sem_inc(da_turned, 1)
            heads(act, head_body)

            act.wait_ge(y_used, KT + 1)
            act.drain()
            for h in range(HEADS):
                op = act.activation(SQ[:, h, :], YA[:, h, :], ACT.Square)
            op.then_inc(hsq_ready, 1)
            act.activation(U_[:, :], U_[:, :], ACT.Gelu_apprx_tanh).then_inc(gelu_done, 1)
            act.wait_ge(mem_loaded, 16)
            act.wait_ge(hms_ready, 1)
            squares(act, MEMRAW, MEM)
            for blk in range(KT):
                s = blk % 4
                act.wait_ge(mm_done[s], Q_GLU + blk // 4 + 1)
                if blk >= 2:
                    act.wait_ge(ys_ready, blk - 1)
                act.activation(VB[:, blk % 2, :], bank[s % 2][:, :], ACT.Sigmoid,
                               bias=column(V_BGLU + blk)).then_inc(evac_done[s], 1)
                if blk == 1:
                    act.activation(R[:, 0:8 * T], R[:, 0:8 * T], ACT.Sigmoid)
                if blk == 3:
                    act.activation(R[:, 8 * T:16 * T], R[:, 8 * T:16 * T], ACT.Sigmoid).then_inc(gates_done, 1)
            for blk in range(KT):
                s = blk % 4
                act.wait_ge(mm_done[s], Q_MIX + blk // 4 + 1)
                act.activation(VB[:, blk, :], bank[s % 2][:, :], ACT.Copy)
                op = act.activation(SQ[:, blk, :], bank[s % 2][:, :], ACT.Square)
                op.then_inc(evac_done[s], 1)
            act.drain()
            act.sem_inc(sq_ready, 1)
            for blk in range(KT):
                copy_out(act, Q_KX + blk // 4, blk % 4, KX[:, blk, :])
            for blk in range(KT):
                if blk == 4:
                    act.wait_ge(x_ready, 1)
                    squares(act, X)
                s = blk % 4
                act.wait_ge(mm_done[s], Q_VX + blk // 4 + 1)
                act.activation(VX[:, :, blk * P:(blk + 1) * P],
                               bank[s % 2][:, 0:2 * P].rearrange("p (t n) -> p t n", t=2), ACT.Copy).then_inc(evac_done[s], 1)
            for blk in range(KT):
                copy_out(act, Q_XQ + blk // 4, blk % 4, QX[:, blk, :], XD ** -0.5)

            def xa_exponent(i):
                act.wait_ge(xa_max, i + 1)
                if i >= 2:
                    act.wait_ge(xa_turned, i - 1)
                at = i % 2
                act.activation(PR[at][:, 0:MEM], bank[2 + at][:, 0:MEM], ACT.Exp, bias=NMAX[:, at:at + 1],
                               accum_out=RSUM[:, at:at + 1]).then_inc(xa_exp, 1)

            def xa_copy(i):
                act.wait_ge(xa_turned, i + 1)
                if i >= 2:
                    act.wait_ge(xa_pv, i - 1)
                act.activation(PTB[i % 2][:, 0:MEM], bank[4 + i % 2][:, 0:MEM], ACT.Copy).then_inc(xa_copied, 1)

            def xa_store(h):
                act.wait_ge(xa_pv, TT * (h + 1))
                for e in range(2):
                    op = act.activation(OX[:, 2 * h + e, :], bank[6 + e][:, :], ACT.Copy)
                op.then_inc(xa_out, 1)

            for i in range(XH * TT + 3):
                if i < XH * TT:
                    xa_exponent(i)
                if 1 <= i <= XH * TT:
                    xa_copy(i - 1)
                if i >= 3 and (i - 3) % TT == TT - 1:
                    xa_store((i - 3) // TT)

            def store_and_square(quad, s, src, blk):
                act.wait_ge(mm_done[s], quad + 1)
                act.activation(one(VB, blk), src, ACT.Copy)
                return act.activation(one(SQ, blk), src, ACT.Square)

            for blk in range(KT):
                op = store_and_square(Q_XO + blk // 4, blk % 4, bank[blk % 2][:, :], blk)
                op.then_inc(evac_done[blk % 4], 1)
            act.drain()
            act.sem_inc(sq_ready, 1)
            act.wait_ge(x_ready, 2)
            act.wait_ge(ms_ready, 5)
            squares(act, X)
            with act.Fori(0, Q_FF2 - Q_FF1) as f:
                for s in range(4):
                    act.wait_ge(mm_done[s], f + (Q_FF1 + 1))
                    act.activation(one(RB, 4 * f + s), bank[s % 2][:, :], ACT.Relu).then_inc(evac_done[s], 1)
            act.wait_ge(ms_ready, 6)
            with act.Fori(0, KT // 2) as f:
                for o in range(2):
                    op = store_and_square(2 * f + (Q_FF2 + o), 3, bank[o][:, :], 2 * f + o)
                    op.then_inc(evac_done[2], 1)
                    for s in (0, 1, 3):
                        act.sem_inc(evac_done[s], 1)
            act.drain()
            act.sem_inc(sq_ready, 1)

            with act.Fori(0, LAYERS) as L:
                q0 = act.snap(QL * L + Q_L2)
                act.wait_ge(x_ready, L + 3)
                act.wait_ge(ms_ready, L + 7)
                squares(act, X)
                act.wait_ge(lvec_in, 16 * L + 16)

                def store(quad, s, dst, scale=1.0):
                    copy_out(act, quad, s, dst, scale)

                store(q0, 0, RAW[:, 0, :], 64 ** -0.5)
                store(q0, 1, RAW[:, 1, :], 64 ** -0.5)
                store(q0, 2, RAW[:, 2, :])
                store(q0, 3, KCVC)
                store(q0 + 1, 0, VSW)
                act.wait_ge(mm_done[1], q0 + 2)
                act.activation(FZ, bank[1][:, :], ACT.Identity, bias=LVEC[:, L_FBIAS:L_FBIAS + 1])
                act.activation(G12[:, :, 0:12], bank[4][:, 0:64].rearrange("p (t g) -> p t g", t=TT)[:, :, 0:12],
                               ACT.Sigmoid).then_inc(evac_done[1], 1)
                act.drain()
                act.activation(FL, FZ, ACT.Abs)
                act.drain()
                act.activation(FL, FL, ACT.Exp, scale=-1.0)
                act.drain()
                act.activation(FL, FL, ACT.Ln, bias=1.0).then_inc(f_log, 1)
                store(q0 + 1, 2, FQ[:, 0, :], 64 ** -0.5)
                store(q0 + 1, 3, FQ[:, 1, :], 64 ** -0.5)
                store(q0 + 2, 0, FK[:, 0, :])
                store(q0 + 2, 1, FK[:, 1, :])
                store(q0 + 2, 2, FV[:, 0, :])
                store(q0 + 2, 3, FV[:, 1, :])
                for i in range(2):
                    for s in range(4):
                        store(q0 + (3 + i), s, RB[:, 4 * i + s, :])
                    if i == 0:
                        act.wait_ge(hid_mm, L + 1)
                        for c in range(2):
                            op = act.activation(HID[:, 32 * c:32 * c + NC], bank[6 + c][:, 32 * c:32 * c + NC], ACT.Silu,
                                                bias=LVEC[:, L_B1 + c:L_B1 + c + 1])
                        op.then_inc(hid_ready, 1)
                act.wait_ge(kv2_mm, L + 1)
                act.activation(VC[0:NC, :], bank[6][0:NC, 128:192], ACT.Copy)
                act.activation(KCR, bank[6][:, 64:64 + NC], ACT.Identity,
                               bias=LVEC[:, L_B2K:L_B2K + 1]).then_inc(kcr_ready, 1)
                for i in range(2):
                    for s in range(4):
                        act.wait_ge(mm_done[s], q0 + (6 + i))
                        act.activation(U[:, 4 * i + s, :], bank[s % 2][:, :], ACT.Silu).then_inc(evac_done[s], 1)
                    if i == 0:
                        act.wait_ge(pool_mm, L + 1)
                        for c in range(2):
                            op = act.activation(OBR[:, 2 + c, :], bank[2 + c][:, :], ACT.Copy,
                                                scale=LVEC[:, L_POOL + c:L_POOL + c + 1])
                        op.then_inc(pool_out, 1)

                def exponent(i):
                    h, j, kind = STEPS[i]
                    width = NC if kind == "cmp" else (j + 1) * P
                    act.wait_ge(at_max, L * NS + (i + 1))
                    act.wait_ge(at_turned, L * NS + (i + 1))
                    at = i % 2
                    act.activation(PR[at][:, 0:width], bank[2 + at][:, 0:width], ACT.Exp, bias=NMAX[:, at:at + 1],
                                   accum_out=RSUM[:, at:at + 1]).then_inc(at_exp, 1)

                def turned_copy(i):
                    h, j, kind = STEPS[i]
                    act.wait_ge(at_turned, L * NS + (i + 3))
                    act.wait_ge(at_pv, L * NS + (i + 1))
                    if kind == "cmp":
                        act.activation(PTB[i % 2][0:NC, 0:P], bank[4 + i % 2][0:NC, 0:P], ACT.Copy).then_inc(at_copied, 1)
                    else:
                        width = (j + 1) * P
                        act.activation(PTB[i % 2][:, 0:width], bank[4 + i % 2][:, 0:width], ACT.Copy).then_inc(at_copied, 1)

                def head_out(h):
                    rows = slice(64 * (h % 2), 64 * (h % 2) + 64)
                    act.wait_ge(at_pv, L * NS + (16 * (h + 1) + 2))
                    act.activation(OBR[rows, h // 2, :], bank[6][rows, :], ACT.Copy).then_inc(at_out, 1)
                    act.activation(OBR[rows, 6 + h // 2, :], bank[7][rows, :], ACT.Copy).then_inc(at_out, 1)

                act.wait_ge(conv_out, L + 1)
                for i in range(NS + 3):
                    if i < NS:
                        exponent(i)
                    if i < NS and i % 2 == 1:
                        store(q0 + (7 + i // 8), (i // 2) % 4, RB[:, i // 2, :])
                    if 1 <= i <= NS:
                        turned_copy(i - 1)
                    if i >= 3 and (i - 3) % 16 == 15:
                        head_out((i - 3) // 16)
                act.drain()
                for ob in range(KT):
                    act.activation(R[:, 4 * ob * T:4 * (ob + 1) * T], R[:, 4 * ob * T:4 * (ob + 1) * T],
                                   ACT.Sigmoid).then_inc(sig_ready, 1)
            act.wait_ge(x_ready, 3 + LAYERS)
            squares(act, X)

        @block.vector
        def _(dve):
            dve.memset(SMALL[:, 0:4], 1.0)
            dve.memset(HALF, -0.5)
            dve.memset(ONE_ROW, 1.0)
            dve.drain()
            dve.sem_inc(bu_used, 1)
            dve.sem_inc(ss_ready, 2)
            dve.sem_inc(y_used, 1)
            dve.wait_ge(consts_in, 48)
            dve.sem_inc(const_ready, 1)
            norm_mean(dve, 0)

            dve.tensor_tensor(LAMP[:, 0:1], vec(V_LQ1, 1), vec(V_LK1, 1), ALU.mult)
            dve.tensor_tensor(LAMP[:, 1:2], vec(V_LQ2, 1), vec(V_LK2, 1), ALU.mult).then_inc(lam_prod, 1)
            dve.tensor_scalar(HN08, vec(V_HEADNORM, 1), 1.0 - LAM_INIT, None, ALU.mult)
            norm_apply(dve, 0, H, X, vec(V_MIX_PRE))
            dve.wait_ge(lam_exp, 1)
            dve.tensor_tensor(NLAM, LAME[:, 1:2], LAME[:, 0:1], ALU.subtract)
            dve.drain()
            dve.tensor_scalar(NLAM, NLAM, LAM_INIT, None, ALU.subtract)

            DT, RE, ARG, ARGC, SN, CS = (PREP[:, i, :] for i in range(1, 7))
            A, B, C, E, F, G, I, J = (PREP[:, i, :] for i in range(8, 16))
            lre, lim = vec(V_LRE, PAIRS), vec(V_LIM, PAIRS)

            def seq(*ops):
                for op in ops:
                    op()
                dve.drain()

            def tt(o, a, b, op):
                return lambda: dve.tensor_tensor(o, a, b, op)

            def ts(o, a, x, y, op0, op1=None):
                if op1 is None:
                    return lambda: dve.tensor_scalar(o, a, x, None, op0)
                return lambda: dve.tensor_scalar(o, a, x, y, op0, op1)

            def stt(o, a, x, b, op0, op1):
                return lambda: dve.scalar_tensor_tensor(o, a, x, b, op0, op1)

            dve.wait_ge(prep_dt, 1)
            dve.tensor_tensor(RE, lre, DT, ALU.mult).then_inc(prep_arg, 1)
            seq(tt(A, lim, DT, ALU.mult))
            turns = 1.5 * 2.0 ** 23
            two_pi = 2 * np.pi
            c1 = 6.28125
            c2 = float(np.float32(np.round((two_pi - c1) * 2.0 ** 22) / 2.0 ** 22))
            c3 = two_pi - c1 - c2
            pi32 = 3.1415925
            seq(ts(B, A, 1 / two_pi, turns, ALU.mult, ALU.add))
            seq(ts(B, B, turns, None, ALU.subtract))
            seq(stt(A, B, -c1, A, ALU.mult, ALU.add))
            seq(stt(A, B, -c2, A, ALU.mult, ALU.add))
            seq(stt(A, B, -c3, A, ALU.mult, ALU.add))
            seq(ts(ARG, A, pi32, -pi32, ALU.min, ALU.max), ts(C, A, np.pi / 2, None, ALU.add))
            seq(ts(E, C, pi32, -two_pi, ALU.is_gt, ALU.mult))
            seq(tt(C, C, E, ALU.add))
            dve.tensor_scalar(ARGC, C, pi32, -pi32, ALU.min, ALU.max).then_inc(prep_arg, 1)
            dve.wait_ge(prep_sin, 1)
            dve.wait_ge(prep_exp, 1)
            for table in (LOT, HIT):
                seq(lambda: dve.memset(table[:, :, 0, 0:1], 1.0), lambda: dve.memset(table[:, :, 1, 0:1], 0.0))
                size, n = table.shape[-1], 1
                while n < size:
                    w = [x.rearrange("p (n a) -> p n a", a=1).to_broadcast([P, PAIRS, n]) for x in (CS, SN)]
                    t = [W.rearrange("p (n a) -> p n a", n=PAIRS)[:, :, 0:n] for W in TMP[0:4]]
                    re, im = table[:, :, 0, 0:n], table[:, :, 1, 0:n]
                    seq(tt(t[0], re, w[0], ALU.mult), tt(t[1], im, w[1], ALU.mult),
                        tt(t[2], im, w[0], ALU.mult), tt(t[3], re, w[1], ALU.mult),
                        tt(E, CS, CS, ALU.mult), tt(F, SN, SN, ALU.mult), tt(G, CS, SN, ALU.mult))
                    if n == 1 and table is LOT:
                        seq(tt(A, RADIUS, CS, ALU.mult), tt(B, RADIUS, SN, ALU.mult))
                    seq(tt(table[:, :, 0, n:2 * n], t[0], t[1], ALU.subtract),
                        tt(table[:, :, 1, n:2 * n], t[2], t[3], ALU.add),
                        tt(CS, E, F, ALU.subtract), ts(SN, G, 2.0, None, ALU.mult))
                    n *= 2
            seq(ts(A, A, 1.0, None, ALU.subtract), tt(C, lre, lre, ALU.mult), tt(E, lim, lim, ALU.mult))
            seq(tt(C, C, E, ALU.add), tt(G, A, lre, ALU.mult), tt(F, B, lim, ALU.mult))
            seq(lambda: dve.reciprocal(C, C), tt(E, G, F, ALU.add), tt(I, B, lre, ALU.mult), tt(J, A, lim, ALU.mult))
            seq(tt(F, I, J, ALU.subtract))
            seq(tt(E, E, C, ALU.mult), tt(F, F, C, ALU.mult))
            dve.wait_ge(ct_in, 16)
            er, ei = [x.rearrange("p (n a) -> p n a", a=1).to_broadcast([P, PAIRS, 32]) for x in (E, F)]
            t = [R3[:, 1024 * i:1024 * i + 1024].rearrange("p (n m) -> p n m", n=PAIRS) for i in range(4)]
            seq(tt(t[0], CT[:, :, 0, :], er, ALU.mult), tt(t[1], CT[:, :, 1, :], ei, ALU.mult),
                tt(t[2], CT[:, :, 0, :], ei, ALU.mult), tt(t[3], CT[:, :, 1, :], er, ALU.mult))
            seq(tt(CT[:, :, 0, :], t[0], t[1], ALU.subtract), stt(CT[:, :, 1, :], t[2], -1.0, t[3], ALU.mult, ALU.subtract))
            dve.sem_inc(prep_done, 1)

            def da_row_max(b, j, c):
                dve.wait_ge(da_scores, 8 * b + 2 * j + c + 1)
                at = 2 * (j % 2) + c
                dve.tensor_reduce(NMAX[:, at:at + 1], bank[5][:, 0:(j + 1) * P], AX.X, ALU.max,
                                  negate=True).then_inc(da_max, 1)

            def da_combine(b, j):
                dve.wait_ge(da_exp, 8 * b + 2 * j + 3)
                o, w = 2 * (j % 2), (j + 1) * P
                dve.reciprocal(RINV[:, 0:2], RSUM[:, o:o + 2])
                dve.drain()
                dve.tensor_scalar(PR[0][:, 0:w], PR[0][:, 0:w], RINV[:, 0:1], None, ALU.mult)
                dve.tensor_scalar(PR[1][:, 0:w], PR[1][:, 0:w], RINV[:, 1:2], NLAM, ALU.mult, ALU.mult)
                dve.drain()
                dve.wait_ge(da_turned, 4 * b + j + 1)
                dve.tensor_tensor(PC[:, 0:w], PR[0][:, 0:w], PR[1][:, 0:w], ALU.add).then_inc(da_probs, 1)

            def s5_scan(b, q):
                n = 4 * b + q
                cs, sn = ROT[q % 2]
                rad = PREP[:, 0, n:n + 1] if isinstance(b, int) else PREP[:, 0, bass.ds(n, 1)]
                dve.wait_ge(tab_ready, n + 1)
                dve.wait_ge(bu_ready, n + 1)
                dve.tensor_tensor(TMP[0], bank[2][:, :], cs, ALU.mult)
                dve.tensor_tensor(TMP[1], bank[3][:, :], sn, ALU.mult)
                dve.tensor_tensor(TMP[2], bank[3][:, :], cs, ALU.mult)
                dve.tensor_tensor(TMP[3], bank[2][:, :], sn, ALU.mult).then_inc(bu_used, 1)
                dve.drain()
                dve.tensor_tensor(TMP[0], TMP[0], TMP[1], ALU.add)
                dve.tensor_tensor(TMP[2], TMP[2], TMP[3], ALU.subtract)
                dve.drain()
                dve.tensor_tensor_scan(TMP[1], rad.to_broadcast([P, T]), TMP[0], 0.0, ALU.mult, ALU.add)
                dve.tensor_tensor_scan(TMP[3], rad.to_broadcast([P, T]), TMP[2], 0.0, ALU.mult, ALU.add)
                dve.drain()

            def s5_turn_back(b, q):
                n = 4 * b + q
                cs, sn = ROT[q % 2]
                re, im = SS[q % 2]
                dve.wait_ge(y_done, n + 3)
                dve.tensor_tensor(re, TMP[1], cs, ALU.mult)
                dve.tensor_tensor(TMP[0], TMP[3], sn, ALU.mult)
                dve.tensor_tensor(im, TMP[3], cs, ALU.mult)
                dve.tensor_tensor(TMP[2], TMP[1], sn, ALU.mult)
                dve.drain()
                dve.tensor_tensor(re, re, TMP[0], ALU.subtract)
                dve.tensor_tensor(im, im, TMP[2], ALU.add).then_inc(ss_ready, 1)

            def head_body(b, last):
                for q in range(PPB):
                    da_row_max(b, q, 0)
                    s5_scan(b, q)
                    da_row_max(b, q, 1)
                    s5_turn_back(b, q)
                    da_combine(b, q)
                dve.wait_ge(y_done, 4 * b + 8)
                dve.scalar_tensor_tensor(one(U, b), one(U, b), column(b + V_SSMD), bank[4][:, :],
                                         ALU.mult, ALU.add).then_inc(y_used, 1)

            heads(dve, head_body)

            dve.wait_ge(hms_ready, 1)
            dve.tensor_scalar(HVAR, bank[6][:, 0:32], 1.0 / P, EPS, ALU.mult, ALU.add).then_inc(hvar_ready, 1)

            def glu(blk):
                s = blk % 4
                dve.wait_ge(evac_done[s], Q_GLU + blk // 4 + 1)
                dve.tensor_tensor(YS2[:, blk, :], VB[:, blk % 2, :], U[:, blk, :], ALU.mult).then_inc(ys_ready, 1)

            for blk in range(4):
                glu(blk)
            norm_mean(dve, 1, 2)
            for blk in range(4, KT):
                glu(blk)
            norm_apply(dve, 1, MEMN, MEMRAW, vec(V_MEM), MEM)
            for h in range(HEADS):
                dve.wait_ge(hbc_ready, h + 1)
                dve.scalar_tensor_tensor(YA[:, h, :], YA[:, h, :], HN08, bank[2 + h % 2][:, :],
                                         ALU.mult, ALU.mult).then_inc(ya_ready, 1)
            dve.wait_ge(gates_done, 1)
            for blk in range(KT):
                s = blk % 4
                dve.wait_ge(mm_done[s], Q_SSM + blk // 4 + 1)
                dve.tensor_tensor(MG[:, blk, :], RB[:, blk, :], bank[s % 2][:, :], ALU.mult).then_inc(evac_done[s], 1)
            for blk in range(KT):
                s = blk % 4
                dve.wait_ge(mm_done[s], Q_DA + blk // 4 + 1)
                dve.tensor_tensor(VB[:, blk, :], RB[:, 8 + blk, :], bank[s % 2][:, :], ALU.mult).then_inc(evac_done[s], 1)
                dve.drain()
                dve.tensor_tensor(MG[:, blk, :], MG[:, blk, :], VB[:, blk, :], ALU.add).then_inc(mg_ready, 1)
            norm_mean(dve, 2)
            residual_add(dve, 2, VB, vec(V_MIX_POST))
            norm_mean(dve, 3)
            norm_apply(dve, 3, HX, X, vec(V_X_PRE))
            for i in range(XH * TT + 1):
                if i < XH * TT:
                    at = i % 2
                    dve.wait_ge(xa_scores, i + 1)
                    dve.tensor_reduce(NMAX[:, at:at + 1], bank[2 + at][:, 0:MEM], AX.X, ALU.max,
                                      negate=True).then_inc(xa_max, 1)
                if i:
                    at = (i - 1) % 2
                    dve.wait_ge(xa_exp, i)
                    dve.reciprocal(RINV[:, at:at + 1], RSUM[:, at:at + 1])
                    dve.drain()
                    dve.tensor_scalar(PR[at][:, 0:MEM], PR[at][:, 0:MEM], RINV[:, at:at + 1], None,
                                      ALU.mult).then_inc(xa_probs, 1)
            norm_mean(dve, 4)
            residual_add(dve, 4, VB, vec(V_X_POST))
            norm_mean(dve, 5)
            norm_apply(dve, 5, H, X, vec(V_FF_PRE))
            norm_mean(dve, 6)
            residual_add(dve, 6, VB, vec(V_FF_POST))

            with dve.Fori(0, LAYERS) as L:
                q0 = dve.snap(QL * L + Q_L2)
                norm_mean(dve, L + 7)
                dve.wait_ge(lvec_in, 16 * L + 16)
                norm_apply(dve, L + 7, H, X, LVEC[:, L_NORM:L_NORM + KT])
                dve.memset(PA[:, 0:16], 0.0)
                dve.memset(PB[:, 0:16], 0.0)
                dve.memset(CP[:, 0:2], 0.0)
                dve.wait_ge(evac_done[3], q0 + 1)
                dve.wait_ge(lw_in, 16 * 5 * L + 80)
                kv = KCVC.rearrange("p (m b) -> p b m", b=16)
                for a in range(2):
                    op = dve.tensor_tensor(FLAT[:, 16 * a:16 * a + 16, :], kv[:, :, a:a + NC],
                                           POS[:, 16 * a:16 * a + 16].rearrange("p (l n) -> p l n", n=1)
                                           .to_broadcast([P, 16, NC]), ALU.add)
                op.then_inc(flat_ready, 1)
                dve.wait_ge(sw_ready, L + 1)
                dve.wait_ge(rope2_in, 16)
                for i in range(3):
                    dve.tensor_tensor(RTMP[:, i, :], RAW[:, i, :], COS, ALU.mult)
                dve.drain()
                for i in range(3):
                    op = dve.tensor_tensor(RAW[:, i, :], bank[(2, 3, 5)[i]][:, :], SIN, ALU.mult)
                op.then_inc(sw_used, 1)
                dve.drain()
                for i in range(2):
                    dve.tensor_tensor(NQ[:, i, :], RTMP[:, i, :], RAW[:, i, :], ALU.add)
                for dst, src in ((KS, 0), (KW, 64)):
                    for half in (0, 64):
                        op = dve.tensor_tensor(dst[half:half + 64, :], RTMP[src:src + 64, 2, :], RAW[src:src + 64, 2, :],
                                               ALU.add)
                op.then_inc(nq_ready, 1)
                dve.wait_ge(f_log, L + 1)
                dve.scalar_tensor_tensor(FZ, FZ, 0.0, FL, ALU.min, ALU.subtract)
                dve.drain()
                dve.tensor_tensor_scan(FL, ones.to_broadcast([P, T]), FZ, 0.0, ALU.mult, ALU.add)
                dve.drain()
                dve.tensor_scalar(FCQ, FL, CON[:, C_FQ:C_FQ + 1], CON[:, C_FK:C_FK + 1], ALU.mult, ALU.add)
                dve.tensor_scalar(FCK, FL, CON[:, C_NFK:C_NFK + 1], CON[:, C_FQ:C_FQ + 1], ALU.mult,
                                  ALU.add)
                dve.tensor_tensor(G12[:, :, 0:NH], G12[:, :, 0:NH],
                                  CON[:, C_VALID:C_VALID + TT].rearrange("p (t g) -> p t g", g=1)
                                  .to_broadcast([P, TT, NH]), ALU.mult)
                dve.drain()
                dve.sem_inc(f_ready, 1)
                for i in range(2):
                    dve.wait_ge(evac_done[i], q0 + 4)
                dve.wait_ge(hid_mm, L + 1)
                for i in range(2):
                    u = PIN[:, i, :]
                    dve.tensor_copy(PA[:, 16:528], u)
                    dve.drain()
                    dve.tensor_tensor(PB[:, 16:528], PA[:, 16:528], PA[:, 15:527], ALU.add)
                    dve.drain()
                    if i == 0:
                        dve.tensor_tensor(PA[64:128, 16:528], PB[64:128, 16:528], PB[64:128, 14:526], ALU.add)
                    else:
                        dve.tensor_tensor(PA[:, 16:528], PB[:, 16:528], PB[:, 14:526], ALU.add)
                        dve.drain()
                        dve.tensor_tensor(PB[:, 16:528], PA[:, 16:528], PA[:, 12:524], ALU.add)
                        dve.drain()
                        dve.tensor_tensor(PA[64:128, 16:528], PB[64:128, 16:528], PB[64:128, 8:520], ALU.add)
                    dve.drain()
                    for rows, s in ((slice(0, 64), PB), (slice(64, 128), PA)):
                        dve.scalar_tensor_tensor(RB[rows, 16 + i, 16:T], s[rows, 32:528], CON[rows, C_W + i:C_W + i + 1],
                                                 u[rows, 16:T], ALU.mult, ALU.subtract)
                        dve.tensor_tensor(s[rows, 16:32], s[rows, 16:32], CON[rows, C_INV + 16 * i:C_INV + 16 * i + 16],
                                          ALU.mult)
                    dve.drain()
                    for rows, s in ((slice(0, 64), PB), (slice(64, 128), PA)):
                        dve.tensor_tensor(RB[rows, 16 + i, 0:16], s[rows, 16:32], u[rows, 0:16], ALU.subtract)
                    dve.drain()
                dve.sem_inc(pooled_ready, 1)
                dve.wait_ge(kcs_mm, L + 1)
                ends = slice(CMP_LEN - 1, T, CMP_STRIDE)
                dve.tensor_tensor(KCT[:, 0:NC], KCR, COS[:, ends], ALU.mult)
                dve.tensor_tensor(KCT[:, 32:32 + NC], bank[6][:, 96:96 + NC], SIN[:, ends], ALU.mult)
                dve.drain()
                dve.tensor_tensor(KC, KCT[:, 0:NC], KCT[:, 32:32 + NC], ALU.add).then_inc(kc_ready, 1)
                for s in range(4):
                    dve.wait_ge(evac_done[s], q0 + 5)
                for i in range(2):
                    dve.tensor_tensor(CP[:, 2:514], CC[:, i, :], CX[:, i, :], ALU.mult)
                    dve.drain()
                    for tap in range(3):
                        w = LVEC[:, L_CONV + 2 * tap + i:L_CONV + 2 * tap + i + 1]
                        if tap == 0:
                            dve.tensor_scalar(OBR[:, 4 + i, :], CP[:, 0:T], w, None, ALU.mult)
                        else:
                            dve.scalar_tensor_tensor(OBR[:, 4 + i, :], CP[:, tap:tap + T], w, OBR[:, 4 + i, :],
                                                     ALU.mult, ALU.add)
                        dve.drain()
                    dve.tensor_tensor(OBR[:, 4 + i, :], OBR[:, 4 + i, :], CB[:, i, :], ALU.mult)
                    dve.drain()
                dve.wait_ge(pool_mm, L + 1)
                dve.sem_inc(conv_out, 1)

                for i in range(NS + 1):
                    if i < NS:
                        h, j, kind = STEPS[i]
                        width = NC if kind == "cmp" else (j + 1) * P
                        at = i % 2
                        dve.wait_ge(at_scores, L * NS + (i + 1))
                        dve.tensor_reduce(NMAX[:, at:at + 1], bank[2 + at][:, 0:width], AX.X, ALU.max,
                                          negate=True).then_inc(at_max, 1)
                    if i:
                        h, j, kind = STEPS[i - 1]
                        width = NC if kind == "cmp" else (j + 1) * P
                        at = (i - 1) % 2
                        dve.wait_ge(at_exp, L * NS + (i + 2))
                        dve.reciprocal(RINV[:, at:at + 1], RSUM[:, at:at + 1])
                        dve.drain()
                        pr = PR[at][:, 0:width]
                        if kind == "fox":
                            op = dve.tensor_scalar(pr, pr, RINV[:, at:at + 1], None, ALU.mult)
                        else:
                            g = NH * ("cmp", "slc", "win").index(kind) + h
                            op = dve.tensor_scalar(pr, pr, RINV[:, at:at + 1], G12[:, j, g:g + 1], ALU.mult, ALU.mult)
                        op.then_inc(at_probs, 1)
                dve.wait_ge(at_out, L * 8 + 10)
                for k in range(KT):
                    op = dve.tensor_tensor(OBR[:, k, :], OBR[:, k, :], U[:, k, :], ALU.mult)
                op.then_inc(obr_ready, 1)
                for ob in range(KT):
                    s, quad = ob % 4, q0 + (15 + ob // 4)
                    dve.wait_ge(sig_ready, L * KT + (ob + 1))
                    dve.wait_ge(mm_done[s], quad + 1)
                    for i in range(NBR):
                        op = dve.tensor_tensor(RB[:, 4 * ob + i, :], RB[:, 4 * ob + i, :],
                                               bank[4 * (ob % 2) + i][:, :], ALU.mult)
                    op.then_inc(evac_done[s], 1)
                    dve.drain()
                    for i in (0, 2):
                        dve.tensor_tensor(RB[:, 4 * ob + i, :], RB[:, 4 * ob + i, :], RB[:, 4 * ob + i + 1, :], ALU.add)
                    dve.drain()
                    dve.tensor_tensor(H[:, ob, :], RB[:, 4 * ob, :], RB[:, 4 * ob + 2, :], ALU.add).then_inc(acc_ready, 1)
                for blk in range(KT):
                    s = blk % 4
                    dve.wait_ge(mm_done[s], q0 + (18 + blk // 4))
                    op = dve.tensor_tensor(X[:, blk, :], X[:, blk, :], bank[s % 2][:, :], ALU.add)
                    op.then_inc(evac_done[s], 1)
                dve.drain()
                dve.sem_inc(x_ready, 1)
            norm_mean(dve, 9)
            norm_apply(dve, 9, H, X, vec(V_FINAL))

        @block.gpsimd
        def _(pool):
            pool.dma_start(CT, c_pad).then_inc(ct_in, 16)
            for q in range(PPB):
                pool.dma_start(BL[q], b_pad[q]).then_inc(bl_full[q], 16)
            for q in range(PPB):
                op = pool.memset(CL[q], 0.0)
            pool.drain()
            pool.sem_inc(cl_zero, 1)
            pool.sem_inc(y_done, 4)
            pool.sem_inc(da_pv, 2)
            pool.sem_inc(at_turned, 2)
            pool.sem_inc(at_pv, 2)
            pool.wait_ge(const_ready, 1)
            norm_root(pool, 0)

            def table(b, q):
                n = 4 * b + q

                def part(tab, c):
                    if isinstance(b, int):
                        return tab[:, n, c, :]
                    return tab[:, bass.ds(n, 1), c, :].rearrange("p a i -> p (a i)")

                hi = [part(HIT, c).rearrange("p (j i) -> p j i", i=1).to_broadcast([P, HI, LO]) for c in range(2)]
                lo = [part(LOT, c).rearrange("p (j i) -> p j i", j=1).to_broadcast([P, HI, LO]) for c in range(2)]
                to = [x.rearrange("p (j i) -> p j i", j=HI) for x in (*ROT[q % 2], *PTMP)]
                pool.wait_ge(ss_ready, n + 1)
                pool.tensor_tensor(to[0], hi[0], lo[0], ALU.mult)
                pool.tensor_tensor(to[2], hi[1], lo[1], ALU.mult)
                pool.tensor_tensor(to[1], hi[1], lo[0], ALU.mult)
                pool.tensor_tensor(to[3], hi[0], lo[1], ALU.mult)
                pool.drain()
                pool.tensor_tensor(to[0], to[0], to[2], ALU.subtract)
                pool.tensor_tensor(to[1], to[1], to[3], ALU.add).then_inc(tab_ready, 1)
                pool.drain()

            def rope(hd):
                for s in range(2):
                    pool.wait_ge(evac_done[s], hd + (Q_HEAD + 1))
                if not isinstance(hd, int):
                    pool.wait_ge(da_scores, 8 * hd)
                for raw, swapped in ((QRAW, QSW), (KRAW, KSW)):
                    pool.tensor_tensor(raw, raw, COS, ALU.mult)
                    pool.tensor_tensor(swapped, swapped, SIN, ALU.mult)
                pool.drain()
                pool.tensor_tensor(QH, QRAW, QSW, ALU.add)
                pool.tensor_tensor(KH, KRAW, KSW, ALU.add).then_inc(rope_done, 1)

            def head_body(b, last):
                for q in range(PPB):
                    table(b, q)
                    if not last:
                        pool.wait_ge(bu_ready, 4 * b + q + 1)
                        src = b_pad[4 * b + q + 4] if isinstance(b, int) else \
                            b_pad[bass.ds(4 * b + q + 4, 1)].rearrange("a p c m -> (a p) c m")
                        pool.dma_start(BL[q], src).then_inc(bl_full[q], 16)
                if not last:
                    rope(b + 1)

            rope(0)
            pool.wait_ge(prep_done, 1)
            heads(pool, head_body)
            for s in range(4):
                pool.wait_ge(mm_done[s], Q_GLU)
            pool.dma_start(MEMRAW, mem_in).then_inc(mem_loaded, 16)
            pool.wait_ge(da_scores, 8 * HEADS)
            pool.dma_start(TAB[:, :], rope2).then_inc(rope2_in, 16)
            pool.wait_ge(hvar_ready, 1)
            root(pool, HVAR, HR0, HRT, HRS).then_inc(hrs_ready, 1)
            norm_root(pool, 1, 2)
            norm_root(pool, 2)
            norm_root(pool, 3)
            norm_root(pool, 4)
            norm_root(pool, 5)
            with pool.Fori(0, Q_FF2 - Q_FF1) as f:
                for s in range(4):
                    pool.wait_ge(evac_done[s], f + (Q_FF1 + 1))
                    a = one(RB, 4 * f + s)
                    pool.tensor_tensor(a, a, a, ALU.mult).then_inc(ff_ready, 1)
            norm_root(pool, 6)
            with pool.Fori(0, LAYERS) as L:
                def layer(ap):
                    return ap[bass.ds(L, 1)].rearrange("a p n -> (a p) n")
                pool.wait_ge(x_ready, L + 3)
                pool.dma_start(LVEC[:, :], layer(lvecs)).then_inc(lvec_in, 16)
                for dst, src in ((W2K, cmp_w2k), (W2V, cmp_w2v), (B2V, cmp_b2v), (POS, cmp_pos), (LW[:, 288:544], pool_w)):
                    pool.dma_start(dst, layer(src)).then_inc(lw_in, 16)
                pool.dma_start(R[:, 24 * T:32 * T], layer(cmp_w1)).then_inc(w1_in, 16)
                norm_root(pool, L + 7)
            norm_root(pool, 9)


def tables():
    f = np.float32

    def angles(theta, half, dim):
        inv = (f(theta) ** (-np.arange(half, dtype=f) * f(2.0) / f(dim))).astype(f)
        return (np.arange(T, dtype=f)[None, :] * inv[:, None]).astype(f)

    a1 = angles(10000.0, DH // 2, DH)
    cos1, sin1 = np.cos(a1).astype(f), np.sin(a1).astype(f)
    rope1 = np.concatenate([np.tile(cos1, (4, 1)), np.concatenate([-sin1, sin1] * 2, 0)], 1)
    a2 = angles(500000.0, 8, 16)
    cos2, sin2 = np.cos(a2).astype(f), np.sin(a2).astype(f)
    c = np.concatenate([cos2, cos2, np.ones((48, T), f)], 0)
    s = np.concatenate([-sin2, sin2, np.zeros((48, T), f)], 0)
    rope2 = np.concatenate([np.tile(c, (2, 1)), np.tile(s, (2, 1))], 1)

    con = np.zeros((P, C_END), f)
    con[:, C_ID:C_ID + P] = np.eye(P, dtype=f)
    i, j = np.arange(P)[:, None], np.arange(P)[None, :]
    con[:, C_CAUSAL:C_CAUSAL + P] = np.where(j > i, MASKED, 0)
    con[:, C_CHUNK:C_CHUNK + P] = np.where(j // 64 > i // 64, MASKED, 0)
    for base in (0, 64):
        for d in range(16):
            con[base + d, C_SWAP + base + (d + 8) % 16] = 1
    ends = np.arange(NC) * CMP_STRIDE + CMP_LEN - 1
    for t in range(TT):
        tok = t * P + np.arange(P)
        con[:, C_CMP + 32 * t:C_CMP + 32 * t + NC] = np.where(ends[None, :] <= tok[:, None], 0, MASKED)
        con[:, C_VALID + t] = tok >= ends[0]
    for h in range(4):
        con[32 * h, C_FQ] = 1
        con[32 * h + 1, C_FK] = 1
        con[32 * h + 1, C_NFK] = -1
    for blk in range(2):
        for half in range(2):
            w = (2, 4, 8, 16)[2 * blk + half]
            rows = slice(64 * half, 64 * half + 64)
            con[rows, C_W + blk] = 1 / w
            con[rows, C_INV + 16 * blk:C_INV + 16 * blk + 16] = 1 / np.minimum(np.arange(1, 17), w)
    return rope1.astype(f), rope2.astype(f), con


def stream(w):
    k, n = w.shape
    return w.reshape(k // P, P, n // P, P).transpose(2, 1, 0, 3)


def by_partition(v):
    return v.reshape(-1, P).T


def kernel(x, mem, norm_mix_pre, w_in, b_gate, ssm_lambda_re, ssm_lambda_im, ssm_log_dt,
           ssm_b_re, ssm_b_im, ssm_c_re, ssm_c_im, ssm_d, w_glu, b_glu, w_ssm_proj,
           da_lambda_q1, da_lambda_k1, da_lambda_q2, da_lambda_k2, da_head_norm, w_da_proj,
           w_mix_out, norm_mix_post, norm_x_pre, norm_mem, w_xq, w_xkv, w_xo, norm_x_post,
           norm_ff_pre, w_ff1, w_ff2, norm_ff_post, norm_g_2, w_in_2, fox_f_bias_2, cmp_pos_2,
           cmp_w1_2, cmp_b1_2, cmp_w2_2, cmp_b2_2, pool_w_2, pool_scale_2, conv_w_2, w_branch_2,
           w_out_2, final_norm_g_2):
    import concourse.bacc as bacc
    from concourse.bass_utils import run_bass_kernel_spmd

    f = np.float32
    npa = lambda a: np.asarray(a)
    cat = np.concatenate

    wi = stream(npa(w_in)[0])
    u_blk, q_blk, k_blk, v_blk, ga, gb = (wi[i * 8:(i + 1) * 8] for i in range(6))
    per_head = np.stack([q_blk, k_blk, ga, v_blk], 1).reshape(32, P, KT, P)
    wkv = stream(npa(w_xkv)[0])
    ff2 = stream(npa(w_ff2)[0]).reshape(8, P, 4, KT, P).transpose(0, 2, 1, 3, 4).reshape(32, P, KT, P)
    parts = [u_blk, gb, per_head, stream(npa(w_glu)[0]), stream(npa(w_ssm_proj)[0]),
             stream(npa(w_da_proj)[0]), stream(npa(w_mix_out)[0]), wkv, stream(npa(w_xq)[0]),
             stream(npa(w_xo)[0]), stream(npa(w_ff1)[0]), ff2]
    kv0, pool0, conv0, fox0, gate0, merge0 = 256, 652, 908, 1676, 2448, 3472
    r = lambda a, n: list(range(a, a + n))
    kvc = lambda i: r(kv0 + 64 * i, 64)
    small = [-1] * P
    for h in range(4):
        small[32 * h] = small[32 * h + 1] = 2444 + h
    for g in range(12):
        small[2 + g] = 640 + g
    cols = (r(0, 256) + kvc(2) + kvc(4) + kvc(0) + kvc(1) + kvc(3) + kvc(5) + small
            + r(fox0, 768) + r(pool0, 256) + r(conv0, 768) + r(gate0, 1024))
    for ob in range(8):
        for i in range(4):
            cols += r(merge0 + i * D + ob * P, P)
    cols = np.array(cols)
    for l in range(LAYERS):
        w = npa(w_in_2)[l]
        w = cat([w, np.zeros((D, 1), w.dtype)], 1)[:, cols]
        parts.append(stream(w))
        parts.append(npa(w_branch_2)[l].reshape(4, 2, P, 8, P).transpose(3, 2, 0, 1, 4).reshape(8, P, KT, P))
        parts.append(stream(npa(w_out_2)[l]))
    weights = np.ascontiguousarray(cat(parts, 0))
    assert weights.shape[0] == 4 * Q_END

    pad64 = lambda v: cat([npa(v)[0], np.zeros(64, f)])[:, None]
    state = lambda a: npa(a)[0].reshape(PAIRS, P).T
    ldt = np.repeat(npa(ssm_log_dt)[0], STATE).reshape(PAIRS, P).T
    vecs = cat([by_partition(npa(norm_mix_pre)[0]), by_partition(npa(b_gate)[0]), by_partition(npa(ssm_d)[0]),
                by_partition(npa(b_glu)[0]), by_partition(npa(norm_mix_post)[0]), by_partition(npa(norm_x_pre)[0]),
                by_partition(npa(norm_mem)[0]), by_partition(npa(norm_x_post)[0]), by_partition(npa(norm_ff_pre)[0]),
                by_partition(npa(norm_ff_post)[0]), npa(da_head_norm)[0][:, None],
                pad64(da_lambda_q1), pad64(da_lambda_k1), pad64(da_lambda_q2), pad64(da_lambda_k2),
                by_partition(npa(final_norm_g_2)), state(ssm_lambda_re), state(ssm_lambda_im), ldt], 1)

    b_pad = np.zeros((PAIRS, P, 2, P), f)
    c_pad = np.zeros((P, PAIRS, 2, 32), f)
    for n in range(PAIRS):
        for g2 in range(2):
            rows = slice(32 * (n % 4) + 16 * g2, 32 * (n % 4) + 16 * g2 + 16)
            st = slice(64 * g2, 64 * g2 + 64)
            for c, (b, cc) in enumerate(((ssm_b_re, ssm_c_re), (ssm_b_im, ssm_c_im))):
                b_pad[n, rows, c, st] = npa(b)[0, 2 * n + g2].T
                c_pad[st, n, c, 16 * g2:16 * g2 + 16] = npa(cc)[0, 2 * n + g2].T

    lv = np.zeros((LAYERS, P, L_END), f)
    pw = np.zeros((LAYERS, P, 2, P), f)
    for l in range(LAYERS):
        lv[l, :, L_NORM:L_NORM + 8] = by_partition(npa(norm_g_2)[l])
        lv[l, :, L_POOL:L_POOL + 2] = by_partition(npa(pool_scale_2)[l])
        for tap in range(3):
            lv[l, :, L_CONV + 2 * tap:L_CONV + 2 * tap + 2] = by_partition(npa(conv_w_2)[l, tap])
        for h in range(4):
            lv[l, 32 * h:32 * h + 2, L_FBIAS] = npa(fox_f_bias_2)[l, h]
        lv[l, :, L_B1:L_B1 + 2] = npa(cmp_b1_2)[l].T
        for half in (0, 64):
            lv[l, half:half + 64, L_B2K] = npa(cmp_b2_2)[l, 0]
        for i in range(4):
            rows = slice(64 * (i % 2), 64 * (i % 2) + 64)
            pw[l, rows, i // 2, rows] = npa(pool_w_2)[l, i]
    cw1 = npa(cmp_w1_2).reshape(LAYERS, 2, CMP_LEN, 64, P).transpose(0, 1, 3, 2, 4).reshape(LAYERS, P, CMP_LEN * P)
    pos = npa(cmp_pos_2).transpose(0, 1, 3, 2).reshape(LAYERS, P, CMP_LEN)
    w2k = cat([npa(cmp_w2_2)[:, 0]] * 2, 2)
    w2v = npa(cmp_w2_2)[:, 1]
    b2v = npa(cmp_b2_2)[:, 1:2]
    rope1, rope2, con = tables()

    feat = lambda a: npa(a)[0].T.reshape(KT, P, -1).transpose(1, 0, 2)
    arrays = {
        "x_in": feat(x), "mem_in": feat(mem), "weights": weights, "vecs": vecs, "lvecs": lv, "consts": con,
        "rope1": rope1, "rope2": rope2, "b_pad": b_pad, "c_pad": c_pad, "cmp_w1": cw1, "cmp_pos": pos,
        "cmp_w2k": w2k, "cmp_w2v": w2v, "cmp_b2v": b2v, "pool_w": pw.reshape(LAYERS, P, 2 * P),
    }
    arrays = {k: np.ascontiguousarray(v) for k, v in arrays.items()}
    nc = bacc.Bacc("TRN2", target_bir_lowering=False, num_devices=1)
    args = {k: nc.dram_tensor(k, v.shape, mybir.dt.from_np(v.dtype), kind="ExternalInput").ap()
            for k, v in arrays.items()}
    out = nc.dram_tensor("out", (P, KT, T), F32, kind="ExternalOutput").ap()
    build(nc, out=out, **args)
    res = run_bass_kernel_spmd(nc, [arrays], core_ids=[0])
    got = res.results[0]["out"]
    return got.transpose(2, 1, 0).reshape(1, T, D)
```

```python
from contextlib import ExitStack

import numpy as np

import concourse.bass as bass
from concourse import mybir

F32 = mybir.dt.float32
F32R = mybir.dt.float32r
ALU = mybir.AluOpType
ACT = mybir.ActivationFunctionType
AX = mybir.AxisListType

P = 128
D = 1024
T = 512
KT = D // P
TT = T // P
MEM = 256
EPS = 1e-6
MASKED = -1e30

HEADS = 8
DH = 64
GROUPS, STATE, GW = 64, 64, 16
PAIRS = GROUPS // 2
PPB = 4
LO, HI = 16, 32
LAM_INIT = 0.8 - 0.6
XH = 4
XD = D // XH

LAYERS = 2
NH = 4
CMP_LEN, CMP_STRIDE = 32, 16
NC = (T - CMP_LEN) // CMP_STRIDE + 1
NBR = 4

Q_U, Q_GB, Q_HEAD = 0, 2, 4
Q_GLU, Q_DA, Q_SSM, Q_MIX = 12, 14, 16, 18
Q_KX, Q_VX, Q_XQ, Q_XO = 20, 22, 24, 26
Q_FF, Q_L2 = 28, 44
Q_SPLIT = Q_GLU
FF_ORDER = ((1, 0), (1, 1), (2, 0), (1, 2), (2, 1), (1, 3), (2, 2), (2, 3))
S_YSG, S_YA, S_MEMN, S_YS2, S_MG, S_HX, S_OX, S_HF, S_L2 = (KT * i for i in range(9))
S_H, S_OBR, S_ACC, SL = (KT * i for i in range(4))
QL = 19
Q_END = Q_L2 + LAYERS * QL

V_MIX_PRE, V_BGATE, V_SSMD, V_BGLU, V_MIX_POST = 0, 8, 24, 32, 40
V_X_PRE, V_MEM, V_X_POST, V_FF_PRE, V_FF_POST = 48, 56, 64, 72, 80
V_HEADNORM, V_LQ1, V_LK1, V_LQ2, V_LK2, V_FINAL = 88, 89, 90, 91, 92, 93
V_LRE, V_LIM, V_LDT = 101, 133, 165
V_END = 197
L_NORM, L_POOL, L_CONV, L_FBIAS, L_B1, L_B2K = 0, 8, 10, 16, 17, 19
L_END = 20
C_ID, C_CAUSAL, C_CHUNK, C_SWAP = 0, 128, 256, 384
C_CMP = 512
C_VALID = 640
C_FQ, C_FK, C_NFK = 644, 645, 646
C_INV = 648
C_W = 680
C_END = 682


def build(nc, x_in, mem_in, weights, vecs, lvecs, consts, rope1, rope2, b_pad, c_pad,
          cmp_w1, cmp_pos, cmp_w2k, cmp_w2v, cmp_b2v, pool_w, out):
    ctx = ExitStack()
    with ctx:
        place = {"end": 16512}

        def sb(name, cols):
            place[name] = place["end"]
            place["end"] += -(-4 * cols // 32) * 32
            assert place["end"] <= 229344
            return nc.alloc_sbuf_tensor_at(name, [P, cols], F32, offset=place[name])

        def rounded(name, home, first, n, width=T):
            t = nc.alloc_sbuf_tensor_at(name, [P, n * width], F32R, offset=place[home] + 4 * T * first)
            return t[:, :].rearrange("p (k t) -> p k t", k=n, t=width)

        def sem(name):
            return ctx.enter_context(nc.semaphore(name))

        def sems(name, n):
            return [sem(f"{name}{i}") for i in range(n)]

        def blocks(ap, n, width=T):
            return ap.rearrange("p (k t) -> p k t", k=n, t=width)

        X = blocks(sb("residual", KT * T)[:, :], KT)
        H_ = sb("normed", KT * T)
        H = blocks(H_[:, :], KT)
        SLOTS = sb("weight_slots", 4 * KT * P)
        slot = [blocks(SLOTS[:, s * KT * P:(s + 1) * KT * P], KT, P) for s in range(4)]
        U_ = sb("u_region", KT * T)
        U = blocks(U_[:, :], KT)
        R = sb("wide_region", 32 * T)
        RB = blocks(R[:, :], 32)
        R3 = sb("work_region", 16 * T)
        WB = blocks(R3[:, :], 16)
        V_ = sb("v_region", KT * T)
        VB = blocks(V_[:, :], KT)
        TAB = sb("rope_tables", 2 * T)
        COS, SIN = TAB[:, 0:T], TAB[:, T:2 * T]
        EX = blocks(sb("attention_work", 11 * T)[:, :], 11)
        VEC = sb("vectors", V_END)
        LVEC = sb("layer_vectors", L_END)
        CON = sb("constants", C_END)
        SMALL = sb("small", 240)

        ident = CON[:, C_ID:C_ID + P]
        ones = SMALL[:, 0:1]
        VAR, R0, RT, RSTD = SMALL[:, 4:8], SMALL[:, 8:12], SMALL[:, 12:16], SMALL[:, 16:20]
        HALF = SMALL[:, 20:52]
        HVAR, HR0, HRT, HRS = (SMALL[:, 52 + 32 * i:84 + 32 * i] for i in range(4))
        NMAX, RSUM, RINV = SMALL[:, 180:184], SMALL[:, 184:188], SMALL[:, 188:192]
        LAMP, LAME, NLAM, HN08 = SMALL[:, 192:194], SMALL[:, 194:196], SMALL[:, 196:197], SMALL[:, 197:198]
        ONE_ROW = SMALL[0:1, 200:232]

        bank = [ctx.enter_context(nc.psum_tensor(f"bank{i}", [P, T], F32)) for i in range(8)]

        TMP = [WB[:, i, :] for i in range(4)]
        ROT = [[WB[:, 6 + 2 * d + c, :] for c in range(2)] for d in range(2)]
        SS = [[WB[:, 10 + 2 * d + c, :] for c in range(2)] for d in range(2)]
        PTMP = [WB[:, 14 + c, :] for c in range(2)]
        S5C = R[:, 24 * T:32 * T]
        CT = S5C[:, 0:2048].rearrange("p (n c m) -> p n c m", n=PAIRS, c=2)
        BL = [S5C[:, 2048 + 256 * q:2304 + 256 * q].rearrange("p (c m) -> p c m", c=2) for q in range(PPB)]
        CL = [S5C[:, 3072 + 256 * q:3328 + 256 * q].rearrange("p (c m) -> p c m", c=2) for q in range(PPB)]
        LOT = V_[:, 0:1024].rearrange("p (n c i) -> p n c i", n=PAIRS, c=2)
        HIT = V_[:, 1024:3072].rearrange("p (n c j) -> p n c j", n=PAIRS, c=2)
        PREP = V_[:, 3072:4096].rearrange("p (a n) -> p a n", a=32)
        RADIUS = PREP[:, 0, :]

        WH = [rounded(f"weight_hi{i}", "attention_work", 2 * i, KT, P) for i in range(2)]
        WL = [rounded(f"weight_lo{i}", "attention_work", 4 + 2 * i, KT, P) for i in range(2)]
        YSG_HI, YSG_LO = rounded("gelu_hi", "wide_region", 24, 8), rounded("gelu_lo", "work_region", 0, 8)
        YA_HI, YA_LO = rounded("ya_hi", "work_region", 8, 8), rounded("ya_lo", "wide_region", 16, 8)
        MEMN_HI, MEMN_LO = rounded("memn_hi", "normed", 0, KT, MEM), rounded("memn_lo", "normed", 4, KT, MEM)
        YS2_HI, YS2_LO = rounded("ys2_hi", "wide_region", 24, 8), rounded("ys2_lo", "u_region", 0, 8)
        MG_HI, MG_LO = rounded("mg_hi", "v_region", 0, 8), rounded("mg_lo", "work_region", 0, 8)
        HX_HI, HX_LO = rounded("hx_hi", "wide_region", 16, 8), rounded("hx_lo", "wide_region", 8, 8)
        OX_HI, OX_LO = rounded("ox_hi", "v_region", 0, 8), rounded("ox_lo", "normed", 0, 8)
        H_HI, H_LO = rounded("h_hi", "v_region", 0, 8), rounded("h_lo", "normed", 0, 8)
        F_HI = [rounded(f"ff_hi{i}", "wide_region", 16 * i + 8, 8) for i in range(2)]
        F_LO = [rounded(f"ff_lo{i}", "wide_region", 16 * i, 8) for i in range(2)]
        OBR_HI, OBR_LO = rounded("obr_hi", "wide_region", 16, 8), rounded("obr_lo", "wide_region", 24, 8)
        ACC_HI, ACC_LO = rounded("acc_hi", "v_region", 0, 8), rounded("acc_lo", "u_region", 0, 8)

        QRAW, QSW, KRAW, KSW, QH, KH, VH = (EX[:, i, :] for i in range(7))
        PR = [EX[:, 7, :], EX[:, 8, :]]
        PC = WB[:, 4, :]
        PTB = [EX[:, 9, :], EX[:, 10, :]]
        YA = RB[:, 16:24, :]
        YS2 = U
        PAIR = [EX[:, 8, :], EX[:, 9, :]]
        MG = WB[:, 0:8, :]
        SQ = WB[:, 8:16, :]
        MEMRAW, MEMN = blocks(V_[:, 2048:4096], KT, MEM), blocks(H_[:, 2048:4096], KT, MEM)
        MSQ = blocks(V_[:, 0:2048], KT, MEM)
        KX, VX = blocks(U_[:, 0:2048], KT, MEM), blocks(U_[:, 2048:4096], 2, D)
        YB = RB[:, 0:8, :]
        HX, QX = RB[:, 8:16, :], RB[:, 24:32, :]
        YF = U
        RELU = [EX[:, 8 + i, :] for i in range(3)]
        APR, APT = [EX[:, 8, :], EX[:, 9, :]], [EX[:, 10, :], WB[:, 15, :]]

        NQ, KS, KW, VSW = WB[:, 0:2, :], WB[:, 2, :], WB[:, 3, :], WB[:, 4, :]
        FQ, FK, FV = WB[:, 5:7, :], WB[:, 7:9, :], WB[:, 9:11, :]
        FCQ, FCK, KCVC = WB[:, 11, :], WB[:, 12, :], WB[:, 13, :]
        CW = R3[:, 14 * T:15 * T]
        G12 = CW[:, 0:64].rearrange("p (t g) -> p t g", t=TT)
        HID, KCR, KC, VC, KCT = CW[:, 64:128], CW[:, 128:128 + NC], CW[:, 160:160 + NC], CW[:, 192:256], CW[:, 256:320]
        RAW, RTMP = RB[:, 8:11, :], RB[:, 11:14, :]
        FZ, FL = RB[:, 14, :], RB[:, 15, :]
        FLAT = R[:, 16 * T:16 * T + CMP_LEN * NC].rearrange("p (l n) -> p l n", l=CMP_LEN)
        LW = R[:, 18 * T:20 * T]
        W2K, W2V, B2V, POS = LW[:, 0:128], LW[:, 128:192], LW[0:1, 192:256], LW[:, 256:288]
        PW = LW[:, 288:544].rearrange("p (b n) -> p b n", b=2)
        PA, PB = R[:, 20 * T:20 * T + 528], R[:, 20 * T + 528:20 * T + 1056]
        CP = R[:, 20 * T + 1056:20 * T + 1570]
        W1 = R[:, 24 * T:32 * T].rearrange("p (l n) -> p l n", l=CMP_LEN)
        PIN, CX, CB, CC = RB[:, 0:2, :], RB[:, 2:4, :], RB[:, 4:6, :], RB[:, 6:8, :]
        OBR = RB[:, 24:32, :]
        ACC = U
        ML = [RB[:, i, :] for i in range(16)] + [WB[:, i, :] for i in range(16)]

        w_full, mm_done, evac_done = sems("w_full", 4), sems("mm_done", 4), sems("evac_done", 4)
        x_loaded, consts_in, mem_loaded, rope2_in, out_stored = (
            sem("x_loaded"), sem("consts_in"), sem("mem_loaded"), sem("rope2_in"), sem("out_stored"))
        const_ready = sem("const_ready")
        w_hi, w_lo = sems("w_hi", 4), sems("w_lo", 4)
        t_ready, hi_ready, lo_ready = sem("t_ready"), sem("hi_ready"), sem("lo_ready")
        sq_ready, ms_ready, var_ready = sem("sq_ready"), sem("ms_ready"), sem("var_ready")
        rstd_ready, bc_ready, bc_used = sem("rstd_ready"), sem("bc_ready"), sem("bc_used")
        x_ready = sem("x_ready")
        cl_zero, prep_dt, prep_exp, prep_arg, prep_sin, prep_done = (
            sem("cl_zero"), sem("prep_dt"), sem("prep_exp"), sem("prep_arg"), sem("prep_sin"), sem("prep_done"))
        ct_in = sem("ct_in")
        bl_full = sems("bl_full", PPB)
        bu_ready, bu_used, tab_ready, ss_ready = sem("bu_ready"), sem("bu_used"), sem("tab_ready"), sem("ss_ready")
        cl_ready, y_done, y_used = sem("cl_ready"), sem("y_done"), sem("y_used")
        lam_prod, lam_sum, lam_exp = sem("lam_prod"), sem("lam_sum"), sem("lam_exp")
        rope_done, da_scores, da_max, da_exp = sem("rope_done"), sem("da_scores"), sem("da_max"), sem("da_exp")
        da_probs, da_turned, da_copied, da_pv, da_out = (
            sem("da_probs"), sem("da_turned"), sem("da_copied"), sem("da_pv"), sem("da_out"))
        hsq_ready, hms_ready, hvar_ready, hrs_ready, hbc_ready, ya_ready = (
            sem("hsq_ready"), sem("hms_ready"), sem("hvar_ready"), sem("hrs_ready"), sem("hbc_ready"), sem("ya_ready"))
        gates_done, ys_ready = sem("gates_done"), sem("ys_ready")
        xa_scores, xa_max, xa_exp, xa_probs, xa_turned, xa_copied, xa_pv, xa_out = (
            sem("xa_scores"), sem("xa_max"), sem("xa_exp"), sem("xa_probs"), sem("xa_turned"),
            sem("xa_copied"), sem("xa_pv"), sem("xa_out"))
        ff_hi, ff_lo, ff_out = sem("ff_hi"), sem("ff_lo"), sem("ff_out")
        lw_in, w1_in, lvec_in = sem("lw_in"), sem("w1_in"), sem("lvec_in")
        sw_ready, sw_used, nq_ready, f_log, f_ready = (
            sem("sw_ready"), sem("sw_used"), sem("nq_ready"), sem("f_log"), sem("f_ready"))
        flat_ready, hid_mm, hid_ready, kv2_mm, kcr_ready, kcs_mm, kc_ready = (
            sem("flat_ready"), sem("hid_mm"), sem("hid_ready"), sem("kv2_mm"), sem("kcr_ready"),
            sem("kcs_mm"), sem("kc_ready"))
        pooled_ready, pool_mm, pool_out, conv_out = sem("pooled_ready"), sem("pool_mm"), sem("pool_out"), sem("conv_out")
        at_scores, at_max, at_exp, at_probs, at_turned, at_copied, at_pv, at_out = (
            sem("at_scores"), sem("at_max"), sem("at_exp"), sem("at_probs"), sem("at_turned"),
            sem("at_copied"), sem("at_pv"), sem("at_out"))
        silu_done, sig_ready = sem("silu_done"), sem("sig_ready")

        def bank_free(pe, quad, s):
            if s >= 2:
                pe.wait_ge(evac_done[s - 2], quad + 1)
            elif not (isinstance(quad, int) and quad == 0):
                pe.wait_ge(evac_done[s + 2], quad)

        def gemm(pe, quad, s, rhs, width=T):
            pe.wait_ge(w_full[s], 16 * quad + 16)
            bank_free(pe, quad, s)
            for k in range(KT):
                mm = pe.matmul(bank[s % 2][:, 0:width], slot[s][:, k, :], rhs[:, k, 0:width],
                               start=(k == 0), stop=(k == KT - 1))
            mm.then_inc(mm_done[s], 1)

        def gemm_tokens(pe, quad, s, lhs, tiles=TT):
            pe.wait_ge(w_full[s], 16 * quad + 16)
            bank_free(pe, quad, s)
            for t in range(tiles):
                for k in range(KT):
                    mm = pe.matmul(bank[s % 2][:, t * P:(t + 1) * P], lhs[:, k, t * P:(t + 1) * P],
                                   slot[s][:, k, :], start=(k == 0), stop=(k == KT - 1))
            mm.then_inc(mm_done[s], 1)

        def gemm_split(pe, quad, s, hi, lo, width=T, stage=None):
            pe.wait_ge(w_lo[s], quad + (1 - Q_SPLIT))
            bank_free(pe, quad, s)
            to = bank[s % 2][:, 0:width]
            for k in range(KT):
                if stage is not None:
                    pe.wait_ge(lo_ready, stage + (k + 1))
                pe.matmul(to, WH[s % 2][:, k, :], hi[:, k, 0:width], start=(k == 0), stop=False)
                pe.matmul(to, WH[s % 2][:, k, :], lo[:, k, 0:width], start=False, stop=False)
                mm = pe.matmul(to, WL[s % 2][:, k, :], hi[:, k, 0:width], start=False, stop=(k == KT - 1))
            mm.then_inc(mm_done[s], 1)

        def gemm_tokens_split(pe, quad, s, hi, lo, tiles=TT):
            pe.wait_ge(w_lo[s], quad + (1 - Q_SPLIT))
            bank_free(pe, quad, s)
            for t in range(tiles):
                to, at = bank[s % 2][:, t * P:(t + 1) * P], slice(t * P, (t + 1) * P)
                for k in range(KT):
                    pe.matmul(to, hi[:, k, at], WH[s % 2][:, k, :], start=(k == 0), stop=False)
                    pe.matmul(to, hi[:, k, at], WL[s % 2][:, k, :], start=False, stop=False)
                    mm = pe.matmul(to, lo[:, k, at], WH[s % 2][:, k, :], start=False, stop=(k == KT - 1))
            mm.then_inc(mm_done[s], 1)

        def both(pe, quad, hi, lo, stage, width=T):
            for i in range(2):
                for s in range(4):
                    gemm_split(pe, quad + i, s, hi, lo, width, stage if i == 0 and s == 0 else None)

        def weight_hi(act, quad, s):
            act.wait_ge(w_full[s], 16 * quad + 16)
            if s >= 2:
                act.wait_ge(mm_done[s - 2], quad + 1)
            else:
                act.wait_ge(mm_done[s + 2], quad)
            act.activation(WH[s % 2], slot[s], ACT.Copy).then_inc(w_hi[s], 1)

        def weight_lo(pool, quad, s):
            pool.wait_ge(w_hi[s], quad + (1 - Q_SPLIT))
            pool.tensor_tensor(WL[s % 2], slot[s], WH[s % 2].bitcast(F32), ALU.subtract).then_inc(w_lo[s], 1)

        def ahead(act, quad, s):
            if s < 2:
                weight_hi(act, quad, s + 2)
            else:
                weight_hi(act, quad + 1, s - 2)

        def round_hi(act, stage, k, hi, t):
            act.wait_ge(t_ready, stage + (k + 1))
            act.activation(hi, t, ACT.Copy).then_inc(hi_ready, 1)

        def rest_lo(dve, stage, k, lo, t, hi):
            dve.wait_ge(hi_ready, stage + (k + 1))
            dve.tensor_tensor(lo, t, hi.bitcast(F32), ALU.subtract).then_inc(lo_ready, 1)

        def squares(act, src, width=T, to=SQ):
            for k in range(KT):
                op = act.activation(to[:, k, 0:width], src[:, k, 0:width], ACT.Square)
            op.then_inc(sq_ready, 1)

        def norm_sums(pe, n, tiles=TT, squared=SQ):
            pe.wait_ge(sq_ready, n + 1)
            if not (isinstance(n, int) and n == 0):
                pe.wait_ge(var_ready, n)
            for t in range(tiles):
                for k in range(KT):
                    mm = pe.matmul(bank[6][:, t:t + 1], squared[:, k, t * P:(t + 1) * P], ones,
                                   start=(k == 0), stop=(k == KT - 1))
            mm.then_inc(ms_ready, 1)

        def norm_mean(dve, n, tiles=TT):
            dve.wait_ge(ms_ready, n + 1)
            if not (isinstance(n, int) and n == 0):
                dve.wait_ge(rstd_ready, n)
            dve.tensor_scalar(VAR[:, 0:tiles], bank[6][:, 0:tiles], 1.0 / D, EPS, ALU.mult,
                              ALU.add).then_inc(var_ready, 1)

        def root(pool, v, r0, rt, rs):
            pool.tensor_tensor(r0, v, HALF[:, 0:v.shape[-1]], ALU.pow)
            pool.drain()
            pool.tensor_tensor(rt, r0, r0, ALU.mult)
            pool.drain()
            pool.tensor_tensor(rt, rt, v, ALU.mult)
            pool.drain()
            pool.tensor_scalar(rt, rt, -0.5, 1.5, ALU.mult, ALU.add)
            pool.drain()
            return pool.tensor_tensor(rs, rt, r0, ALU.mult)

        def norm_root(pool, n, tiles=TT):
            pool.wait_ge(var_ready, n + 1)
            if not (isinstance(n, int) and n == 0):
                pool.wait_ge(bc_ready, n)
            root(pool, VAR[:, 0:tiles], R0[:, 0:tiles], RT[:, 0:tiles],
                 RSTD[:, 0:tiles]).then_inc(rstd_ready, 1)

        def norm_spread(pe, n, tiles=TT):
            pe.wait_ge(rstd_ready, n + 1)
            if not (isinstance(n, int) and n == 0):
                pe.wait_ge(bc_used, n)
            for t in range(tiles):
                mm = pe.matmul(bank[7][:, t * P:(t + 1) * P],
                               RSTD[:, t:t + 1].to_broadcast([P, P]), ident, start=True, stop=True)
            mm.then_inc(bc_ready, 1)

        def norm_apply(dve, n, dst, src, gain, width=T):
            dve.wait_ge(bc_ready, n + 1)
            for k in range(KT):
                op = dve.scalar_tensor_tensor(dst[:, k, 0:width], src[:, k, 0:width], gain[:, k:k + 1],
                                              bank[7][:, 0:width], ALU.mult, ALU.mult)
            op.then_inc(bc_used, 1)
            return op

        def norm_split(dve, n, stage, t, hi, lo, src, gain, width=T):
            dve.wait_ge(bc_ready, n + 1)
            for k in range(KT + 2):
                if k < KT:
                    dve.scalar_tensor_tensor(t[:, k, 0:width], src[:, k, 0:width], gain[:, k:k + 1],
                                             bank[7][:, 0:width], ALU.mult, ALU.mult).then_inc(t_ready, 1)
                if k >= 2:
                    rest_lo(dve, stage, k - 2, lo[:, k - 2, :], t[:, k - 2, :], hi[:, k - 2, :])
            dve.sem_inc(bc_used, 1)

        def residual_add(dve, n, y, gain):
            norm_apply(dve, n, y, y, gain)
            dve.drain()
            for k in range(KT):
                op = dve.tensor_tensor(X[:, k, :], X[:, k, :], y[:, k, :], ALU.add)
            op.then_inc(x_ready, 1)

        def copy_out(act, quad, s, dst, scale=1.0):
            act.wait_ge(mm_done[s], quad + 1)
            act.activation(dst, bank[s % 2][:, 0:dst.shape[-1]], ACT.Copy, scale=scale).then_inc(evac_done[s], 1)

        def one(ap, i):
            if isinstance(i, int):
                return ap[:, i, :]
            return ap[:, bass.ds(i, 1), :].rearrange("p a t -> p (a t)")

        def column(i):
            return VEC[:, i:i + 1] if isinstance(i, int) else VEC[:, bass.ds(i, 1)]

        def vec(col, n=KT):
            return VEC[:, col:col + n]

        def heads(eng, body):
            with eng.Fori(0, HEADS - 1) as b:
                body(b, False)
            body(HEADS - 1, True)

        STEPS = [(h, j, kind) for h in range(NH) for j in range(TT) for kind in ("cmp", "slc", "win", "fox")]
        NS = len(STEPS)
        FILL = 20

        def filler(i):
            if i >= NS or (i + 1) * FILL // NS == i * FILL // NS:
                return None
            return i * FILL // NS

        block = ctx.enter_context(nc.Block())

        @block.sync
        def _(sp):
            for s in range(4):
                sp.dma_start(slot[s], weights[s]).then_inc(w_full[s], 16)
            with sp.Fori(1, Q_SPLIT + 1) as quad:
                for s in range(4):
                    src = sp.snap(quad * 4 + s)
                    need = sp.snap(quad + 0)
                    sp.wait_ge(mm_done[s], need)
                    sp.dma_start(slot[s], weights[bass.ds(src, 1)].rearrange("a p k n -> (a p) k n")).then_inc(w_full[s], 16)
            with sp.Fori(Q_SPLIT + 1, Q_END) as quad:
                for s in range(4):
                    src = sp.snap(quad * 4 + s)
                    need = sp.snap(quad - Q_SPLIT)
                    sp.wait_ge(w_lo[s], need)
                    sp.dma_start(slot[s], weights[bass.ds(src, 1)].rearrange("a p k n -> (a p) k n")).then_inc(w_full[s], 16)
            sp.wait_ge(bc_used, 10)
            sp.dma_start(out, H).then_inc(out_stored, 16)
            sp.wait_ge(out_stored, 16)

        @block.tensor
        def _(pe):
            pe.wait_ge(const_ready, 1)
            norm_sums(pe, 0)
            pe.wait_ge(lam_prod, 1)
            for c in range(2):
                mm = pe.matmul(bank[5][:, c:c + 1], LAMP[:, c:c + 1].to_broadcast([P, P]), ones, start=True, stop=True)
            mm.then_inc(lam_sum, 1)
            norm_spread(pe, 0)
            pe.wait_ge(bc_used, 1)
            for quad in range(Q_U, Q_HEAD + 1):
                for s in range(4):
                    if quad == Q_HEAD and s == 3:
                        gemm_tokens(pe, quad, s, H)
                    else:
                        gemm(pe, quad, s, H)
            for s in range(4):
                pe.wait_ge(evac_done[s], 2)
            pe.wait_ge(prep_done, 1)

            def da_score(b, j, c):
                m = 8 * b + 2 * j + c
                if j == 0 and c == 0:
                    pe.wait_ge(rope_done, b + 1)
                pe.wait_ge(da_exp, m + 1)
                rows = slice(DH * c, DH * c + DH)
                pe.matmul(bank[5][:, 0:(j + 1) * P], QH[rows, j * P:(j + 1) * P], KH[rows, 0:(j + 1) * P],
                          start=True, stop=False)
                pe.matmul(bank[5][:, j * P:(j + 1) * P], ident, CON[:, C_CHUNK:C_CHUNK + P],
                          start=False, stop=True).then_inc(da_scores, 1)

            def da_turn(b, j):
                pe.wait_ge(da_probs, 4 * b + j + 1)
                pe.wait_ge(da_copied, 4 * b + j + 1)
                for t in range(j + 1):
                    mm = pe.transpose(bank[6][:, t * P:(t + 1) * P], PC[:, t * P:(t + 1) * P], ident)
                mm.then_inc(da_turned, 1)

            def da_values(b, j):
                if j == 0:
                    pe.wait_ge(da_out, b + 1)
                    pe.wait_ge(evac_done[3], b + (Q_HEAD + 1))
                pe.wait_ge(da_copied, 4 * b + j + 2)
                for t in range(j + 1):
                    mm = pe.matmul(bank[7][:, j * P:(j + 1) * P], VH[:, t * P:(t + 1) * P],
                                   PTB[j % 2][:, t * P:(t + 1) * P], start=(t == 0), stop=(t == j))
                mm.then_inc(da_pv, 1)

            def s5_in(b, q):
                pe.wait_ge(bl_full[q], 16 * b + 16)
                pe.wait_ge(bu_used, 4 * b + q + 1)
                for c in range(2):
                    mm = pe.matmul(bank[2 + c][:, :], BL[q][:, c, :], one(U, b), start=True, stop=True)
                mm.then_inc(bu_ready, 1)

            def s5_out(b, q):
                pe.wait_ge(ss_ready, 4 * b + q + 3)
                pe.wait_ge(cl_ready, 4 * b + q + 1)
                if q == 0:
                    pe.wait_ge(y_used, b + 1)
                for c in range(2):
                    mm = pe.matmul(bank[4][:, :], CL[q][:, c, :], SS[q % 2][c], start=(q == 0 and c == 0),
                                   stop=(q == PPB - 1 and c == 1))
                mm.then_inc(y_done, 1)

            def head_body(b, last):
                for q in range(PPB):
                    s5_in(b, q)
                    da_score(b, q, 0)
                    if not last:
                        if q == 3:
                            gemm_tokens(pe, b + (Q_HEAD + 1), q, H)
                        else:
                            gemm(pe, b + (Q_HEAD + 1), q, H)
                    da_score(b, q, 1)
                    if q:
                        da_turn(b, q - 1)
                        s5_out(b, q - 1)
                        da_values(b, q - 1)
                da_turn(b, 3)
                s5_out(b, 3)
                da_values(b, 3)

            heads(pe, head_body)

            gemm_split(pe, Q_GLU, 0, YSG_HI, YSG_LO, T, S_YSG)
            pe.wait_ge(hsq_ready, 1)
            for h in range(HEADS):
                for t in range(TT):
                    mm = pe.matmul(bank[6][:, TT * h + t:TT * h + t + 1], SQ[:, h, t * P:(t + 1) * P], ones,
                                   start=True, stop=True)
            mm.then_inc(hms_ready, 1)
            gemm_split(pe, Q_GLU, 1, YSG_HI, YSG_LO)
            pe.wait_ge(hvar_ready, 1)
            norm_sums(pe, 1, 2, MSQ)
            for s in (2, 3):
                gemm_split(pe, Q_GLU, s, YSG_HI, YSG_LO)
            norm_spread(pe, 1, 2)
            pe.wait_ge(hrs_ready, 1)
            for s in range(4):
                for h in (2 * s, 2 * s + 1):
                    if h >= 2:
                        pe.wait_ge(t_ready, S_YA + (h - 1))
                    for t in range(TT):
                        mm = pe.matmul(bank[2 + h % 2][:, t * P:(t + 1) * P],
                                       HRS[:, TT * h + t:TT * h + t + 1].to_broadcast([P, P]), ident,
                                       start=True, stop=True)
                    mm.then_inc(hbc_ready, 1)
                gemm_split(pe, Q_GLU + 1, s, YSG_HI, YSG_LO)
            both(pe, Q_DA, YA_HI, YA_LO, S_YA)
            both(pe, Q_SSM, YS2_HI, YS2_LO, S_YS2)
            both(pe, Q_MIX, MG_HI, MG_LO, S_MG)
            norm_sums(pe, 2)
            for s in range(4):
                gemm_split(pe, Q_KX, s, MEMN_HI, MEMN_LO, MEM)
            norm_spread(pe, 2)
            for s in range(4):
                gemm_split(pe, Q_KX + 1, s, MEMN_HI, MEMN_LO, MEM)
            for s in range(4):
                gemm_tokens_split(pe, Q_VX, s, MEMN_HI, MEMN_LO, 2)
            norm_sums(pe, 3)
            for s in range(4):
                gemm_tokens_split(pe, Q_VX + 1, s, MEMN_HI, MEMN_LO, 2)
            norm_spread(pe, 3)
            both(pe, Q_XQ, HX_HI, HX_LO, S_HX)
            for s in range(4):
                pe.wait_ge(evac_done[s], Q_XQ + 2)

            def xa_score(i):
                h, j = divmod(i, TT)
                if i >= 2:
                    pe.wait_ge(xa_exp, i - 1)
                for k in range(2):
                    mm = pe.matmul(bank[2 + i % 2][:, 0:MEM], QX[:, 2 * h + k, j * P:(j + 1) * P],
                                   KX[:, 2 * h + k, :], start=(k == 0), stop=(k == 1))
                mm.then_inc(xa_scores, 1)

            def xa_turn(i):
                pe.wait_ge(xa_probs, i + 1)
                if i >= 2:
                    pe.wait_ge(xa_copied, i - 1)
                for k in range(2):
                    mm = pe.transpose(bank[4 + i % 2][:, k * P:(k + 1) * P], APR[i % 2][:, k * P:(k + 1) * P], ident)
                mm.then_inc(xa_turned, 1)

            def xa_values(i):
                h, j = divmod(i, TT)
                if j == 0 and h >= 1:
                    pe.wait_ge(lo_ready, S_OX + 2 * h)
                pe.wait_ge(xa_copied, i + 1)
                for e in range(2):
                    for k in range(2):
                        mm = pe.matmul(bank[6 + e][:, j * P:(j + 1) * P],
                                       VX[:, k, h * XD + e * P:h * XD + (e + 1) * P],
                                       APT[i % 2][:, k * P:(k + 1) * P], start=(k == 0), stop=(k == 1))
                mm.then_inc(xa_pv, 1)

            for i in range(XH * TT + 2):
                if i < XH * TT:
                    xa_score(i)
                if 1 <= i <= XH * TT:
                    xa_turn(i - 1)
                if i >= 2:
                    xa_values(i - 2)
            both(pe, Q_XO, OX_HI, OX_LO, S_OX)
            norm_sums(pe, 4)
            norm_spread(pe, 4)
            norm_sums(pe, 5)
            norm_spread(pe, 5)
            for step, (which, c) in enumerate(FF_ORDER):
                hi, lo = (H_HI, H_LO) if which == 1 else (F_HI[c % 2], F_LO[c % 2])
                if which == 1 and c == 0:
                    pe.wait_ge(lo_ready, S_HF + KT)
                if which == 2:
                    pe.wait_ge(ff_lo, KT * (c + 1) + 2)
                with pe.Fori(0, 2) as i:
                    for s in range(4):
                        gemm_split(pe, i + (Q_FF + 2 * step), s, hi, lo)
            norm_sums(pe, 6)
            norm_spread(pe, 6)

            with pe.Fori(0, LAYERS) as L:
                q0 = pe.snap(QL * L + Q_L2)
                norm_sums(pe, L + 7)
                norm_spread(pe, L + 7)
                for s in range(4):
                    gemm_split(pe, q0, s, H_HI, H_LO, T, SL * L + (S_L2 + S_H) if s == 0 else None)
                gemm_tokens_split(pe, q0 + 1, 0, H_HI, H_LO)
                pe.wait_ge(w_lo[1], q0 + (2 - Q_SPLIT))
                bank_free(pe, q0 + 1, 1)
                terms = ((WH[1], H_HI), (WH[1], H_LO), (WL[1], H_HI))
                for k in range(KT):
                    for n, (w, h) in enumerate(terms):
                        pe.matmul(bank[1][:, :], w[:, k, :], h[:, k, :], start=(k == 0 and n == 0),
                                  stop=(k == KT - 1 and n == 2))
                for t in range(TT):
                    for k in range(KT):
                        for n, (w, h) in enumerate(terms):
                            mm = pe.matmul(bank[4][:, 16 * t:16 * t + 12], h[:, k, t * P:(t + 1) * P],
                                           w[:, k, 2:14], start=(k == 0 and n == 0),
                                           stop=(k == KT - 1 and n == 2))
                mm.then_inc(mm_done[1], 1)
                for s in (0, 1, 2):
                    pe.wait_ge(evac_done[s], q0 + 1)
                for i in range(3):
                    mm = pe.matmul(bank[(2, 3, 5)[i]][:, :], CON[:, C_SWAP:C_SWAP + P], RAW[:, i, :],
                                   start=True, stop=True)
                mm.then_inc(sw_ready, 1)
                for s in (2, 3):
                    gemm_split(pe, q0 + 1, s, H_HI, H_LO)
                for s in (0, 1):
                    gemm_split(pe, q0 + 2, s, H_HI, H_LO)
                for s in (2, 3):
                    gemm_tokens_split(pe, q0 + 2, s, H_HI, H_LO)
                for s in range(4):
                    gemm_split(pe, q0 + 3, s, H_HI, H_LO)
                pe.wait_ge(flat_ready, L + 1)
                pe.wait_ge(w1_in, 16 * L + 16)
                for c in range(2):
                    rows = slice(64 * c, 64 * c + 64)
                    for l in range(CMP_LEN):
                        mm = pe.matmul(bank[6 + c][:, 32 * c:32 * c + NC], W1[rows, l, :], FLAT[rows, l, :],
                                       start=(l == 0), stop=(l == CMP_LEN - 1))
                mm.then_inc(hid_mm, 1)
                for s in range(4):
                    gemm_split(pe, q0 + 4, s, H_HI, H_LO)
                pe.wait_ge(hid_ready, L + 1)
                pe.matmul(bank[6][:, 64:64 + NC], W2K, HID[:, 0:NC], start=True, stop=True)
                pe.matmul(bank[6][0:NC, 128:192], HID[:, 32:32 + NC], W2V, start=True, stop=False)
                pe.matmul(bank[6][0:NC, 128:192], ONE_ROW[:, 0:NC], B2V, start=False, stop=True).then_inc(kv2_mm, 1)
                for s in range(4):
                    gemm_split(pe, q0 + 5, s, H_HI, H_LO)
                pe.wait_ge(kcr_ready, L + 1)
                pe.matmul(bank[6][:, 96:96 + NC], CON[:, C_SWAP:C_SWAP + P], KCR, start=True, stop=True).then_inc(kcs_mm, 1)
                pe.wait_ge(pooled_ready, L + 1)
                pe.wait_ge(sw_used, L + 1)
                for i in range(2):
                    mm = pe.matmul(bank[2 + i][:, :], PW[:, i, :], RB[:, 16 + i, :], start=True, stop=True)
                mm.then_inc(pool_mm, 1)
                pe.wait_ge(nq_ready, L + 1)
                pe.wait_ge(f_ready, L + 1)
                pe.wait_ge(kc_ready, L + 1)
                pe.wait_ge(pool_out, L + 1)

                def score(i):
                    h, j, kind = STEPS[i]
                    rows = slice(64 * (h % 2), 64 * (h % 2) + 64)
                    to = bank[2 + i % 2]
                    pe.wait_ge(at_exp, L * NS + (i + 1))
                    if kind == "cmp":
                        pe.matmul(to[:, 0:NC], NQ[rows, h // 2, j * P:(j + 1) * P], KC[rows, :], start=True, stop=False)
                        mm = pe.matmul(to[:, 0:NC], ident, CON[:, C_CMP + 32 * j:C_CMP + 32 * j + NC],
                                       start=False, stop=True)
                    else:
                        keys = {"slc": KS, "win": KW, "fox": FK[:, h // 2, :]}[kind]
                        q = FQ if kind == "fox" else NQ
                        width = (j + 1) * P
                        pe.matmul(to[:, 0:width], q[rows, h // 2, j * P:(j + 1) * P], keys[rows, 0:width],
                                  start=True, stop=False)
                        if kind == "fox":
                            pair = slice(32 * h, 32 * h + 2)
                            pe.matmul(to[:, 0:width], FCQ[pair, j * P:(j + 1) * P], FCK[pair, 0:width],
                                      start=False, stop=False)
                        mm = pe.matmul(to[:, j * P:width], ident, CON[:, C_CAUSAL:C_CAUSAL + P],
                                       start=False, stop=True)
                    mm.then_inc(at_scores, 1)

                def turn(i):
                    h, j, kind = STEPS[i]
                    pe.wait_ge(at_probs, L * NS + (i + 1))
                    pe.wait_ge(at_copied, L * NS + (i + 1))
                    to = bank[4 + i % 2]
                    if kind == "cmp":
                        mm = pe.transpose(to[0:NC, 0:P], APR[i % 2][:, 0:NC], ident)
                    else:
                        for t in range(j + 1):
                            mm = pe.transpose(to[:, t * P:(t + 1) * P], APR[i % 2][:, t * P:(t + 1) * P], ident)
                    mm.then_inc(at_turned, 1)

                def values(i):
                    h, j, kind = STEPS[i]
                    rows = slice(64 * (h % 2), 64 * (h % 2) + 64)
                    if j == 0 and kind in ("cmp", "fox"):
                        pe.wait_ge(at_out, L * 8 + (2 * h + (kind == "fox") + 1))
                    pe.wait_ge(at_copied, L * NS + (i + 3))
                    pt = APT[i % 2]
                    to = bank[7 if kind == "fox" else 6][rows, j * P:(j + 1) * P]
                    if kind == "cmp":
                        mm = pe.matmul(to, VC[0:NC, :], pt[0:NC, 0:P], start=True, stop=False)
                    else:
                        for t in range(j + 1):
                            if kind == "fox":
                                v = FV[:, h // 2, t * P + 64 * (h % 2):t * P + 64 * (h % 2) + 64]
                            else:
                                o = t * P + (64 if kind == "win" else 0)
                                v = VSW[:, o:o + 64]
                            mm = pe.matmul(to, v, pt[:, t * P:(t + 1) * P], start=(kind == "fox" and t == 0),
                                           stop=(kind != "slc" and t == j))
                    mm.then_inc(at_pv, 1)

                for i in range(NS + 2):
                    if i < NS:
                        score(i)
                    if filler(i) is not None:
                        gemm_split(pe, q0 + (6 + filler(i) // 4), filler(i) % 4, H_HI, H_LO)
                    if 1 <= i <= NS:
                        turn(i - 1)
                    if i >= 2:
                        values(i - 2)

                for n in range(16):
                    gemm_split(pe, q0 + (11 + n // 4), n % 4, H_HI, H_LO)
                pe.wait_ge(evac_done[3], q0 + 15)
                pe.wait_ge(lo_ready, SL * L + (S_L2 + S_OBR + KT))
                for ob in range(KT):
                    s, quad = ob % 4, q0 + (15 + ob // 4)
                    pe.wait_ge(w_lo[s], quad + (1 - Q_SPLIT))
                    bank_free(pe, quad, s)
                    for i in range(NBR):
                        for k in (2 * i, 2 * i + 1):
                            to = bank[4 * (ob % 2) + i][:, :]
                            pe.matmul(to, WH[s % 2][:, k, :], OBR_HI[:, k, :], start=(k == 2 * i), stop=False)
                            pe.matmul(to, WH[s % 2][:, k, :], OBR_LO[:, k, :], start=False, stop=False)
                            mm = pe.matmul(to, WL[s % 2][:, k, :], OBR_HI[:, k, :], start=False,
                                           stop=(k == 2 * i + 1))
                    mm.then_inc(mm_done[s], 1)
                both(pe, q0 + 17, ACC_HI, ACC_LO, SL * L + (S_L2 + S_ACC))
            norm_sums(pe, 9)
            norm_spread(pe, 9)

        @block.scalar
        def _(act):
            act.dma_start(X, x_in).then_inc(x_loaded, 16)
            act.dma_start(VEC[:, :], vecs).then_inc(consts_in, 16)
            act.dma_start(CON[:, :], consts).then_inc(consts_in, 16)
            act.dma_start(TAB[:, :], rope1).then_inc(consts_in, 16)
            act.sem_inc(da_exp, 1)
            act.sem_inc(da_copied, 1)
            act.sem_inc(da_out, 1)
            act.sem_inc(at_exp, 2)
            act.sem_inc(at_copied, 2)
            act.sem_inc(at_out, 2)
            act.wait_ge(x_loaded, 16)
            squares(act, X)
            act.wait_ge(consts_in, 48)
            act.activation(PREP[:, 1, :], vec(V_LDT, PAIRS), ACT.Exp).then_inc(prep_dt, 1)
            act.wait_ge(lam_sum, 1)
            act.activation(LAME, bank[5][:, 0:2], ACT.Exp).then_inc(lam_exp, 1)
            act.wait_ge(prep_arg, 1)
            act.activation(RADIUS, PREP[:, 2, :], ACT.Exp).then_inc(prep_exp, 1)
            act.wait_ge(prep_arg, 2)
            act.activation(PREP[:, 5, :], PREP[:, 3, :], ACT.Sin)
            act.activation(PREP[:, 6, :], PREP[:, 4, :], ACT.Sin).then_inc(prep_sin, 1)
            for blk in range(KT):
                copy_out(act, Q_U + blk // 4, blk % 4, U[:, blk, :])
            for blk in range(KT):
                s = blk % 4
                act.wait_ge(mm_done[s], Q_GB + blk // 4 + 1)
                act.activation(RB[:, 8 + blk, :], bank[s % 2][:, :], ACT.Identity,
                               bias=column(V_BGATE + 8 + blk)).then_inc(evac_done[s], 1)

            def head_evac(hd, s):
                act.wait_ge(mm_done[s], hd + (Q_HEAD + 1))
                if s < 2:
                    raw, swapped = ((QRAW, QSW), (KRAW, KSW))[s]
                    scale = DH ** -0.5 if s == 0 else 1.0
                    if not isinstance(hd, int):
                        act.wait_ge(rope_done, hd)
                    for quarter in range(4):
                        other = quarter ^ 1
                        act.activation(swapped[32 * quarter:32 * quarter + 32, :],
                                       bank[s][32 * other:32 * other + 32, :], ACT.Copy, scale=scale)
                    act.activation(raw, bank[s][:, :], ACT.Copy, scale=scale).then_inc(evac_done[s], 1)
                elif s == 2:
                    act.activation(one(RB, hd), bank[0][:, :], ACT.Identity,
                                   bias=column(hd + V_BGATE)).then_inc(evac_done[s], 1)
                else:
                    act.activation(VH, bank[1][:, :], ACT.Copy).then_inc(evac_done[s], 1)

            for s in range(4):
                head_evac(0, s)
            act.wait_ge(prep_done, 1)
            act.wait_ge(cl_zero, 1)

            def da_exponent(b, j, c):
                act.wait_ge(da_max, 8 * b + 2 * j + c + 1)
                at = 2 * (j % 2) + c
                act.activation(PR[c][:, 0:(j + 1) * P], bank[5][:, 0:(j + 1) * P], ACT.Exp,
                               bias=NMAX[:, at:at + 1], accum_out=RSUM[:, at:at + 1]).then_inc(da_exp, 1)

            def da_copy(b, j):
                act.wait_ge(da_turned, 4 * b + j + 2)
                act.wait_ge(da_pv, 4 * b + j + 1)
                act.activation(PTB[j % 2][:, 0:(j + 1) * P], bank[6][:, 0:(j + 1) * P], ACT.Copy).then_inc(da_copied, 1)

            def head_body(b, last):
                for q in range(PPB):
                    act.wait_ge(y_done, 4 * b + q + 1)
                    act.activation(CL[q][:, :, 32 * q:32 * q + 32],
                                   CT[:, 4 * b + q, :, :] if isinstance(b, int) else
                                   CT[:, bass.ds(4 * b + q, 1), :, :].rearrange("p a c m -> p (a c) m"),
                                   ACT.Copy).then_inc(cl_ready, 1)
                    da_exponent(b, q, 0)
                    if not last and q < 3:
                        head_evac(b + 1, q)
                    da_exponent(b, q, 1)
                    if q:
                        da_copy(b, q - 1)
                da_copy(b, 3)
                act.wait_ge(da_pv, 4 * b + 6)
                act.activation(one(YA, b), bank[7][:, :], ACT.Copy).then_inc(da_out, 1)
                if not last:
                    head_evac(b + 1, 3)

            act.sem_inc(da_turned, 1)
            heads(act, head_body)

            act.wait_ge(rope_done, HEADS)
            act.wait_ge(da_scores, 8 * HEADS)
            weight_hi(act, Q_GLU, 0)
            weight_hi(act, Q_GLU, 1)
            act.wait_ge(y_used, KT + 1)
            for k in range(KT):
                act.activation(YSG_HI[:, k, :], U[:, k, :], ACT.Gelu_apprx_tanh).then_inc(hi_ready, 1)
                act.activation(U[:, k, :], U[:, k, :], ACT.Gelu_apprx_tanh).then_inc(t_ready, 1)
            act.drain()
            for h in range(HEADS):
                op = act.activation(SQ[:, h, :], YA[:, h, :], ACT.Square)
            op.then_inc(hsq_ready, 1)
            act.wait_ge(mem_loaded, 16)
            squares(act, MEMRAW, MEM, MSQ)
            for blk in range(KT):
                s = blk % 4
                if blk >= 4:
                    for h in (2 * s, 2 * s + 1):
                        round_hi(act, S_YA, h, YA_HI[:, h, :], YA[:, h, :])
                ahead(act, Q_GLU + blk // 4, s)
                act.wait_ge(mm_done[s], Q_GLU + blk // 4 + 1)
                if blk >= 2:
                    act.wait_ge(ys_ready, blk - 1)
                act.activation(PAIR[blk % 2], bank[s % 2][:, :], ACT.Sigmoid,
                               bias=column(V_BGLU + blk)).then_inc(evac_done[s], 1)
                if blk < 4:
                    act.activation(R[:, 4 * blk * T:4 * (blk + 1) * T], R[:, 4 * blk * T:4 * (blk + 1) * T],
                                   ACT.Sigmoid).then_inc(gates_done, 1)
            for k in range(KT):
                round_hi(act, S_MEMN, k, MEMN_HI[:, k, :], MEMN[:, k, :])
            for k in range(KT):
                round_hi(act, S_YS2, k, YS2_HI[:, k, :], YS2[:, k, :])
            for blk in range(KT):
                ahead(act, Q_DA + blk // 4, blk % 4)
            for blk in range(KT + 1):
                if blk < KT:
                    ahead(act, Q_SSM + blk // 4, blk % 4)
                if blk:
                    round_hi(act, S_MG, blk - 1, MG_HI[:, blk - 1, :], MG[:, blk - 1, :])

            def store_and_square(quad, s, blk):
                ahead(act, quad, s)
                act.wait_ge(mm_done[s], quad + 1)
                act.activation(YB[:, blk, :], bank[s % 2][:, :], ACT.Copy)
                act.activation(SQ[:, blk, :], bank[s % 2][:, :], ACT.Square).then_inc(evac_done[s], 1)

            for blk in range(KT):
                store_and_square(Q_MIX + blk // 4, blk % 4, blk)
            act.drain()
            act.sem_inc(sq_ready, 1)
            for blk in range(KT):
                ahead(act, Q_KX + blk // 4, blk % 4)
                copy_out(act, Q_KX + blk // 4, blk % 4, KX[:, blk, :])
            for blk in range(KT):
                if blk == 4:
                    act.wait_ge(x_ready, 1)
                    squares(act, X)
                s = blk % 4
                ahead(act, Q_VX + blk // 4, s)
                act.wait_ge(mm_done[s], Q_VX + blk // 4 + 1)
                act.activation(VX[:, :, blk * P:(blk + 1) * P],
                               bank[s % 2][:, 0:2 * P].rearrange("p (t n) -> p t n", t=2), ACT.Copy).then_inc(evac_done[s], 1)
            for k in range(KT):
                round_hi(act, S_HX, k, HX_HI[:, k, :], HX[:, k, :])
            for blk in range(KT):
                ahead(act, Q_XQ + blk // 4, blk % 4)
                copy_out(act, Q_XQ + blk // 4, blk % 4, QX[:, blk, :], XD ** -0.5)

            def xa_exponent(i):
                act.wait_ge(xa_max, i + 1)
                if i >= 2:
                    act.wait_ge(xa_turned, i - 1)
                at = i % 2
                act.activation(APR[at][:, 0:MEM], bank[2 + at][:, 0:MEM], ACT.Exp, bias=NMAX[:, at:at + 1],
                               accum_out=RSUM[:, at:at + 1]).then_inc(xa_exp, 1)

            def xa_copy(i):
                act.wait_ge(xa_turned, i + 1)
                if i >= 2:
                    act.wait_ge(xa_pv, i - 1)
                act.activation(APT[i % 2][:, 0:MEM], bank[4 + i % 2][:, 0:MEM], ACT.Copy).then_inc(xa_copied, 1)

            def xa_round(h):
                act.wait_ge(xa_pv, TT * (h + 1))
                for e in range(2):
                    act.activation(OX_HI[:, 2 * h + e, :], bank[6 + e][:, :], ACT.Copy).then_inc(hi_ready, 1)

            act.sem_inc(t_ready, KT)
            for i in range(XH * TT + 3):
                if i < XH * TT:
                    xa_exponent(i)
                if 1 <= i <= XH * TT:
                    xa_copy(i - 1)
                if i >= 3 and (i - 3) % TT == TT - 1:
                    xa_round((i - 3) // TT)
            for blk in range(KT):
                store_and_square(Q_XO + blk // 4, blk % 4, blk)
            act.drain()
            act.sem_inc(sq_ready, 1)
            act.wait_ge(x_ready, 2)
            act.wait_ge(ms_ready, 5)
            squares(act, X)
            for k in range(KT):
                round_hi(act, S_HF, k, H_HI[:, k, :], H[:, k, :])

            def ff_block(c, quad, i, s):
                ahead(act, quad, s)
                act.wait_ge(ff_lo, 4 * i + (KT * c + s + 1))
                act.wait_ge(mm_done[s], quad + 1)
                act.activation(RELU[s % 2], bank[s % 2][:, :], ACT.Relu).then_inc(evac_done[s], 1)
                act.drain()
                act.activation(one(F_HI[c % 2], 4 * i + s), RELU[s % 2], ACT.Square).then_inc(ff_hi, 1)

            for step, (which, c) in enumerate(FF_ORDER[:-1]):
                with act.Fori(0, 2) as i:
                    for s in range(4):
                        if which == 1:
                            ff_block(c, i + (Q_FF + 2 * step), i, s)
                        else:
                            ahead(act, i + (Q_FF + 2 * step), s)
            act.wait_ge(ms_ready, 6)
            for blk in range(KT):
                s, quad = blk % 4, Q_L2 - 2 + blk // 4
                if blk < KT - 2:
                    ahead(act, quad, s)
                act.wait_ge(evac_done[s], quad + 1)
                op = act.activation(SQ[:, blk, :], YF[:, blk, :], ACT.Square)
            op.then_inc(sq_ready, 1)

            with act.Fori(0, LAYERS) as L:
                q0 = act.snap(QL * L + Q_L2)
                stages = act.snap(SL * L + S_L2)
                weight_hi(act, q0, 0)
                weight_hi(act, q0, 1)
                act.wait_ge(x_ready, L + 3)
                act.wait_ge(ms_ready, L + 7)
                squares(act, X)
                act.wait_ge(lvec_in, 16 * L + 16)
                for k in range(KT):
                    round_hi(act, stages + S_H, k, H_HI[:, k, :], H[:, k, :])

                def store(quad, s, dst, scale=1.0):
                    ahead(act, quad, s)
                    copy_out(act, quad, s, dst, scale)

                store(q0, 0, RAW[:, 0, :], 64 ** -0.5)
                store(q0, 1, RAW[:, 1, :], 64 ** -0.5)
                store(q0, 2, RAW[:, 2, :])
                store(q0, 3, KCVC)
                store(q0 + 1, 0, VSW)
                ahead(act, q0 + 1, 1)
                act.wait_ge(mm_done[1], q0 + 2)
                act.activation(FZ, bank[1][:, :], ACT.Identity, bias=LVEC[:, L_FBIAS:L_FBIAS + 1])
                act.activation(G12[:, :, 0:12], bank[4][:, 0:64].rearrange("p (t g) -> p t g", t=TT)[:, :, 0:12],
                               ACT.Sigmoid).then_inc(evac_done[1], 1)
                act.drain()
                act.activation(FL, FZ, ACT.Abs)
                act.drain()
                act.activation(FL, FL, ACT.Exp, scale=-1.0)
                act.drain()
                act.activation(FL, FL, ACT.Ln, bias=1.0).then_inc(f_log, 1)
                store(q0 + 1, 2, FQ[:, 0, :], 64 ** -0.5)
                store(q0 + 1, 3, FQ[:, 1, :], 64 ** -0.5)
                store(q0 + 2, 0, FK[:, 0, :])
                store(q0 + 2, 1, FK[:, 1, :])
                store(q0 + 2, 2, FV[:, 0, :])
                store(q0 + 2, 3, FV[:, 1, :])
                for i in range(2):
                    for s in range(4):
                        store(q0 + (3 + i), s, RB[:, 4 * i + s, :])
                    if i == 0:
                        act.wait_ge(hid_mm, L + 1)
                        for c in range(2):
                            op = act.activation(HID[:, 32 * c:32 * c + NC], bank[6 + c][:, 32 * c:32 * c + NC], ACT.Silu,
                                                bias=LVEC[:, L_B1 + c:L_B1 + c + 1])
                        op.then_inc(hid_ready, 1)
                act.wait_ge(kv2_mm, L + 1)
                act.activation(VC[0:NC, :], bank[6][0:NC, 128:192], ACT.Copy)
                act.activation(KCR, bank[6][:, 64:64 + NC], ACT.Identity,
                               bias=LVEC[:, L_B2K:L_B2K + 1]).then_inc(kcr_ready, 1)
                for s in range(4):
                    store(q0 + 5, s, U[:, s, :])
                act.wait_ge(pool_mm, L + 1)
                for c in range(2):
                    op = act.activation(OBR[:, 2 + c, :], bank[2 + c][:, :], ACT.Copy,
                                        scale=LVEC[:, L_POOL + c:L_POOL + c + 1])
                op.then_inc(pool_out, 1)

                def exponent(i):
                    h, j, kind = STEPS[i]
                    width = NC if kind == "cmp" else (j + 1) * P
                    act.wait_ge(at_max, L * NS + (i + 1))
                    act.wait_ge(at_turned, L * NS + (i + 1))
                    at = i % 2
                    act.activation(APR[at][:, 0:width], bank[2 + at][:, 0:width], ACT.Exp, bias=NMAX[:, at:at + 1],
                                   accum_out=RSUM[:, at:at + 1]).then_inc(at_exp, 1)

                def turned_copy(i):
                    h, j, kind = STEPS[i]
                    act.wait_ge(at_turned, L * NS + (i + 3))
                    act.wait_ge(at_pv, L * NS + (i + 1))
                    if kind == "cmp":
                        act.activation(APT[i % 2][0:NC, 0:P], bank[4 + i % 2][0:NC, 0:P], ACT.Copy).then_inc(at_copied, 1)
                    else:
                        width = (j + 1) * P
                        act.activation(APT[i % 2][:, 0:width], bank[4 + i % 2][:, 0:width], ACT.Copy).then_inc(at_copied, 1)

                def head_out(h):
                    rows = slice(64 * (h % 2), 64 * (h % 2) + 64)
                    act.wait_ge(at_pv, L * NS + (16 * (h + 1) + 2))
                    act.activation(OBR[rows, h // 2, :], bank[6][rows, :], ACT.Copy).then_inc(at_out, 1)
                    act.activation(OBR[rows, 6 + h // 2, :], bank[7][rows, :], ACT.Copy).then_inc(at_out, 1)

                act.wait_ge(conv_out, L + 1)
                for i in range(NS + 3):
                    if i < NS:
                        exponent(i)
                    n = filler(i)
                    if n is not None:
                        store(q0 + (6 + n // 4), n % 4, U[:, 4 + n, :] if n < 4 else ML[n - 4])
                    if 1 <= i <= NS:
                        turned_copy(i - 1)
                    if i >= 3 and (i - 3) % 16 == 15:
                        head_out((i - 3) // 16)
                act.drain()
                for i in range(2):
                    act.activation(U_[:, 4 * i * T:4 * (i + 1) * T], U_[:, 4 * i * T:4 * (i + 1) * T],
                                   ACT.Silu).then_inc(silu_done, 1)
                for n in range(16):
                    s, quad = n % 4, q0 + (11 + n // 4)
                    ahead(act, quad, s)
                    act.wait_ge(mm_done[s], quad + 1)
                    act.activation(ML[16 + n], bank[s % 2][:, :], ACT.Sigmoid).then_inc(evac_done[s], 1)
                    if n < KT:
                        round_hi(act, stages + S_OBR, n, OBR_HI[:, n, :], OBR[:, n, :])
                    if n >= 12:
                        ob = n - 12
                        act.activation(R[:, 4 * ob * T:4 * (ob + 1) * T], R[:, 4 * ob * T:4 * (ob + 1) * T],
                                       ACT.Sigmoid).then_inc(sig_ready, 1)
                for ob in range(KT + 1):
                    if ob < KT:
                        ahead(act, q0 + (15 + ob // 4), ob % 4)
                    if ob:
                        round_hi(act, stages + S_ACC, ob - 1, ACC_HI[:, ob - 1, :], ACC[:, ob - 1, :])
                for blk in range(KT - 2):
                    ahead(act, q0 + (17 + blk // 4), blk % 4)
            act.wait_ge(x_ready, 3 + LAYERS)
            squares(act, X)

        @block.vector
        def _(dve):
            dve.memset(SMALL[:, 0:4], 1.0)
            dve.memset(HALF, -0.5)
            dve.memset(ONE_ROW, 1.0)
            dve.drain()
            dve.sem_inc(bu_used, 1)
            dve.sem_inc(ss_ready, 2)
            dve.sem_inc(y_used, 1)
            dve.sem_inc(ff_lo, 2)
            dve.wait_ge(consts_in, 48)
            dve.sem_inc(const_ready, 1)
            norm_mean(dve, 0)

            dve.tensor_tensor(LAMP[:, 0:1], vec(V_LQ1, 1), vec(V_LK1, 1), ALU.mult)
            dve.tensor_tensor(LAMP[:, 1:2], vec(V_LQ2, 1), vec(V_LK2, 1), ALU.mult).then_inc(lam_prod, 1)
            dve.tensor_scalar(HN08, vec(V_HEADNORM, 1), 1.0 - LAM_INIT, None, ALU.mult)
            norm_apply(dve, 0, H, X, vec(V_MIX_PRE))
            dve.wait_ge(lam_exp, 1)
            dve.tensor_tensor(NLAM, LAME[:, 1:2], LAME[:, 0:1], ALU.subtract)
            dve.drain()
            dve.tensor_scalar(NLAM, NLAM, LAM_INIT, None, ALU.subtract)

            DT, RE, ARG, ARGC, SN, CS = (PREP[:, i, :] for i in range(1, 7))
            A, B, C, E, F, G, I, J = (PREP[:, i, :] for i in range(8, 16))
            lre, lim = vec(V_LRE, PAIRS), vec(V_LIM, PAIRS)

            def seq(*ops):
                for op in ops:
                    op()
                dve.drain()

            def tt(o, a, b, op):
                return lambda: dve.tensor_tensor(o, a, b, op)

            def ts(o, a, x, y, op0, op1=None):
                if op1 is None:
                    return lambda: dve.tensor_scalar(o, a, x, None, op0)
                return lambda: dve.tensor_scalar(o, a, x, y, op0, op1)

            def stt(o, a, x, b, op0, op1):
                return lambda: dve.scalar_tensor_tensor(o, a, x, b, op0, op1)

            dve.wait_ge(prep_dt, 1)
            dve.tensor_tensor(RE, lre, DT, ALU.mult).then_inc(prep_arg, 1)
            seq(tt(A, lim, DT, ALU.mult))
            turns = 1.5 * 2.0 ** 23
            two_pi = 2 * np.pi
            c1 = 6.28125
            c2 = float(np.float32(np.round((two_pi - c1) * 2.0 ** 22) / 2.0 ** 22))
            c3 = two_pi - c1 - c2
            pi32 = 3.1415925
            seq(ts(B, A, 1 / two_pi, turns, ALU.mult, ALU.add))
            seq(ts(B, B, turns, None, ALU.subtract))
            seq(stt(A, B, -c1, A, ALU.mult, ALU.add))
            seq(stt(A, B, -c2, A, ALU.mult, ALU.add))
            seq(stt(A, B, -c3, A, ALU.mult, ALU.add))
            seq(ts(ARG, A, pi32, -pi32, ALU.min, ALU.max), ts(C, A, np.pi / 2, None, ALU.add))
            seq(ts(E, C, pi32, -two_pi, ALU.is_gt, ALU.mult))
            seq(tt(C, C, E, ALU.add))
            dve.tensor_scalar(ARGC, C, pi32, -pi32, ALU.min, ALU.max).then_inc(prep_arg, 1)
            dve.wait_ge(prep_sin, 1)
            dve.wait_ge(prep_exp, 1)
            for table in (LOT, HIT):
                seq(lambda: dve.memset(table[:, :, 0, 0:1], 1.0), lambda: dve.memset(table[:, :, 1, 0:1], 0.0))
                size, n = table.shape[-1], 1
                while n < size:
                    w = [x.rearrange("p (n a) -> p n a", a=1).to_broadcast([P, PAIRS, n]) for x in (CS, SN)]
                    t = [W.rearrange("p (n a) -> p n a", n=PAIRS)[:, :, 0:n] for W in TMP[0:4]]
                    re, im = table[:, :, 0, 0:n], table[:, :, 1, 0:n]
                    seq(tt(t[0], re, w[0], ALU.mult), tt(t[1], im, w[1], ALU.mult),
                        tt(t[2], im, w[0], ALU.mult), tt(t[3], re, w[1], ALU.mult),
                        tt(E, CS, CS, ALU.mult), tt(F, SN, SN, ALU.mult), tt(G, CS, SN, ALU.mult))
                    if n == 1 and table is LOT:
                        seq(tt(A, RADIUS, CS, ALU.mult), tt(B, RADIUS, SN, ALU.mult))
                    seq(tt(table[:, :, 0, n:2 * n], t[0], t[1], ALU.subtract),
                        tt(table[:, :, 1, n:2 * n], t[2], t[3], ALU.add),
                        tt(CS, E, F, ALU.subtract), ts(SN, G, 2.0, None, ALU.mult))
                    n *= 2
            seq(ts(A, A, 1.0, None, ALU.subtract), tt(C, lre, lre, ALU.mult), tt(E, lim, lim, ALU.mult))
            seq(tt(C, C, E, ALU.add), tt(G, A, lre, ALU.mult), tt(F, B, lim, ALU.mult))
            seq(lambda: dve.reciprocal(C, C), tt(E, G, F, ALU.add), tt(I, B, lre, ALU.mult), tt(J, A, lim, ALU.mult))
            seq(tt(F, I, J, ALU.subtract))
            seq(tt(E, E, C, ALU.mult), tt(F, F, C, ALU.mult))
            dve.wait_ge(ct_in, 16)
            er, ei = [x.rearrange("p (n a) -> p n a", a=1).to_broadcast([P, PAIRS, 32]) for x in (E, F)]
            t = [R3[:, 1024 * i:1024 * i + 1024].rearrange("p (n m) -> p n m", n=PAIRS) for i in range(4)]
            seq(tt(t[0], CT[:, :, 0, :], er, ALU.mult), tt(t[1], CT[:, :, 1, :], ei, ALU.mult),
                tt(t[2], CT[:, :, 0, :], ei, ALU.mult), tt(t[3], CT[:, :, 1, :], er, ALU.mult))
            seq(tt(CT[:, :, 0, :], t[0], t[1], ALU.subtract), stt(CT[:, :, 1, :], t[2], -1.0, t[3], ALU.mult, ALU.subtract))
            dve.sem_inc(prep_done, 1)

            def da_row_max(b, j, c):
                dve.wait_ge(da_scores, 8 * b + 2 * j + c + 1)
                at = 2 * (j % 2) + c
                dve.tensor_reduce(NMAX[:, at:at + 1], bank[5][:, 0:(j + 1) * P], AX.X, ALU.max,
                                  negate=True).then_inc(da_max, 1)

            def da_combine(b, j):
                dve.wait_ge(da_exp, 8 * b + 2 * j + 3)
                o, w = 2 * (j % 2), (j + 1) * P
                dve.reciprocal(RINV[:, 0:2], RSUM[:, o:o + 2])
                dve.drain()
                dve.tensor_scalar(PR[0][:, 0:w], PR[0][:, 0:w], RINV[:, 0:1], None, ALU.mult)
                dve.tensor_scalar(PR[1][:, 0:w], PR[1][:, 0:w], RINV[:, 1:2], NLAM, ALU.mult, ALU.mult)
                dve.drain()
                dve.wait_ge(da_turned, 4 * b + j + 1)
                dve.tensor_tensor(PC[:, 0:w], PR[0][:, 0:w], PR[1][:, 0:w], ALU.add).then_inc(da_probs, 1)

            def s5_scan(b, q):
                n = 4 * b + q
                cs, sn = ROT[q % 2]
                rad = PREP[:, 0, n:n + 1] if isinstance(b, int) else PREP[:, 0, bass.ds(n, 1)]
                dve.wait_ge(tab_ready, n + 1)
                dve.wait_ge(bu_ready, n + 1)
                dve.tensor_tensor(TMP[0], bank[2][:, :], cs, ALU.mult)
                dve.tensor_tensor(TMP[1], bank[3][:, :], sn, ALU.mult)
                dve.tensor_tensor(TMP[2], bank[3][:, :], cs, ALU.mult)
                dve.tensor_tensor(TMP[3], bank[2][:, :], sn, ALU.mult).then_inc(bu_used, 1)
                dve.drain()
                dve.tensor_tensor(TMP[0], TMP[0], TMP[1], ALU.add)
                dve.tensor_tensor(TMP[2], TMP[2], TMP[3], ALU.subtract)
                dve.drain()
                dve.tensor_tensor_scan(TMP[1], rad.to_broadcast([P, T]), TMP[0], 0.0, ALU.mult, ALU.add)
                dve.tensor_tensor_scan(TMP[3], rad.to_broadcast([P, T]), TMP[2], 0.0, ALU.mult, ALU.add)
                dve.drain()

            def s5_turn_back(b, q):
                n = 4 * b + q
                cs, sn = ROT[q % 2]
                re, im = SS[q % 2]
                dve.wait_ge(y_done, n + 3)
                dve.tensor_tensor(re, TMP[1], cs, ALU.mult)
                dve.tensor_tensor(TMP[0], TMP[3], sn, ALU.mult)
                dve.tensor_tensor(im, TMP[3], cs, ALU.mult)
                dve.tensor_tensor(TMP[2], TMP[1], sn, ALU.mult)
                dve.drain()
                dve.tensor_tensor(re, re, TMP[0], ALU.subtract)
                dve.tensor_tensor(im, im, TMP[2], ALU.add).then_inc(ss_ready, 1)

            def head_body(b, last):
                for q in range(PPB):
                    da_row_max(b, q, 0)
                    s5_scan(b, q)
                    da_row_max(b, q, 1)
                    s5_turn_back(b, q)
                    da_combine(b, q)
                dve.wait_ge(y_done, 4 * b + 8)
                dve.scalar_tensor_tensor(one(U, b), one(U, b), column(b + V_SSMD), bank[4][:, :],
                                         ALU.mult, ALU.add).then_inc(y_used, 1)

            heads(dve, head_body)

            dve.wait_ge(da_turned, 4 * HEADS + 1)
            dve.drain()
            for k in range(KT):
                dve.wait_ge(t_ready, S_YSG + (k + 1))
                rest_lo(dve, S_YSG, k, YSG_LO[:, k, :], U[:, k, :], YSG_HI[:, k, :])
            dve.drain()
            dve.wait_ge(hms_ready, 1)
            dve.tensor_scalar(HVAR, bank[6][:, 0:32], 1.0 / P, EPS, ALU.mult, ALU.add).then_inc(hvar_ready, 1)

            def glu(blk):
                s = blk % 4
                dve.wait_ge(evac_done[s], Q_GLU + blk // 4 + 1)
                dve.tensor_tensor(U[:, blk, :], PAIR[blk % 2], U[:, blk, :], ALU.mult).then_inc(ys_ready, 1)

            norm_mean(dve, 1, 2)
            for blk in range(4):
                glu(blk)
            for s in range(4):
                for h in (2 * s, 2 * s + 1):
                    dve.wait_ge(hbc_ready, h + 1)
                    dve.scalar_tensor_tensor(YA[:, h, :], YA[:, h, :], HN08, bank[2 + h % 2][:, :],
                                             ALU.mult, ALU.mult).then_inc(t_ready, 1)
                for h in (2 * s, 2 * s + 1):
                    rest_lo(dve, S_YA, h, YA_LO[:, h, :], YA[:, h, :], YA_HI[:, h, :])
                glu(4 + s)
            norm_split(dve, 1, S_MEMN, MEMN, MEMN_HI, MEMN_LO, MEMRAW, vec(V_MEM), MEM)
            dve.drain()
            dve.sem_inc(t_ready, KT)
            for k in range(KT):
                rest_lo(dve, S_YS2, k, YS2_LO[:, k, :], YS2[:, k, :], YS2_HI[:, k, :])
            dve.wait_ge(gates_done, 4)
            for blk in range(KT):
                s = blk % 4
                dve.wait_ge(mm_done[s], Q_DA + blk // 4 + 1)
                dve.tensor_tensor(MG[:, blk, :], RB[:, 8 + blk, :], bank[s % 2][:, :], ALU.mult).then_inc(evac_done[s], 1)
            for blk in range(KT + 1):
                if blk < KT:
                    s = blk % 4
                    dve.wait_ge(mm_done[s], Q_SSM + blk // 4 + 1)
                    dve.tensor_tensor(PAIR[blk % 2], RB[:, blk, :], bank[s % 2][:, :], ALU.mult).then_inc(evac_done[s], 1)
                    dve.drain()
                    dve.tensor_tensor(MG[:, blk, :], MG[:, blk, :], PAIR[blk % 2], ALU.add).then_inc(t_ready, 1)
                if blk:
                    rest_lo(dve, S_MG, blk - 1, MG_LO[:, blk - 1, :], MG[:, blk - 1, :], MG_HI[:, blk - 1, :])
            norm_mean(dve, 2)
            residual_add(dve, 2, YB, vec(V_MIX_POST))
            norm_mean(dve, 3)
            norm_split(dve, 3, S_HX, HX, HX_HI, HX_LO, X, vec(V_X_PRE))

            def xa_rest(h):
                for e in range(2):
                    rest_lo(dve, S_OX, 2 * h + e, OX_LO[:, 2 * h + e, :], bank[6 + e][:, :], OX_HI[:, 2 * h + e, :])

            for i in range(XH * TT + 1):
                if i >= 7 and (i - 7) % TT == 0:
                    xa_rest((i - 7) // TT)
                if i < XH * TT:
                    at = i % 2
                    dve.wait_ge(xa_scores, i + 1)
                    dve.tensor_reduce(NMAX[:, at:at + 1], bank[2 + at][:, 0:MEM], AX.X, ALU.max,
                                      negate=True).then_inc(xa_max, 1)
                if i:
                    at = (i - 1) % 2
                    dve.wait_ge(xa_exp, i)
                    dve.reciprocal(RINV[:, at:at + 1], RSUM[:, at:at + 1])
                    dve.drain()
                    dve.tensor_scalar(APR[at][:, 0:MEM], APR[at][:, 0:MEM], RINV[:, at:at + 1], None,
                                      ALU.mult).then_inc(xa_probs, 1)
            xa_rest(XH - 1)
            norm_mean(dve, 4)
            residual_add(dve, 4, YB, vec(V_X_POST))
            norm_mean(dve, 5)
            norm_split(dve, 5, S_HF, H, H_HI, H_LO, X, vec(V_FF_PRE))
            for step, (which, c) in enumerate(FF_ORDER):
                with dve.Fori(0, 2) as i:
                    for s in range(4):
                        if which == 1:
                            f_lo = one(F_LO[c % 2], 4 * i + s)
                            f = one(RB[:, 16 * (c % 2):16 * (c % 2) + 8, :], 4 * i + s)
                            dve.wait_ge(ff_hi, 4 * i + (KT * c + s + 1))
                            dve.tensor_tensor(f, RELU[s % 2], RELU[s % 2], ALU.mult)
                            dve.drain()
                            dve.tensor_tensor(f_lo, f, one(F_HI[c % 2], 4 * i + s).bitcast(F32),
                                              ALU.subtract).then_inc(ff_lo, 1)
                        else:
                            y = one(YF, 4 * i + s)
                            dve.drain()
                            dve.wait_ge(mm_done[s], i + (Q_FF + 2 * step + 1))
                            if c == 0:
                                op = dve.tensor_copy(y, bank[s % 2][:, :])
                            else:
                                op = dve.tensor_tensor(y, y, bank[s % 2][:, :], ALU.add)
                            op.then_inc(evac_done[s], 1)
            norm_mean(dve, 6)
            residual_add(dve, 6, YF, vec(V_FF_POST))

            with dve.Fori(0, LAYERS) as L:
                q0 = dve.snap(QL * L + Q_L2)
                stages = dve.snap(SL * L + S_L2)
                norm_mean(dve, L + 7)
                dve.wait_ge(lvec_in, 16 * L + 16)
                norm_split(dve, L + 7, stages + S_H, H, H_HI, H_LO, X, LVEC[:, L_NORM:L_NORM + KT])
                dve.memset(PA[:, 0:16], 0.0)
                dve.memset(PB[:, 0:16], 0.0)
                dve.memset(CP[:, 0:2], 0.0)
                dve.wait_ge(evac_done[3], q0 + 1)
                dve.wait_ge(lw_in, 16 * 5 * L + 80)
                kv = KCVC.rearrange("p (m b) -> p b m", b=16)
                for a in range(2):
                    op = dve.tensor_tensor(FLAT[:, 16 * a:16 * a + 16, :], kv[:, :, a:a + NC],
                                           POS[:, 16 * a:16 * a + 16].rearrange("p (l n) -> p l n", n=1)
                                           .to_broadcast([P, 16, NC]), ALU.add)
                op.then_inc(flat_ready, 1)
                dve.wait_ge(sw_ready, L + 1)
                dve.wait_ge(rope2_in, 16)
                for i in range(3):
                    dve.tensor_tensor(RTMP[:, i, :], RAW[:, i, :], COS, ALU.mult)
                dve.drain()
                for i in range(3):
                    op = dve.tensor_tensor(RAW[:, i, :], bank[(2, 3, 5)[i]][:, :], SIN, ALU.mult)
                op.then_inc(sw_used, 1)
                dve.drain()
                for i in range(2):
                    dve.tensor_tensor(NQ[:, i, :], RTMP[:, i, :], RAW[:, i, :], ALU.add)
                for dst, src in ((KS, 0), (KW, 64)):
                    for half in (0, 64):
                        op = dve.tensor_tensor(dst[half:half + 64, :], RTMP[src:src + 64, 2, :], RAW[src:src + 64, 2, :],
                                               ALU.add)
                op.then_inc(nq_ready, 1)
                dve.wait_ge(f_log, L + 1)
                dve.scalar_tensor_tensor(FZ, FZ, 0.0, FL, ALU.min, ALU.subtract)
                dve.drain()
                dve.tensor_tensor_scan(FL, ones.to_broadcast([P, T]), FZ, 0.0, ALU.mult, ALU.add)
                dve.drain()
                dve.tensor_scalar(FCQ, FL, CON[:, C_FQ:C_FQ + 1], CON[:, C_FK:C_FK + 1], ALU.mult, ALU.add)
                dve.tensor_scalar(FCK, FL, CON[:, C_NFK:C_NFK + 1], CON[:, C_FQ:C_FQ + 1], ALU.mult,
                                  ALU.add)
                dve.tensor_tensor(G12[:, :, 0:NH], G12[:, :, 0:NH],
                                  CON[:, C_VALID:C_VALID + TT].rearrange("p (t g) -> p t g", g=1)
                                  .to_broadcast([P, TT, NH]), ALU.mult)
                dve.drain()
                dve.sem_inc(f_ready, 1)
                for i in range(2):
                    dve.wait_ge(evac_done[i], q0 + 4)
                dve.wait_ge(hid_mm, L + 1)
                for i in range(2):
                    u = PIN[:, i, :]
                    dve.tensor_copy(PA[:, 16:528], u)
                    dve.drain()
                    dve.tensor_tensor(PB[:, 16:528], PA[:, 16:528], PA[:, 15:527], ALU.add)
                    dve.drain()
                    if i == 0:
                        dve.tensor_tensor(PA[64:128, 16:528], PB[64:128, 16:528], PB[64:128, 14:526], ALU.add)
                    else:
                        dve.tensor_tensor(PA[:, 16:528], PB[:, 16:528], PB[:, 14:526], ALU.add)
                        dve.drain()
                        dve.tensor_tensor(PB[:, 16:528], PA[:, 16:528], PA[:, 12:524], ALU.add)
                        dve.drain()
                        dve.tensor_tensor(PA[64:128, 16:528], PB[64:128, 16:528], PB[64:128, 8:520], ALU.add)
                    dve.drain()
                    for rows, s in ((slice(0, 64), PB), (slice(64, 128), PA)):
                        dve.scalar_tensor_tensor(RB[rows, 16 + i, 16:T], s[rows, 32:528], CON[rows, C_W + i:C_W + i + 1],
                                                 u[rows, 16:T], ALU.mult, ALU.subtract)
                        dve.tensor_tensor(s[rows, 16:32], s[rows, 16:32], CON[rows, C_INV + 16 * i:C_INV + 16 * i + 16],
                                          ALU.mult)
                    dve.drain()
                    for rows, s in ((slice(0, 64), PB), (slice(64, 128), PA)):
                        dve.tensor_tensor(RB[rows, 16 + i, 0:16], s[rows, 16:32], u[rows, 0:16], ALU.subtract)
                    dve.drain()
                dve.sem_inc(pooled_ready, 1)
                dve.wait_ge(kcs_mm, L + 1)
                ends = slice(CMP_LEN - 1, T, CMP_STRIDE)
                dve.tensor_tensor(KCT[:, 0:NC], KCR, COS[:, ends], ALU.mult)
                dve.tensor_tensor(KCT[:, 32:32 + NC], bank[6][:, 96:96 + NC], SIN[:, ends], ALU.mult)
                dve.drain()
                dve.tensor_tensor(KC, KCT[:, 0:NC], KCT[:, 32:32 + NC], ALU.add).then_inc(kc_ready, 1)
                for s in range(4):
                    dve.wait_ge(evac_done[s], q0 + 5)
                for i in range(2):
                    dve.tensor_tensor(CP[:, 2:514], CC[:, i, :], CX[:, i, :], ALU.mult)
                    dve.drain()
                    for tap in range(3):
                        w = LVEC[:, L_CONV + 2 * tap + i:L_CONV + 2 * tap + i + 1]
                        if tap == 0:
                            dve.tensor_scalar(OBR[:, 4 + i, :], CP[:, 0:T], w, None, ALU.mult)
                        else:
                            dve.scalar_tensor_tensor(OBR[:, 4 + i, :], CP[:, tap:tap + T], w, OBR[:, 4 + i, :],
                                                     ALU.mult, ALU.add)
                        dve.drain()
                    dve.tensor_tensor(OBR[:, 4 + i, :], OBR[:, 4 + i, :], CB[:, i, :], ALU.mult)
                    dve.drain()
                dve.wait_ge(pool_mm, L + 1)
                dve.sem_inc(conv_out, 1)

                for i in range(NS + 1):
                    if i < NS:
                        h, j, kind = STEPS[i]
                        width = NC if kind == "cmp" else (j + 1) * P
                        at = i % 2
                        dve.wait_ge(at_scores, L * NS + (i + 1))
                        dve.tensor_reduce(NMAX[:, at:at + 1], bank[2 + at][:, 0:width], AX.X, ALU.max,
                                          negate=True).then_inc(at_max, 1)
                    if i:
                        h, j, kind = STEPS[i - 1]
                        width = NC if kind == "cmp" else (j + 1) * P
                        at = (i - 1) % 2
                        dve.wait_ge(at_exp, L * NS + (i + 2))
                        dve.reciprocal(RINV[:, at:at + 1], RSUM[:, at:at + 1])
                        dve.drain()
                        pr = APR[at][:, 0:width]
                        if kind == "fox":
                            op = dve.tensor_scalar(pr, pr, RINV[:, at:at + 1], None, ALU.mult)
                        else:
                            g = NH * ("cmp", "slc", "win").index(kind) + h
                            op = dve.tensor_scalar(pr, pr, RINV[:, at:at + 1], G12[:, j, g:g + 1], ALU.mult, ALU.mult)
                        op.then_inc(at_probs, 1)
                dve.wait_ge(at_out, L * 8 + 10)
                for k in range(KT + 2):
                    if k < KT:
                        dve.wait_ge(silu_done, L * 2 + (k // 4 + 1))
                        dve.tensor_tensor(OBR[:, k, :], OBR[:, k, :], U[:, k, :], ALU.mult).then_inc(t_ready, 1)
                    if k >= 2:
                        rest_lo(dve, stages + S_OBR, k - 2, OBR_LO[:, k - 2, :], OBR[:, k - 2, :], OBR_HI[:, k - 2, :])
                for ob in range(KT + 1):
                    if ob < KT:
                        s, quad = ob % 4, q0 + (15 + ob // 4)
                        ml = (RB if ob < 4 else WB)[:, 4 * s:4 * s + 4, :]
                        if ob < 4:
                            dve.wait_ge(sig_ready, L * 4 + (ob + 1))
                        else:
                            for i in range(4):
                                dve.wait_ge(evac_done[i], q0 + (12 + s))
                        dve.wait_ge(mm_done[s], quad + 1)
                        for i in range(NBR):
                            op = dve.tensor_tensor(ml[:, i, :], ml[:, i, :], bank[4 * (ob % 2) + i][:, :], ALU.mult)
                        op.then_inc(evac_done[s], 1)
                        dve.drain()
                        dve.tensor_tensor(ml[:, 0:2, :], ml[:, 0:2, :], ml[:, 2:4, :], ALU.add)
                        dve.drain()
                        dve.tensor_tensor(ACC[:, ob, :], ml[:, 0, :], ml[:, 1, :], ALU.add).then_inc(t_ready, 1)
                    if ob:
                        rest_lo(dve, stages + S_ACC, ob - 1, ACC_LO[:, ob - 1, :], ACC[:, ob - 1, :], ACC_HI[:, ob - 1, :])
                for blk in range(KT):
                    s = blk % 4
                    dve.wait_ge(mm_done[s], q0 + (18 + blk // 4))
                    op = dve.tensor_tensor(X[:, blk, :], X[:, blk, :], bank[s % 2][:, :], ALU.add)
                    op.then_inc(evac_done[s], 1)
                dve.drain()
                dve.sem_inc(x_ready, 1)
            norm_mean(dve, 9)
            norm_apply(dve, 9, H, X, vec(V_FINAL))

        @block.gpsimd
        def _(pool):
            pool.dma_start(CT, c_pad).then_inc(ct_in, 16)
            for q in range(PPB):
                pool.dma_start(BL[q], b_pad[q]).then_inc(bl_full[q], 16)
            for q in range(PPB):
                op = pool.memset(CL[q], 0.0)
            pool.drain()
            pool.sem_inc(cl_zero, 1)
            pool.sem_inc(y_done, 4)
            pool.sem_inc(da_pv, 2)
            pool.sem_inc(at_turned, 2)
            pool.sem_inc(at_pv, 2)
            pool.wait_ge(const_ready, 1)
            norm_root(pool, 0)

            def table(b, q):
                n = 4 * b + q

                def part(tab, c):
                    if isinstance(b, int):
                        return tab[:, n, c, :]
                    return tab[:, bass.ds(n, 1), c, :].rearrange("p a i -> p (a i)")

                hi = [part(HIT, c).rearrange("p (j i) -> p j i", i=1).to_broadcast([P, HI, LO]) for c in range(2)]
                lo = [part(LOT, c).rearrange("p (j i) -> p j i", j=1).to_broadcast([P, HI, LO]) for c in range(2)]
                to = [x.rearrange("p (j i) -> p j i", j=HI) for x in (*ROT[q % 2], *PTMP)]
                pool.wait_ge(ss_ready, n + 1)
                pool.tensor_tensor(to[0], hi[0], lo[0], ALU.mult)
                pool.tensor_tensor(to[2], hi[1], lo[1], ALU.mult)
                pool.tensor_tensor(to[1], hi[1], lo[0], ALU.mult)
                pool.tensor_tensor(to[3], hi[0], lo[1], ALU.mult)
                pool.drain()
                pool.tensor_tensor(to[0], to[0], to[2], ALU.subtract)
                pool.tensor_tensor(to[1], to[1], to[3], ALU.add).then_inc(tab_ready, 1)
                pool.drain()

            def rope(hd):
                for s in range(2):
                    pool.wait_ge(evac_done[s], hd + (Q_HEAD + 1))
                if not isinstance(hd, int):
                    pool.wait_ge(da_scores, 8 * hd)
                for raw, swapped in ((QRAW, QSW), (KRAW, KSW)):
                    pool.tensor_tensor(raw, raw, COS, ALU.mult)
                    pool.tensor_tensor(swapped, swapped, SIN, ALU.mult)
                pool.drain()
                pool.tensor_tensor(QH, QRAW, QSW, ALU.add)
                pool.tensor_tensor(KH, KRAW, KSW, ALU.add).then_inc(rope_done, 1)

            def head_body(b, last):
                for q in range(PPB):
                    table(b, q)
                    if not last:
                        pool.wait_ge(bu_ready, 4 * b + q + 1)
                        src = b_pad[4 * b + q + 4] if isinstance(b, int) else \
                            b_pad[bass.ds(4 * b + q + 4, 1)].rearrange("a p c m -> (a p) c m")
                        pool.dma_start(BL[q], src).then_inc(bl_full[q], 16)
                if not last:
                    rope(b + 1)

            rope(0)
            pool.wait_ge(prep_done, 1)
            heads(pool, head_body)
            pool.wait_ge(ss_ready, PAIRS + 2)
            pool.dma_start(MEMRAW, mem_in).then_inc(mem_loaded, 16)
            pool.wait_ge(da_scores, 8 * HEADS)
            pool.dma_start(TAB[:, :], rope2).then_inc(rope2_in, 16)
            pool.wait_ge(da_pv, 4 * HEADS + 2)
            for s in range(3):
                weight_lo(pool, Q_GLU, s)
            pool.wait_ge(hvar_ready, 1)
            root(pool, HVAR, HR0, HRT, HRS).then_inc(hrs_ready, 1)
            weight_lo(pool, Q_GLU, 3)
            norm_root(pool, 1, 2)

            def weights_lo(first, last):
                with pool.Fori(first, last) as quad:
                    for s in range(4):
                        weight_lo(pool, quad, s)

            def root_within(quad, *norms):
                for s in range(2):
                    weight_lo(pool, quad, s)
                for n in norms:
                    norm_root(pool, n)
                for s in (2, 3):
                    weight_lo(pool, quad, s)

            weights_lo(Q_GLU + 1, Q_KX)
            root_within(Q_KX, 2)
            weights_lo(Q_KX + 1, Q_VX + 1)
            root_within(Q_VX + 1, 3)
            weights_lo(Q_XQ, Q_FF)
            root_within(Q_FF, 4, 5)
            weights_lo(Q_FF + 1, Q_L2)
            norm_root(pool, 6)
            with pool.Fori(0, LAYERS) as L:
                q0 = pool.snap(QL * L + Q_L2)
                for s in range(2):
                    weight_lo(pool, q0, s)

                def layer(ap):
                    return ap[bass.ds(L, 1)].rearrange("a p n -> (a p) n")
                pool.wait_ge(x_ready, L + 3)
                pool.dma_start(LVEC[:, :], layer(lvecs)).then_inc(lvec_in, 16)
                for dst, src in ((W2K, cmp_w2k), (W2V, cmp_w2v), (B2V, cmp_b2v), (POS, cmp_pos), (LW[:, 288:544], pool_w)):
                    pool.dma_start(dst, layer(src)).then_inc(lw_in, 16)
                pool.dma_start(R[:, 24 * T:32 * T], layer(cmp_w1)).then_inc(w1_in, 16)
                norm_root(pool, L + 7)
                for s in (2, 3):
                    weight_lo(pool, q0, s)
                with pool.Fori(0, QL - 1) as i:
                    quad = pool.snap(q0 + i + 1)
                    for s in range(4):
                        weight_lo(pool, quad, s)
            norm_root(pool, 9)


def tables():
    f = np.float32

    def angles(theta, half, dim):
        inv = (f(theta) ** (-np.arange(half, dtype=f) * f(2.0) / f(dim))).astype(f)
        return (np.arange(T, dtype=f)[None, :] * inv[:, None]).astype(f)

    a1 = angles(10000.0, DH // 2, DH)
    cos1, sin1 = np.cos(a1).astype(f), np.sin(a1).astype(f)
    rope1 = np.concatenate([np.tile(cos1, (4, 1)), np.concatenate([-sin1, sin1] * 2, 0)], 1)
    a2 = angles(500000.0, 8, 16)
    cos2, sin2 = np.cos(a2).astype(f), np.sin(a2).astype(f)
    c = np.concatenate([cos2, cos2, np.ones((48, T), f)], 0)
    s = np.concatenate([-sin2, sin2, np.zeros((48, T), f)], 0)
    rope2 = np.concatenate([np.tile(c, (2, 1)), np.tile(s, (2, 1))], 1)

    con = np.zeros((P, C_END), f)
    con[:, C_ID:C_ID + P] = np.eye(P, dtype=f)
    i, j = np.arange(P)[:, None], np.arange(P)[None, :]
    con[:, C_CAUSAL:C_CAUSAL + P] = np.where(j > i, MASKED, 0)
    con[:, C_CHUNK:C_CHUNK + P] = np.where(j // 64 > i // 64, MASKED, 0)
    for base in (0, 64):
        for d in range(16):
            con[base + d, C_SWAP + base + (d + 8) % 16] = 1
    ends = np.arange(NC) * CMP_STRIDE + CMP_LEN - 1
    for t in range(TT):
        tok = t * P + np.arange(P)
        con[:, C_CMP + 32 * t:C_CMP + 32 * t + NC] = np.where(ends[None, :] <= tok[:, None], 0, MASKED)
        con[:, C_VALID + t] = tok >= ends[0]
    for h in range(4):
        con[32 * h, C_FQ] = 1
        con[32 * h + 1, C_FK] = 1
        con[32 * h + 1, C_NFK] = -1
    for blk in range(2):
        for half in range(2):
            w = (2, 4, 8, 16)[2 * blk + half]
            rows = slice(64 * half, 64 * half + 64)
            con[rows, C_W + blk] = 1 / w
            con[rows, C_INV + 16 * blk:C_INV + 16 * blk + 16] = 1 / np.minimum(np.arange(1, 17), w)
    return rope1.astype(f), rope2.astype(f), con


def stream(w):
    k, n = w.shape
    return w.reshape(k // P, P, n // P, P).transpose(2, 1, 0, 3)


def by_partition(v):
    return v.reshape(-1, P).T


def kernel(x, mem, norm_mix_pre, w_in, b_gate, ssm_lambda_re, ssm_lambda_im, ssm_log_dt,
           ssm_b_re, ssm_b_im, ssm_c_re, ssm_c_im, ssm_d, w_glu, b_glu, w_ssm_proj,
           da_lambda_q1, da_lambda_k1, da_lambda_q2, da_lambda_k2, da_head_norm, w_da_proj,
           w_mix_out, norm_mix_post, norm_x_pre, norm_mem, w_xq, w_xkv, w_xo, norm_x_post,
           norm_ff_pre, w_ff1, w_ff2, norm_ff_post, norm_g_2, w_in_2, fox_f_bias_2, cmp_pos_2,
           cmp_w1_2, cmp_b1_2, cmp_w2_2, cmp_b2_2, pool_w_2, pool_scale_2, conv_w_2, w_branch_2,
           w_out_2, final_norm_g_2):
    import concourse.bacc as bacc
    from concourse.bass_utils import run_bass_kernel_spmd

    f = np.float32
    npa = lambda a: np.asarray(a)
    cat = np.concatenate

    wi = stream(npa(w_in)[0])
    u_blk, q_blk, k_blk, v_blk, ga, gb = (wi[i * 8:(i + 1) * 8] for i in range(6))
    per_head = np.stack([q_blk, k_blk, ga, v_blk], 1).reshape(32, P, KT, P)
    wkv = stream(npa(w_xkv)[0])
    ff1, ff2 = stream(npa(w_ff1)[0]), stream(npa(w_ff2)[0])
    ff = [ff1[KT * c:KT * c + KT] if which == 1 else ff2[:, :, KT * c:KT * c + KT] for which, c in FF_ORDER]
    parts = [u_blk, gb, per_head, stream(npa(w_glu)[0]), stream(npa(w_da_proj)[0]),
             stream(npa(w_ssm_proj)[0]), stream(npa(w_mix_out)[0]), wkv, stream(npa(w_xq)[0]),
             stream(npa(w_xo)[0])] + ff
    kv0, pool0, conv0, fox0, gate0, merge0 = 256, 652, 908, 1676, 2448, 3472
    r = lambda a, n: list(range(a, a + n))
    kvc = lambda i: r(kv0 + 64 * i, 64)
    small = [-1] * P
    for h in range(4):
        small[32 * h] = small[32 * h + 1] = 2444 + h
    for g in range(12):
        small[2 + g] = 640 + g
    cols = (r(0, 256) + kvc(2) + kvc(4) + kvc(0) + kvc(1) + kvc(3) + kvc(5) + small
            + r(fox0, 768) + r(pool0, 256) + r(conv0, 768) + r(gate0, 1024))
    for ob in range(8):
        for i in range(4):
            cols += r(merge0 + i * D + ob * P, P)
    cols = np.array(cols)
    for l in range(LAYERS):
        w = npa(w_in_2)[l]
        w = cat([w, np.zeros((D, 1), w.dtype)], 1)[:, cols]
        parts.append(stream(w))
        parts.append(npa(w_branch_2)[l].reshape(4, 2, P, 8, P).transpose(3, 2, 0, 1, 4).reshape(8, P, KT, P))
        parts.append(stream(npa(w_out_2)[l]))
    weights = np.ascontiguousarray(cat(parts, 0))
    assert weights.shape[0] == 4 * Q_END

    pad64 = lambda v: cat([npa(v)[0], np.zeros(64, f)])[:, None]
    state = lambda a: npa(a)[0].reshape(PAIRS, P).T
    ldt = np.repeat(npa(ssm_log_dt)[0], STATE).reshape(PAIRS, P).T
    vecs = cat([by_partition(npa(norm_mix_pre)[0]), by_partition(npa(b_gate)[0]), by_partition(npa(ssm_d)[0]),
                by_partition(npa(b_glu)[0]), by_partition(npa(norm_mix_post)[0]), by_partition(npa(norm_x_pre)[0]),
                by_partition(npa(norm_mem)[0]), by_partition(npa(norm_x_post)[0]), by_partition(npa(norm_ff_pre)[0]),
                by_partition(npa(norm_ff_post)[0]), npa(da_head_norm)[0][:, None],
                pad64(da_lambda_q1), pad64(da_lambda_k1), pad64(da_lambda_q2), pad64(da_lambda_k2),
                by_partition(npa(final_norm_g_2)), state(ssm_lambda_re), state(ssm_lambda_im), ldt], 1)

    b_pad = np.zeros((PAIRS, P, 2, P), f)
    c_pad = np.zeros((P, PAIRS, 2, 32), f)
    for n in range(PAIRS):
        for g2 in range(2):
            rows = slice(32 * (n % 4) + 16 * g2, 32 * (n % 4) + 16 * g2 + 16)
            st = slice(64 * g2, 64 * g2 + 64)
            for c, (b, cc) in enumerate(((ssm_b_re, ssm_c_re), (ssm_b_im, ssm_c_im))):
                b_pad[n, rows, c, st] = npa(b)[0, 2 * n + g2].T
                c_pad[st, n, c, 16 * g2:16 * g2 + 16] = npa(cc)[0, 2 * n + g2].T

    lv = np.zeros((LAYERS, P, L_END), f)
    pw = np.zeros((LAYERS, P, 2, P), f)
    for l in range(LAYERS):
        lv[l, :, L_NORM:L_NORM + 8] = by_partition(npa(norm_g_2)[l])
        lv[l, :, L_POOL:L_POOL + 2] = by_partition(npa(pool_scale_2)[l])
        for tap in range(3):
            lv[l, :, L_CONV + 2 * tap:L_CONV + 2 * tap + 2] = by_partition(npa(conv_w_2)[l, tap])
        for h in range(4):
            lv[l, 32 * h:32 * h + 2, L_FBIAS] = npa(fox_f_bias_2)[l, h]
        lv[l, :, L_B1:L_B1 + 2] = npa(cmp_b1_2)[l].T
        for half in (0, 64):
            lv[l, half:half + 64, L_B2K] = npa(cmp_b2_2)[l, 0]
        for i in range(4):
            rows = slice(64 * (i % 2), 64 * (i % 2) + 64)
            pw[l, rows, i // 2, rows] = npa(pool_w_2)[l, i]
    cw1 = npa(cmp_w1_2).reshape(LAYERS, 2, CMP_LEN, 64, P).transpose(0, 1, 3, 2, 4).reshape(LAYERS, P, CMP_LEN * P)
    pos = npa(cmp_pos_2).transpose(0, 1, 3, 2).reshape(LAYERS, P, CMP_LEN)
    w2k = cat([npa(cmp_w2_2)[:, 0]] * 2, 2)
    w2v = npa(cmp_w2_2)[:, 1]
    b2v = npa(cmp_b2_2)[:, 1:2]
    rope1, rope2, con = tables()

    feat = lambda a: npa(a)[0].T.reshape(KT, P, -1).transpose(1, 0, 2)
    arrays = {
        "x_in": feat(x), "mem_in": feat(mem), "weights": weights, "vecs": vecs, "lvecs": lv, "consts": con,
        "rope1": rope1, "rope2": rope2, "b_pad": b_pad, "c_pad": c_pad, "cmp_w1": cw1, "cmp_pos": pos,
        "cmp_w2k": w2k, "cmp_w2v": w2v, "cmp_b2v": b2v, "pool_w": pw.reshape(LAYERS, P, 2 * P),
    }
    arrays = {k: np.ascontiguousarray(v) for k, v in arrays.items()}
    nc = bacc.Bacc("TRN2", target_bir_lowering=False, num_devices=1)
    args = {k: nc.dram_tensor(k, v.shape, mybir.dt.from_np(v.dtype), kind="ExternalInput").ap()
            for k, v in arrays.items()}
    out = nc.dram_tensor("out", (P, KT, T), F32, kind="ExternalOutput").ap()
    build(nc, out=out, **args)
    res = run_bass_kernel_spmd(nc, [arrays], core_ids=[0])
    got = res.results[0]["out"]
    return got.transpose(2, 1, 0).reshape(1, T, D)
```

```python
from contextlib import ExitStack

import numpy as np

import concourse.bass as bass
from concourse import mybir

F32 = mybir.dt.float32
F32R = mybir.dt.float32r
ALU = mybir.AluOpType
ACT = mybir.ActivationFunctionType
AX = mybir.AxisListType

P = 128
D = 1024
T = 512
KT = D // P
TT = T // P
MEM = 256
EPS = 1e-6
MASKED = -1e30

HEADS = 8
DH = 64
GROUPS, STATE = 64, 64
PAIRS = GROUPS // 2
PPB = 4
LO, HI = 16, 32
LAM_INIT = 0.8 - 0.6
XH = 4
XD = D // XH

LAYERS = 2
NH = 4
CMP_LEN, CMP_STRIDE = 32, 16
NC = (T - CMP_LEN) // CMP_STRIDE + 1
NBR = 4

Q_U, Q_HEAD, Q_GB = 0, 2, 10
Q_GLU, Q_DA, Q_SSM, Q_MIX = 12, 14, 16, 18
Q_KX, Q_VX, Q_XQ, Q_XO = 20, 22, 24, 26
Q_FF, Q_L2 = 28, 44
FF_ORDER = ((1, 0), (1, 1), (2, 0), (1, 2), (2, 1), (1, 3), (2, 2), (2, 3))
S_H0, S_YSG, S_YA, S_MEMN, S_YS2, S_MG, S_HX, S_OX, S_HF, S_L2 = (KT * i for i in range(10))
S_H, S_OBR, S_ACC, SL = (KT * i for i in range(4))
QL = 19
Q_END = Q_L2 + LAYERS * QL

V_MIX_PRE, V_BGATE, V_SSMD, V_BGLU, V_MIX_POST = 0, 8, 24, 32, 40
V_X_PRE, V_MEM, V_X_POST, V_FF_PRE, V_FF_POST = 48, 56, 64, 72, 80
V_HEADNORM, V_LQ1, V_LK1, V_LQ2, V_LK2, V_FINAL = 88, 89, 90, 91, 92, 93
V_LRE, V_LIM, V_LDT = 101, 133, 165
V_END = 197
L_NORM, L_POOL, L_CONV, L_FBIAS, L_B1, L_B2K = 0, 8, 10, 16, 17, 19
L_END = 20
C_ID, C_CAUSAL, C_CHUNK, C_SWAP = 0, 128, 256, 384
C_CMP = 512
C_VALID = 640
C_FQ, C_FK, C_NFK = 644, 645, 646
C_INV = 648
C_W = 680
C_END = 682


def build(nc, x_in, mem_in, weights, vecs, lvecs, consts, rope1, rope2, b_pad, c_pad,
          cmp_w1, cmp_pos, cmp_w2k, cmp_w2v, cmp_b2v, pool_w, out):
    ctx = ExitStack()
    with ctx:
        place = {"end": 16512}

        def sb(name, cols):
            place[name] = place["end"]
            place["end"] += -(-4 * cols // 32) * 32
            assert place["end"] <= 229344
            return nc.alloc_sbuf_tensor_at(name, [P, cols], F32, offset=place[name])

        def rounded(name, home, first, n, width=T):
            t = nc.alloc_sbuf_tensor_at(name, [P, n * width], F32R, offset=place[home] + 4 * T * first)
            return t[:, :].rearrange("p (k t) -> p k t", k=n, t=width)

        def sem(name):
            return ctx.enter_context(nc.semaphore(name))

        def sems(name, n):
            return [sem(f"{name}{i}") for i in range(n)]

        def blocks(ap, n, width=T):
            return ap.rearrange("p (k t) -> p k t", k=n, t=width)

        X = blocks(sb("residual", KT * T)[:, :], KT)
        H_ = sb("normed", KT * T)
        H = blocks(H_[:, :], KT)
        SLOTS = sb("weight_slots", 4 * KT * P)
        slot = [blocks(SLOTS[:, s * KT * P:(s + 1) * KT * P], KT, P) for s in range(4)]
        U_ = sb("u_region", KT * T)
        U = blocks(U_[:, :], KT)
        R = sb("wide_region", 32 * T)
        RB = blocks(R[:, :], 32)
        R3 = sb("work_region", 16 * T)
        WB = blocks(R3[:, :], 16)
        V_ = sb("v_region", KT * T)
        TAB = sb("rope_tables", 2 * T)
        COS, SIN = TAB[:, 0:T], TAB[:, T:2 * T]
        EX_ = sb("attention_work", 11 * T)
        EX = blocks(EX_[:, :], 11)
        VEC = sb("vectors", V_END)
        LVEC = sb("layer_vectors", L_END)
        CON = sb("constants", C_END)
        SMALL = sb("small", 240)

        ident = CON[:, C_ID:C_ID + P]
        ones = SMALL[:, 0:1]
        VAR, R0, RT, RSTD = SMALL[:, 4:8], SMALL[:, 8:12], SMALL[:, 12:16], SMALL[:, 16:20]
        HALF = SMALL[:, 20:52]
        HVAR, HR0, HRT, HRS = (SMALL[:, 52 + 32 * i:84 + 32 * i] for i in range(4))
        NMAX, RSUM, RINV = SMALL[:, 180:184], SMALL[:, 184:188], SMALL[:, 188:192]
        LAMP, LAME, NLAM, HN08 = SMALL[:, 192:194], SMALL[:, 194:196], SMALL[:, 196:197], SMALL[:, 197:198]
        ONE_ROW = SMALL[0:1, 200:232]

        bank = [ctx.enter_context(nc.psum_tensor(f"bank{i}", [P, T], F32)) for i in range(8)]

        TMP = [WB[:, i, :] for i in range(4)]
        ROT = [[WB[:, 6 + 2 * d + c, :] for c in range(2)] for d in range(2)]
        SS = [[WB[:, 10 + 2 * d + c, :] for c in range(2)] for d in range(2)]
        PTMP = [WB[:, 14 + c, :] for c in range(2)]
        S5C = R[:, 24 * T:32 * T]
        CT = S5C[:, 0:2048].rearrange("p (n c m) -> p n c m", n=PAIRS, c=2)
        BL = [S5C[:, 2048 + 256 * q:2304 + 256 * q].rearrange("p (c m) -> p c m", c=2) for q in range(PPB)]
        CL = [S5C[:, 3072 + 256 * q:3328 + 256 * q].rearrange("p (c m) -> p c m", c=2) for q in range(PPB)]
        LOT = V_[:, 0:1024].rearrange("p (n c i) -> p n c i", n=PAIRS, c=2)
        HIT = V_[:, 1024:3072].rearrange("p (n c j) -> p n c j", n=PAIRS, c=2)
        PREP = V_[:, 3072:4096].rearrange("p (a n) -> p a n", a=32)
        RADIUS = PREP[:, 0, :]

        def weight_parts(name, home, first):
            return [[rounded(f"{name}_{part}{i}", home, first + 4 * n + 2 * i, KT, P) for i in range(2)]
                    for n, part in enumerate(("hi", "lo"))]

        W_HEADS = weight_parts("head_weight", "wide_region", 8)
        W_MAIN = weight_parts("weight", "attention_work", 0)
        H1_HI, H1_LO = rounded("h1_hi", "normed", 0, 8), rounded("h1_lo", "residual", 0, 8)
        YSG_HI, YSG_LO = rounded("gelu_hi", "wide_region", 24, 8), rounded("gelu_lo", "work_region", 0, 8)
        YA_HI, YA_LO = rounded("ya_hi", "work_region", 8, 8), rounded("ya_lo", "wide_region", 16, 8)
        MEMN_HI, MEMN_LO = rounded("memn_hi", "normed", 0, KT, MEM), rounded("memn_lo", "normed", 4, KT, MEM)
        YS2_HI, YS2_LO = rounded("ys2_hi", "wide_region", 24, 8), rounded("ys2_lo", "u_region", 0, 8)
        MG_HI, MG_LO = rounded("mg_hi", "v_region", 0, 8), rounded("mg_lo", "work_region", 0, 8)
        HX_HI, HX_LO = rounded("hx_hi", "wide_region", 16, 8), rounded("hx_lo", "wide_region", 8, 8)
        OX_HI, OX_LO = rounded("ox_hi", "v_region", 0, 8), rounded("ox_lo", "normed", 0, 8)
        H_HI, H_LO = rounded("h_hi", "v_region", 0, 8), rounded("h_lo", "normed", 0, 8)
        F_HI = [rounded(f"ff_hi{i}", "wide_region", 16 * i + 8, 8) for i in range(2)]
        F_LO = [rounded(f"ff_lo{i}", "wide_region", 16 * i, 8) for i in range(2)]
        OBR_HI, OBR_LO = rounded("obr_hi", "work_region", 0, 8), rounded("obr_lo", "wide_region", 24, 8)
        ACC_HI, ACC_LO = rounded("acc_hi", "v_region", 0, 8), rounded("acc_lo", "u_region", 0, 8)

        QRAW, QSW, KRAW, KSW, QH, KH, VH = (EX[:, i, :] for i in range(7))
        PR = [EX[:, 7, :], EX[:, 8, :]]
        VT_H = WB[:, 5, :]
        PC = WB[:, 4, :]
        PTB = [EX[:, 9, :], EX[:, 10, :]]
        YA = RB[:, 16:24, :]
        YS2 = U
        PAIR = [EX[:, 8, :], EX[:, 9, :]]
        MG = WB[:, 0:8, :]
        SQ = WB[:, 8:16, :]
        MEMRAW, MEMN = blocks(V_[:, 2048:4096], KT, MEM), blocks(H_[:, 2048:4096], KT, MEM)
        MSQ = blocks(V_[:, 0:2048], KT, MEM)
        VT_X = [RB[:, 24, :], RB[:, 25, :]]
        KX, VX = blocks(U_[:, 0:2048], KT, MEM), blocks(U_[:, 2048:4096], 2, D)
        YB = RB[:, 0:8, :]
        HX, QX = RB[:, 8:16, :], RB[:, 24:32, :]
        YF = U
        RELU = [EX[:, 8 + i, :] for i in range(3)]
        APR, APT = [EX[:, 8, :], EX[:, 9, :]], [EX[:, 10, :], WB[:, 15, :]]

        NQ, KS, KW, VSW = WB[:, 0:2, :], WB[:, 2, :], WB[:, 3, :], WB[:, 4, :]
        VT = [RB[:, 6, :], RB[:, 7, :]]
        FQ, FK, FV = WB[:, 5:7, :], WB[:, 7:9, :], WB[:, 9:11, :]
        FCQ, FCK, KCVC = WB[:, 11, :], WB[:, 12, :], WB[:, 13, :]
        CW = R3[:, 14 * T:15 * T]
        G12 = CW[:, 0:64].rearrange("p (t g) -> p t g", t=TT)
        HID, KCR, KC, VC, KCT = CW[:, 64:128], CW[:, 128:128 + NC], CW[:, 160:160 + NC], CW[:, 192:256], CW[:, 256:320]
        RAW, RTMP = RB[:, 8:11, :], RB[:, 11:14, :]
        FZ, FL = RB[:, 14, :], RB[:, 15, :]
        FLAT = [buf[:, o:o + CMP_LEN * NC].rearrange("p (l n) -> p l n", l=CMP_LEN // 2)
                for buf, o in ((R, 16 * T), (EX_, 8 * T))]
        LW = R[:, 18 * T:20 * T]
        W2K, W2V, B2V, POS = LW[:, 0:128], LW[:, 128:192], LW[0:1, 192:256], LW[:, 256:288]
        PW = LW[:, 288:544].rearrange("p (b n) -> p b n", b=2)
        PA, PB = R[:, 20 * T:20 * T + 528], R[:, 20 * T + 528:20 * T + 1056]
        CP = R[:, 20 * T + 1056:20 * T + 1570]
        W1 = R[:, 24 * T:32 * T].rearrange("p (l n) -> p l n", l=CMP_LEN)
        PIN, CX, CB, CC = RB[:, 0:2, :], RB[:, 2:4, :], RB[:, 4:6, :], RB[:, 6:8, :]
        OBR = RB[:, 24:32, :]
        ACC = U
        ML = [RB[:, 4 * i:4 * i + 4, :] for i in range(6)] + [WB[:, 8 + 4 * i:12 + 4 * i, :] for i in range(2)]

        w_full, mm_done, evac_done = sems("w_full", 4), sems("mm_done", 4), sems("evac_done", 4)
        x_loaded = sems("x_loaded", 4)
        consts_in, mem_loaded, rope2_in, out_stored = (
            sem("consts_in"), sem("mem_loaded"), sem("rope2_in"), sem("out_stored"))
        rope1_in = sem("rope1_in")
        x_again, out_ready = sem("x_again"), sem("out_ready")
        const_ready = sem("const_ready")
        hv_ready, hv_turned, v_turned, v_used, g_turned = (
            sem("hv_ready"), sem("hv_turned"), sem("v_turned"), sem("v_used"), sem("g_turned"))
        w_hi, w_lo = sems("w_hi", 4), sems("w_lo", 4)
        t_ready, hi_ready, lo_ready = sem("t_ready"), sem("hi_ready"), sem("lo_ready")
        sq_ready, ms_ready, var_ready = sem("sq_ready"), sem("ms_ready"), sem("var_ready")
        rstd_ready, bc_ready, bc_used = sem("rstd_ready"), sem("bc_ready"), sem("bc_used")
        x_ready = sem("x_ready")
        cl_zero, prep_dt, prep_exp, prep_arg, prep_sin, prep_done = (
            sem("cl_zero"), sem("prep_dt"), sem("prep_exp"), sem("prep_arg"), sem("prep_sin"), sem("prep_done"))
        ct_in = sem("ct_in")
        bl_full = sems("bl_full", PPB)
        bu_ready, bu_used, tab_ready, ss_ready = sem("bu_ready"), sem("bu_used"), sem("tab_ready"), sem("ss_ready")
        cl_ready, y_done, y_used = sem("cl_ready"), sem("y_done"), sem("y_used")
        lam_prod, lam_sum, lam_exp = sem("lam_prod"), sem("lam_sum"), sem("lam_exp")
        rope_done, da_scores, da_max, da_exp = sem("rope_done"), sem("da_scores"), sem("da_max"), sem("da_exp")
        da_probs, da_turned, da_copied, da_pv, da_out = (
            sem("da_probs"), sem("da_turned"), sem("da_copied"), sem("da_pv"), sem("da_out"))
        hsq_ready, hms_ready, hvar_ready, hrs_ready, hbc_ready = (
            sem("hsq_ready"), sem("hms_ready"), sem("hvar_ready"), sem("hrs_ready"), sem("hbc_ready"))
        gates_done, ys_ready = sem("gates_done"), sem("ys_ready")
        xa_scores, xa_max, xa_exp, xa_probs, xa_turned, xa_copied, xa_pv = (
            sem("xa_scores"), sem("xa_max"), sem("xa_exp"), sem("xa_probs"), sem("xa_turned"),
            sem("xa_copied"), sem("xa_pv"))
        ff_hi, ff_lo = sem("ff_hi"), sem("ff_lo")
        lw_in, w1_in, lvec_in = sem("lw_in"), sem("w1_in"), sem("lvec_in")
        sw_ready, sw_used, nq_ready, f_log, f_ready = (
            sem("sw_ready"), sem("sw_used"), sem("nq_ready"), sem("f_log"), sem("f_ready"))
        flat_ready, hid_mm, hid_ready, kv2_mm, kcr_ready, kcs_mm, kc_ready = (
            sem("flat_ready"), sem("hid_mm"), sem("hid_ready"), sem("kv2_mm"), sem("kcr_ready"),
            sem("kcs_mm"), sem("kc_ready"))
        pooled_ready, pool_mm, pool_out, conv_out = sem("pooled_ready"), sem("pool_mm"), sem("pool_out"), sem("conv_out")
        at_scores, at_max, at_exp, at_probs, at_turned, at_copied, at_pv, at_out = (
            sem("at_scores"), sem("at_max"), sem("at_exp"), sem("at_probs"), sem("at_turned"),
            sem("at_copied"), sem("at_pv"), sem("at_out"))
        silu_done, sig_ready = sem("silu_done"), sem("sig_ready")

        def bank_free(pe, quad, s):
            if s >= 2:
                pe.wait_ge(evac_done[s - 2], quad + 1)
            elif not (isinstance(quad, int) and quad == 0):
                pe.wait_ge(evac_done[s + 2], quad)

        def gemm(pe, quad, s, hi, lo, width=T, stage=None, part=range(KT), parts=W_MAIN):
            if part[0] == 0:
                pe.wait_ge(w_lo[s], quad + 1)
                bank_free(pe, quad, s)
            to = bank[s % 2][:, 0:width]
            w_h, w_l = parts[0][s % 2], parts[1][s % 2]
            for k in part:
                if stage is not None:
                    pe.wait_ge(lo_ready, stage + (k + 1))
                pe.matmul(to, w_h[:, k, :], hi[:, k, 0:width], start=(k == 0), stop=False)
                pe.matmul(to, w_h[:, k, :], lo[:, k, 0:width], start=False, stop=False)
                mm = pe.matmul(to, w_l[:, k, :], hi[:, k, 0:width], start=False, stop=(k == KT - 1))
            if part[-1] == KT - 1:
                mm.then_inc(mm_done[s], 1)

        def turn_values(pe, quad, s, n, src, to, tiles=TT):
            pe.wait_ge(evac_done[s], quad + 1)
            for t in range(tiles):
                mm = pe.transpose(to[:, t * P:(t + 1) * P], src[:, t * P:(t + 1) * P], ident)
            mm.then_inc(v_turned, 1)

        def both(pe, quad, hi, lo, stage, width=T, norm=None):
            for i in range(2):
                for s in range(4):
                    gemm(pe, quad + i, s, hi, lo, width, stage if i == 0 and s == 0 else None)
                    if norm is not None and 4 * i + s:
                        norm_sum_block(pe, norm, 4 * i + s - 1)
            if norm is not None:
                norm_sum_block(pe, norm, KT - 1)

        def weight_hi(act, quad, s, parts=W_MAIN):
            act.wait_ge(w_full[s], 16 * quad + 16)
            if s >= 2:
                act.wait_ge(mm_done[s - 2], quad + 1)
            elif not (isinstance(quad, int) and quad == 0):
                act.wait_ge(mm_done[s + 2], quad)
            act.activation(parts[0][s % 2], slot[s], ACT.Copy).then_inc(w_hi[s], 1)

        def weight_lo(eng, quad, s, parts=W_MAIN):
            eng.wait_ge(w_hi[s], quad + 1)
            eng.tensor_tensor(parts[1][s % 2], slot[s], parts[0][s % 2].bitcast(F32),
                              ALU.subtract).then_inc(w_lo[s], 1)

        def ahead(act, quad, s, parts=W_MAIN):
            if s < 2:
                weight_hi(act, quad, s + 2, parts)
            else:
                weight_hi(act, quad + 1, s - 2, parts)

        def round_hi(act, stage, k, hi, t):
            act.wait_ge(t_ready, stage + (k + 1))
            act.activation(hi, t, ACT.Copy).then_inc(hi_ready, 1)

        def rest_lo(dve, stage, k, lo, t, hi):
            dve.wait_ge(hi_ready, stage + (k + 1))
            dve.tensor_tensor(lo, t, hi.bitcast(F32), ALU.subtract).then_inc(lo_ready, 1)

        def squares(act, src, width=T, to=SQ):
            for k in range(KT):
                act.activation(to[:, k, 0:width], src[:, k, 0:width], ACT.Square).then_inc(sq_ready, 1)

        def squares_of_sum(act, adds):
            for k in range(KT):
                act.wait_ge(x_ready, KT * (adds - 1) + (k + 1))
                act.activation(SQ[:, k, :], X[:, k, :], ACT.Square).then_inc(sq_ready, 1)

        def norm_sum_block(pe, n, k, tiles=TT, squared=SQ):
            if k == 0 and not (isinstance(n, int) and n == 0):
                pe.wait_ge(var_ready, n)
            pe.wait_ge(sq_ready, n * KT + (k + 1))
            for t in range(tiles):
                mm = pe.matmul(bank[6][:, t * KT + k:t * KT + k + 1], squared[:, k, t * P:(t + 1) * P], ones,
                               start=True, stop=True)
            if k == KT - 1:
                mm.then_inc(ms_ready, 1)

        def norm_sums(pe, n, tiles=TT, squared=SQ):
            for k in range(KT):
                norm_sum_block(pe, n, k, tiles, squared)

        def norm_mean(dve, n, tiles=TT):
            dve.wait_ge(ms_ready, n + 1)
            if not (isinstance(n, int) and n == 0):
                dve.wait_ge(rstd_ready, n)
            dve.tensor_reduce(VAR[:, 0:tiles], bank[6][:, 0:tiles * KT].rearrange("p (t k) -> p t k", t=tiles),
                              AX.X, ALU.add)
            dve.drain()
            dve.tensor_scalar(VAR[:, 0:tiles], VAR[:, 0:tiles], 1.0 / D, EPS, ALU.mult,
                              ALU.add).then_inc(var_ready, 1)

        def root(pool, v, r0, rt, rs):
            pool.tensor_tensor(r0, v, HALF[:, 0:v.shape[-1]], ALU.pow)
            pool.drain()
            pool.tensor_tensor(rt, r0, r0, ALU.mult)
            pool.drain()
            pool.tensor_tensor(rt, rt, v, ALU.mult)
            pool.drain()
            pool.tensor_scalar(rt, rt, -0.5, 1.5, ALU.mult, ALU.add)
            pool.drain()
            return pool.tensor_tensor(rs, rt, r0, ALU.mult)

        def norm_root(pool, n, tiles=TT):
            pool.wait_ge(var_ready, n + 1)
            if not (isinstance(n, int) and n == 0):
                pool.wait_ge(bc_ready, n)
            root(pool, VAR[:, 0:tiles], R0[:, 0:tiles], RT[:, 0:tiles],
                 RSTD[:, 0:tiles]).then_inc(rstd_ready, 1)

        def norm_spread(pe, n, tiles=TT):
            pe.wait_ge(rstd_ready, n + 1)
            if not (isinstance(n, int) and n == 0):
                pe.wait_ge(bc_used, n)
            for t in range(tiles):
                mm = pe.matmul(bank[7][:, t * P:(t + 1) * P],
                               RSTD[:, t:t + 1].to_broadcast([P, P]), ident, start=True, stop=True)
            mm.then_inc(bc_ready, 1)

        def norm_split(dve, n, stage, t, hi, lo, src, gain, width=T):
            dve.wait_ge(bc_ready, n + 1)
            for k in range(KT + 2):
                if k < KT:
                    dve.scalar_tensor_tensor(t[:, k, 0:width], src[:, k, 0:width], gain[:, k:k + 1],
                                             bank[7][:, 0:width], ALU.mult, ALU.mult).then_inc(t_ready, 1)
                if k >= 2:
                    rest_lo(dve, stage, k - 2, lo[:, k - 2, :], t[:, k - 2, :], hi[:, k - 2, :])
            dve.sem_inc(bc_used, 1)

        def residual_add(dve, n, y, gain):
            dve.wait_ge(bc_ready, n + 1)
            for k in range(KT + 1):
                if k < KT:
                    op = dve.scalar_tensor_tensor(y[:, k, :], y[:, k, :], gain[:, k:k + 1], bank[7][:, :],
                                                  ALU.mult, ALU.mult)
                if k == KT - 1:
                    op.then_inc(bc_used, 1)
                if k:
                    dve.tensor_tensor(X[:, k - 1, :], X[:, k - 1, :], y[:, k - 1, :], ALU.add).then_inc(x_ready, 1)
                dve.drain()

        def copy_out(act, quad, s, dst, scale=1.0):
            act.wait_ge(mm_done[s], quad + 1)
            act.activation(dst, bank[s % 2][:, 0:dst.shape[-1]], ACT.Copy, scale=scale).then_inc(evac_done[s], 1)

        def one(ap, i):
            if isinstance(i, int):
                return ap[:, i, :]
            return ap[:, bass.ds(i, 1), :].rearrange("p a t -> p (a t)")

        def column(i):
            return VEC[:, i:i + 1] if isinstance(i, int) else VEC[:, bass.ds(i, 1)]

        def vec(col, n=KT):
            return VEC[:, col:col + n]

        def heads(eng, body):
            with eng.Fori(0, HEADS - 1) as b:
                body(b, False)
            body(HEADS - 1, True)

        STEPS = [(h, j, kind) for h in range(NH) for j in range(TT) for kind in ("cmp", "slc", "win", "fox")]
        NS = len(STEPS)
        FILL = 32

        def filler(i):
            if i >= NS:
                return []
            return [divmod(h, 2) for h in range(2 * i * FILL // NS, 2 * (i + 1) * FILL // NS)]

        block = ctx.enter_context(nc.Block())

        @block.sync
        def _(sp):
            for c in (1, 3):
                sp.dma_start(X[:, 2 * c:2 * c + 2, :], x_in[:, 2 * c:2 * c + 2, :]).then_inc(x_loaded[c], 16)
            for s in range(4):
                sp.dma_start(slot[s], weights[s]).then_inc(w_full[s], 16)
            with sp.Fori(1, Q_END) as quad:
                for s in range(4):
                    src = sp.snap(quad * 4 + s)
                    need = sp.snap(quad + 0)
                    sp.wait_ge(w_lo[s], need)
                    sp.dma_start(slot[s], weights[bass.ds(src, 1)].rearrange("a p k n -> (a p) k n")).then_inc(w_full[s], 16)
            for k in range(0, KT, 2):
                sp.wait_ge(out_ready, k + 2)
                sp.dma_start(out[:, k:k + 2, :], H[:, k:k + 2, :]).then_inc(out_stored, 16)
            sp.wait_ge(out_stored, 16 * KT // 2)

        @block.tensor
        def _(pe):
            pe.wait_ge(const_ready, 1)
            norm_sums(pe, 0)
            pe.wait_ge(lam_prod, 1)
            for c in range(2):
                mm = pe.matmul(bank[5][:, c:c + 1], LAMP[:, c:c + 1].to_broadcast([P, P]), ones, start=True, stop=True)
            mm.then_inc(lam_sum, 1)
            norm_spread(pe, 0)
            for quad in range(Q_U, Q_HEAD + 1):
                for s in range(4):
                    gemm(pe, quad, s, H1_HI, H1_LO, T, S_H0 if quad == 0 and s == 0 else None, parts=W_HEADS)

            def head_values(hd, src=VT_H):
                pe.wait_ge(hv_ready, hd + 1)
                for t in range(TT):
                    mm = pe.transpose(bank[1][:, t * P:(t + 1) * P], src[:, t * P:(t + 1) * P], ident)
                mm.then_inc(hv_turned, 1)

            head_values(0, PR[0])
            for s in range(4):
                pe.wait_ge(evac_done[s], 2)
            pe.wait_ge(prep_done, 1)

            def da_score(b, j, c):
                m = 8 * b + 2 * j + c
                if j == 0 and c == 0:
                    pe.wait_ge(rope_done, b + 1)
                pe.wait_ge(da_exp, m + 1)
                rows = slice(DH * c, DH * c + DH)
                pe.matmul(bank[5][:, 0:(j + 1) * P], QH[rows, j * P:(j + 1) * P], KH[rows, 0:(j + 1) * P],
                          start=True, stop=False)
                pe.matmul(bank[5][:, j * P:(j + 1) * P], ident, CON[:, C_CHUNK:C_CHUNK + P],
                          start=False, stop=True).then_inc(da_scores, 1)

            def da_turn(b, j):
                pe.wait_ge(da_probs, 4 * b + j + 1)
                pe.wait_ge(da_copied, 4 * b + j + 1)
                for t in range(j + 1):
                    mm = pe.transpose(bank[6][:, t * P:(t + 1) * P], PC[:, t * P:(t + 1) * P], ident)
                mm.then_inc(da_turned, 1)

            def da_values(b, j):
                if j == 0:
                    pe.wait_ge(da_out, b + 1)
                    pe.wait_ge(evac_done[3], b + (Q_HEAD + 1))
                pe.wait_ge(da_copied, 4 * b + j + 2)
                for t in range(j + 1):
                    mm = pe.matmul(bank[7][:, j * P:(j + 1) * P], VH[:, t * P:(t + 1) * P],
                                   PTB[j % 2][:, t * P:(t + 1) * P], start=(t == 0), stop=(t == j))
                mm.then_inc(da_pv, 1)

            def s5_in(b, q):
                pe.wait_ge(bl_full[q], 16 * b + 16)
                pe.wait_ge(bu_used, 4 * b + q + 1)
                for c in range(2):
                    mm = pe.matmul(bank[2 + c][:, :], BL[q][:, c, :], one(U, b), start=True, stop=True)
                mm.then_inc(bu_ready, 1)

            def s5_out(b, q):
                pe.wait_ge(ss_ready, 4 * b + q + 3)
                pe.wait_ge(cl_ready, 4 * b + q + 1)
                if q == 0:
                    pe.wait_ge(y_used, b + 1)
                for c in range(2):
                    mm = pe.matmul(bank[4][:, :], CL[q][:, c, :], SS[q % 2][c], start=(q == 0 and c == 0),
                                   stop=(q == PPB - 1 and c == 1))
                mm.then_inc(y_done, 1)

            def head_body(b, last):
                for q in range(PPB):
                    da_score(b, q, 0)
                    if last:
                        if q % 2:
                            gemm(pe, Q_GB, q // 2, H1_HI, H1_LO, parts=W_HEADS)
                    else:
                        gemm(pe, b + (Q_HEAD + 1), q, H1_HI, H1_LO, parts=W_HEADS)
                    da_score(b, q, 1)
                    if q < PPB - 1:
                        s5_in(b, q + 1)
                    elif not last:
                        s5_in(b + 1, 0)
                    if q:
                        da_turn(b, q - 1)
                        s5_out(b, q - 1)
                        da_values(b, q - 1)
                da_turn(b, 3)
                if not last:
                    head_values(b + 1)
                s5_out(b, 3)
                da_values(b, 3)

            s5_in(0, 0)
            heads(pe, head_body)

            for s in (2, 3):
                gemm(pe, Q_GB, s, H1_HI, H1_LO)
            gemm(pe, Q_GB + 1, 0, H1_HI, H1_LO)
            pe.wait_ge(hsq_ready, 1)
            for h in range(HEADS):
                for t in range(TT):
                    mm = pe.matmul(bank[6][:, TT * h + t:TT * h + t + 1], SQ[:, h, t * P:(t + 1) * P], ones,
                                   start=True, stop=True)
            mm.then_inc(hms_ready, 1)
            gemm(pe, Q_GB + 1, 1, H1_HI, H1_LO)
            pe.wait_ge(hvar_ready, 1)
            norm_sums(pe, 1, 2, MSQ)
            gemm(pe, Q_GB + 1, 2, H1_HI, H1_LO)
            norm_spread(pe, 1, 2)
            gemm(pe, Q_GB + 1, 3, H1_HI, H1_LO)
            pe.wait_ge(hrs_ready, 1)
            for s in range(4):
                for h in (2 * s, 2 * s + 1):
                    if h >= 2:
                        pe.wait_ge(t_ready, S_YA + (h - 1))
                    for t in range(TT):
                        mm = pe.matmul(bank[2 + h % 2][:, t * P:(t + 1) * P],
                                       HRS[:, TT * h + t:TT * h + t + 1].to_broadcast([P, P]), ident,
                                       start=True, stop=True)
                    mm.then_inc(hbc_ready, 1)
                gemm(pe, Q_GLU, s, YSG_HI, YSG_LO, T, S_YSG if s == 0 else None)
            for s in range(4):
                gemm(pe, Q_GLU + 1, s, YSG_HI, YSG_LO)
            both(pe, Q_DA, YA_HI, YA_LO, S_YA)
            both(pe, Q_SSM, YS2_HI, YS2_LO, S_YS2)
            both(pe, Q_MIX, MG_HI, MG_LO, S_MG, norm=2)
            for s in range(4):
                gemm(pe, Q_KX, s, MEMN_HI, MEMN_LO, MEM)
            norm_spread(pe, 2)
            for s in range(4):
                gemm(pe, Q_KX + 1, s, MEMN_HI, MEMN_LO, MEM)
            for n in range(KT + 1):
                if n == 4:
                    norm_sums(pe, 3)
                if n < KT:
                    gemm(pe, Q_VX + n // 4, n % 4, MEMN_HI, MEMN_LO, MEM)
                if n:
                    if n > 2:
                        pe.wait_ge(v_used, n - 2)
                    turn_values(pe, Q_VX + (n - 1) // 4, (n - 1) % 4, n - 1, VT_X[(n - 1) % 2],
                                bank[2 + (n - 1) % 2], 2)
            norm_spread(pe, 3)
            both(pe, Q_XQ, HX_HI, HX_LO, S_HX)
            for s in range(4):
                pe.wait_ge(evac_done[s], Q_XQ + 2)

            def xa_score(i):
                h, j = divmod(i, TT)
                if i >= 2:
                    pe.wait_ge(xa_exp, i - 1)
                for k in range(2):
                    mm = pe.matmul(bank[2 + i % 2][:, 0:MEM], QX[:, 2 * h + k, j * P:(j + 1) * P],
                                   KX[:, 2 * h + k, :], start=(k == 0), stop=(k == 1))
                mm.then_inc(xa_scores, 1)

            def xa_turn(i):
                pe.wait_ge(xa_probs, i + 1)
                if i >= 2:
                    pe.wait_ge(xa_copied, i - 1)
                for k in range(2):
                    mm = pe.transpose(bank[4 + i % 2][:, k * P:(k + 1) * P], APR[i % 2][:, k * P:(k + 1) * P], ident)
                mm.then_inc(xa_turned, 1)

            def xa_values(i):
                h, j = divmod(i, TT)
                if j == 0 and h >= 1:
                    pe.wait_ge(lo_ready, S_OX + 2 * h)
                pe.wait_ge(xa_copied, i + 1)
                for e in range(2):
                    for k in range(2):
                        mm = pe.matmul(bank[6 + e][:, j * P:(j + 1) * P],
                                       VX[:, k, h * XD + e * P:h * XD + (e + 1) * P],
                                       APT[i % 2][:, k * P:(k + 1) * P], start=(k == 0), stop=(k == 1))
                mm.then_inc(xa_pv, 1)

            for i in range(XH * TT + 2):
                if i < XH * TT:
                    xa_score(i)
                if i >= 2:
                    xa_values(i - 2)
                if 1 <= i <= XH * TT:
                    xa_turn(i - 1)
            both(pe, Q_XO, OX_HI, OX_LO, S_OX, norm=4)
            norm_spread(pe, 4)
            norm_sums(pe, 5)
            norm_spread(pe, 5)
            for step, (which, c) in enumerate(FF_ORDER):
                hi, lo = (H_HI, H_LO) if which == 1 else (F_HI[c % 2], F_LO[c % 2])
                if which == 1 and c == 0:
                    pe.wait_ge(lo_ready, S_HF + KT)
                if which == 2:
                    pe.wait_ge(ff_lo, KT * (c + 1) + 2)
                if step < len(FF_ORDER) - 1:
                    with pe.Fori(0, 2) as i:
                        for s in range(4):
                            gemm(pe, i + (Q_FF + 2 * step), s, hi, lo)
                else:
                    both(pe, Q_FF + 2 * step, hi, lo, None, norm=6)
            norm_spread(pe, 6)
            norm_sums(pe, 7)

            with pe.Fori(0, LAYERS) as L:
                q0 = pe.snap(QL * L + Q_L2)
                norm_spread(pe, L + 7)
                for s in range(4):
                    gemm(pe, q0, s, H_HI, H_LO, T, SL * L + (S_L2 + S_H) if s == 0 else None)
                gemm(pe, q0 + 1, 0, H_HI, H_LO)
                pe.wait_ge(w_lo[1], q0 + 2)
                bank_free(pe, q0 + 1, 1)
                (w_h, w_l) = W_MAIN[0][1], W_MAIN[1][1]
                terms = ((w_h, H_HI), (w_h, H_LO), (w_l, H_HI))
                for k in range(KT):
                    for n, (w, h) in enumerate(terms):
                        mm = pe.matmul(bank[1][:, :], w[:, k, :], h[:, k, :], start=(k == 0 and n == 0),
                                       stop=(k == KT - 1 and n == 2))
                mm.then_inc(mm_done[1], 1)
                for s in (0, 1, 2):
                    pe.wait_ge(evac_done[s], q0 + 1)
                for i in range(3):
                    mm = pe.matmul(bank[(2, 3, 5)[i]][:, :], CON[:, C_SWAP:C_SWAP + P], RAW[:, i, :],
                                   start=True, stop=True)
                mm.then_inc(sw_ready, 1)
                turn_values(pe, q0 + 1, 0, L * 3 + KT, VT[0], bank[6])
                gemm(pe, q0 + 1, 2, H_HI, H_LO)
                pe.wait_ge(evac_done[1], q0 + 2)
                for t in range(TT):
                    mm = pe.transpose(bank[4][:, t * P:(t + 1) * P], FZ[:, t * P:(t + 1) * P], ident)
                mm.then_inc(g_turned, 1)
                gemm(pe, q0 + 1, 3, H_HI, H_LO)
                for s in range(4):
                    gemm(pe, q0 + 2, s, H_HI, H_LO)
                    if s == 3:
                        turn_values(pe, q0 + 2, 2, L * 3 + (KT + 1), VT[1], bank[7])
                for s in range(4):
                    gemm(pe, q0 + 3, s, H_HI, H_LO)
                    if s == 0:
                        pe.wait_ge(v_used, L * 3 + (KT + 1))
                        turn_values(pe, q0 + 2, 3, L * 3 + (KT + 2), VT[0], bank[6])
                pe.wait_ge(v_used, L * 3 + (KT + 3))
                pe.wait_ge(flat_ready, L + 1)
                pe.wait_ge(w1_in, 16 * L + 16)
                for l in range(CMP_LEN):
                    half, at = divmod(l, CMP_LEN // 2)
                    mm = pe.matmul(bank[6][:, 0:2 * NC], W1[:, l, :], FLAT[half][:, at, :],
                                   start=(l == 0), stop=(l == CMP_LEN - 1))
                mm.then_inc(hid_mm, 1)
                for s in range(4):
                    gemm(pe, q0 + 4, s, H_HI, H_LO)
                pe.wait_ge(hid_ready, L + 1)
                pe.matmul(bank[6][:, 64:64 + NC], W2K, HID[:, 0:NC], start=True, stop=True)
                pe.matmul(bank[6][0:NC, 128:192], HID[:, 32:32 + NC], W2V, start=True, stop=False)
                pe.matmul(bank[6][0:NC, 128:192], ONE_ROW[:, 0:NC], B2V, start=False, stop=True).then_inc(kv2_mm, 1)
                pe.wait_ge(kcr_ready, L + 1)
                pe.matmul(bank[6][:, 96:96 + NC], CON[:, C_SWAP:C_SWAP + P], KCR, start=True, stop=True).then_inc(kcs_mm, 1)
                pe.wait_ge(pooled_ready, L + 1)
                pe.wait_ge(sw_used, L + 1)
                for i in range(2):
                    mm = pe.matmul(bank[2 + i][:, :], PW[:, i, :], RB[:, 16 + i, :], start=True, stop=True)
                mm.then_inc(pool_mm, 1)
                pe.wait_ge(nq_ready, L + 1)
                pe.wait_ge(f_ready, L + 1)
                pe.wait_ge(kc_ready, L + 1)
                pe.wait_ge(pool_out, L + 1)

                def score(i):
                    h, j, kind = STEPS[i]
                    rows = slice(64 * (h % 2), 64 * (h % 2) + 64)
                    to = bank[2 + i % 2]
                    pe.wait_ge(at_exp, L * NS + (i + 1))
                    if kind == "cmp":
                        pe.matmul(to[:, 0:NC], NQ[rows, h // 2, j * P:(j + 1) * P], KC[rows, :], start=True, stop=False)
                        mm = pe.matmul(to[:, 0:NC], ident, CON[:, C_CMP + 32 * j:C_CMP + 32 * j + NC],
                                       start=False, stop=True)
                    else:
                        keys = {"slc": KS, "win": KW, "fox": FK[:, h // 2, :]}[kind]
                        q = FQ if kind == "fox" else NQ
                        width = (j + 1) * P
                        pe.matmul(to[:, 0:width], q[rows, h // 2, j * P:(j + 1) * P], keys[rows, 0:width],
                                  start=True, stop=False)
                        if kind == "fox":
                            pair = slice(32 * h, 32 * h + 2)
                            pe.matmul(to[:, 0:width], FCQ[pair, j * P:(j + 1) * P], FCK[pair, 0:width],
                                      start=False, stop=False)
                        mm = pe.matmul(to[:, j * P:width], ident, CON[:, C_CAUSAL:C_CAUSAL + P],
                                       start=False, stop=True)
                    mm.then_inc(at_scores, 1)

                def turn(i):
                    h, j, kind = STEPS[i]
                    pe.wait_ge(at_probs, L * NS + (i + 1))
                    pe.wait_ge(at_copied, L * NS + (i + 1))
                    to = bank[4 + i % 2]
                    if kind == "cmp":
                        mm = pe.transpose(to[0:NC, 0:P], APR[i % 2][:, 0:NC], ident)
                    else:
                        for t in range(j + 1):
                            mm = pe.transpose(to[:, t * P:(t + 1) * P], APR[i % 2][:, t * P:(t + 1) * P], ident)
                    mm.then_inc(at_turned, 1)

                def values(i):
                    h, j, kind = STEPS[i]
                    rows = slice(64 * (h % 2), 64 * (h % 2) + 64)
                    if j == 0 and kind in ("cmp", "fox"):
                        pe.wait_ge(at_out, L * 8 + (2 * h + (kind == "fox") + 1))
                    pe.wait_ge(at_copied, L * NS + (i + 3))
                    pt = APT[i % 2]
                    to = bank[7 if kind == "fox" else 6][rows, j * P:(j + 1) * P]
                    if kind == "cmp":
                        mm = pe.matmul(to, VC[0:NC, :], pt[0:NC, 0:P], start=True, stop=False)
                    else:
                        for t in range(j + 1):
                            if kind == "fox":
                                v = FV[:, h // 2, t * P + 64 * (h % 2):t * P + 64 * (h % 2) + 64]
                            else:
                                o = t * P + (64 if kind == "win" else 0)
                                v = VSW[:, o:o + 64]
                            mm = pe.matmul(to, v, pt[:, t * P:(t + 1) * P], start=(kind == "fox" and t == 0),
                                           stop=(kind != "slc" and t == j))
                    mm.then_inc(at_pv, 1)

                for i in range(NS + 2):
                    if i < NS:
                        score(i)
                    for n, half in filler(i):
                        gemm(pe, q0 + (5 + n // 4), n % 4, H_HI, H_LO,
                                   part=range(half * KT // 2, (half + 1) * KT // 2))
                    if 1 <= i <= NS:
                        turn(i - 1)
                    if i >= 2:
                        values(i - 2)

                for n in range(FILL, 40):
                    gemm(pe, q0 + (5 + n // 4), n % 4, H_HI, H_LO)
                pe.wait_ge(evac_done[3], q0 + 15)
                pe.wait_ge(lo_ready, SL * L + (S_L2 + S_OBR + KT))
                for ob in range(KT):
                    s, quad = ob % 4, q0 + (15 + ob // 4)
                    pe.wait_ge(w_lo[s], quad + 1)
                    bank_free(pe, quad, s)
                    w_h, w_l = W_MAIN[0][s % 2], W_MAIN[1][s % 2]
                    for i in range(NBR):
                        for k in (2 * i, 2 * i + 1):
                            to = bank[4 * (ob % 2) + i][:, :]
                            pe.matmul(to, w_h[:, k, :], OBR_HI[:, k, :], start=(k == 2 * i), stop=False)
                            pe.matmul(to, w_h[:, k, :], OBR_LO[:, k, :], start=False, stop=False)
                            mm = pe.matmul(to, w_l[:, k, :], OBR_HI[:, k, :], start=False,
                                           stop=(k == 2 * i + 1))
                    mm.then_inc(mm_done[s], 1)
                both(pe, q0 + 17, ACC_HI, ACC_LO, SL * L + (S_L2 + S_ACC), norm=L + 8)
            norm_spread(pe, 9)

        @block.scalar
        def _(act):
            act.dma_start(VEC[:, :], vecs).then_inc(consts_in, 16)
            act.dma_start(CON[:, :], consts).then_inc(consts_in, 16)
            for c in (0, 2):
                act.dma_start(X[:, 2 * c:2 * c + 2, :], x_in[:, 2 * c:2 * c + 2, :]).then_inc(x_loaded[c], 16)
            act.dma_start(TAB[:, :], rope1).then_inc(rope1_in, 16)
            act.sem_inc(da_exp, 1)
            act.sem_inc(da_copied, 1)
            act.sem_inc(da_out, 1)
            act.sem_inc(at_exp, 2)
            act.sem_inc(at_copied, 2)
            act.sem_inc(at_out, 2)
            for k in range(KT):
                act.wait_ge(x_loaded[k // 2], 16)
                act.activation(SQ[:, k, :], X[:, k, :], ACT.Square).then_inc(sq_ready, 1)
            weight_hi(act, Q_U, 0, W_HEADS)
            weight_hi(act, Q_U, 1, W_HEADS)
            act.wait_ge(consts_in, 32)
            act.activation(PREP[:, 1, :], vec(V_LDT, PAIRS), ACT.Exp).then_inc(prep_dt, 1)
            act.wait_ge(lam_sum, 1)
            act.activation(LAME, bank[5][:, 0:2], ACT.Exp).then_inc(lam_exp, 1)
            for k in range(KT):
                round_hi(act, S_H0, k, H1_HI[:, k, :], X[:, k, :])
            for blk in range(KT):
                if blk == 1:
                    act.wait_ge(prep_arg, 1)
                    act.activation(RADIUS, PREP[:, 2, :], ACT.Exp).then_inc(prep_exp, 1)
                    act.wait_ge(prep_arg, 2)
                    act.activation(PREP[:, 5, :], PREP[:, 3, :], ACT.Sin)
                    act.activation(PREP[:, 6, :], PREP[:, 4, :], ACT.Sin).then_inc(prep_sin, 1)
                ahead(act, Q_U + blk // 4, blk % 4, W_HEADS)
                copy_out(act, Q_U + blk // 4, blk % 4, U[:, blk, :])

            def gate_b(blk):
                s = blk % 4
                act.wait_ge(mm_done[s], Q_GB + blk // 4 + 1)
                act.activation(RB[:, 8 + blk, :], bank[s % 2][:, :], ACT.Identity,
                               bias=column(V_BGATE + 8 + blk)).then_inc(evac_done[s], 1)

            def head_evac(hd, s):
                if s < 3:
                    ahead(act, hd + Q_HEAD, s, W_HEADS)
                act.wait_ge(mm_done[s], hd + (Q_HEAD + 1))
                if s < 2:
                    raw, swapped = ((QRAW, QSW), (KRAW, KSW))[s]
                    scale = DH ** -0.5 if s == 0 else 1.0
                    if not isinstance(hd, int):
                        act.wait_ge(rope_done, hd)
                    for quarter in range(4):
                        other = quarter ^ 1
                        act.activation(swapped[32 * quarter:32 * quarter + 32, :],
                                       bank[s][32 * other:32 * other + 32, :], ACT.Copy, scale=scale)
                    act.activation(raw, bank[s][:, :], ACT.Copy, scale=scale).then_inc(evac_done[s], 1)
                elif s == 2:
                    act.activation(one(RB, hd), bank[0][:, :], ACT.Identity,
                                   bias=column(hd + V_BGATE)).then_inc(evac_done[s], 1)
                else:
                    act.wait_ge(hv_turned, hd + 1)
                    act.activation(VH, bank[1][:, :], ACT.Copy).then_inc(evac_done[s], 1)

            def head_values(hd, dst=VT_H):
                ahead(act, hd + Q_HEAD, 3, W_HEADS)
                act.wait_ge(mm_done[3], hd + (Q_HEAD + 1))
                act.activation(dst, bank[1][:, :], ACT.Copy).then_inc(hv_ready, 1)

            for s in range(4):
                if s == 3:
                    head_values(0, PR[0])
                head_evac(0, s)
            act.wait_ge(prep_done, 1)
            act.wait_ge(cl_zero, 1)

            def da_exponent(b, j, c):
                act.wait_ge(da_max, 8 * b + 2 * j + c + 1)
                at = 2 * (j % 2) + c
                act.activation(PR[c][:, 0:(j + 1) * P], bank[5][:, 0:(j + 1) * P], ACT.Exp,
                               bias=NMAX[:, at:at + 1], accum_out=RSUM[:, at:at + 1]).then_inc(da_exp, 1)

            def da_copy(b, j):
                act.wait_ge(da_turned, 4 * b + j + 2)
                act.wait_ge(da_pv, 4 * b + j + 1)
                act.activation(PTB[j % 2][:, 0:(j + 1) * P], bank[6][:, 0:(j + 1) * P], ACT.Copy).then_inc(da_copied, 1)

            def head_body(b, last):
                for q in range(PPB):
                    act.wait_ge(y_done, 4 * b + q + 1)
                    act.activation(CL[q][:, :, 32 * q:32 * q + 32],
                                   CT[:, 4 * b + q, :, :] if isinstance(b, int) else
                                   CT[:, bass.ds(4 * b + q, 1), :, :].rearrange("p a c m -> p (a c) m"),
                                   ACT.Copy).then_inc(cl_ready, 1)
                    da_exponent(b, q, 0)
                    if last and q % 2:
                        gate_b(q // 2)
                    if not last and q < 3:
                        head_evac(b + 1, q)
                    if not last and q == 3:
                        head_values(b + 1)
                    da_exponent(b, q, 1)
                    if q:
                        da_copy(b, q - 1)
                da_copy(b, 3)
                act.wait_ge(da_pv, 4 * b + 6)
                act.activation(one(YA, b), bank[7][:, :], ACT.Copy).then_inc(da_out, 1)
                if not last:
                    head_evac(b + 1, 3)

            act.sem_inc(da_turned, 1)
            heads(act, head_body)

            act.wait_ge(rope_done, HEADS)
            act.wait_ge(da_scores, 8 * HEADS)
            weight_hi(act, Q_GB, 2)
            weight_hi(act, Q_GB, 3)
            act.wait_ge(y_used, KT + 1)
            for k in range(KT):
                if k == 4:
                    ahead(act, Q_GB, 2)
                    gate_b(2)
                act.activation(YSG_HI[:, k, :], U[:, k, :], ACT.Gelu_apprx_tanh).then_inc(hi_ready, 1)
                act.activation(U[:, k, :], U[:, k, :], ACT.Gelu_apprx_tanh).then_inc(t_ready, 1)
            act.drain()
            for h in range(HEADS):
                op = act.activation(SQ[:, h, :], YA[:, h, :], ACT.Square)
            op.then_inc(hsq_ready, 1)
            ahead(act, Q_GB, 3)
            gate_b(3)
            act.wait_ge(mem_loaded, 16)
            squares(act, MEMRAW, MEM, MSQ)
            for blk in range(4, KT):
                ahead(act, Q_GB + 1, blk % 4)
                gate_b(blk)
            act.drain()
            for blk in range(KT):
                s = blk % 4
                if blk < 4:
                    for h in (2 * s, 2 * s + 1):
                        round_hi(act, S_YA, h, YA_HI[:, h, :], YA[:, h, :])
                if blk == 4:
                    for k in range(KT):
                        round_hi(act, S_MEMN, k, MEMN_HI[:, k, :], MEMN[:, k, :])
                ahead(act, Q_GLU + blk // 4, s)
                act.wait_ge(mm_done[s], Q_GLU + blk // 4 + 1)
                if blk >= 2:
                    act.wait_ge(ys_ready, blk - 1)
                act.activation(PAIR[blk % 2], bank[s % 2][:, :], ACT.Sigmoid,
                               bias=column(V_BGLU + blk)).then_inc(evac_done[s], 1)
                if blk >= 4:
                    act.activation(R[:, 4 * s * T:4 * (s + 1) * T], R[:, 4 * s * T:4 * (s + 1) * T],
                                   ACT.Sigmoid).then_inc(gates_done, 1)
            for k in range(KT):
                round_hi(act, S_YS2, k, YS2_HI[:, k, :], YS2[:, k, :])
            for blk in range(KT):
                ahead(act, Q_DA + blk // 4, blk % 4)
            for blk in range(KT + 1):
                if blk < KT:
                    ahead(act, Q_SSM + blk // 4, blk % 4)
                if blk:
                    round_hi(act, S_MG, blk - 1, MG_HI[:, blk - 1, :], MG[:, blk - 1, :])

            def store_values(n, src, dst):
                act.wait_ge(v_turned, n + 1)
                act.activation(dst, src, ACT.Copy).then_inc(v_used, 1)

            def store_and_square(quad, s, blk):
                ahead(act, quad, s)
                act.wait_ge(mm_done[s], quad + 1)
                act.activation(SQ[:, blk, :], bank[s % 2][:, :], ACT.Square).then_inc(sq_ready, 1)
                act.activation(YB[:, blk, :], bank[s % 2][:, :], ACT.Copy).then_inc(evac_done[s], 1)

            for blk in range(KT):
                store_and_square(Q_MIX + blk // 4, blk % 4, blk)
            for blk in range(KT):
                ahead(act, Q_KX + blk // 4, blk % 4)
                copy_out(act, Q_KX + blk // 4, blk % 4, KX[:, blk, :])
            for n in range(KT + 1):
                if n == 4:
                    squares_of_sum(act, 1)
                if n < KT:
                    if n >= 2:
                        act.wait_ge(v_turned, n - 1)
                    ahead(act, Q_VX + n // 4, n % 4)
                    copy_out(act, Q_VX + n // 4, n % 4, VT_X[n % 2][:, 0:MEM])
                if n:
                    store_values(n - 1, bank[2 + (n - 1) % 2][:, 0:2 * P].rearrange("p (t n) -> p t n", t=2),
                                 VX[:, :, (n - 1) * P:n * P])
            for k in range(KT):
                round_hi(act, S_HX, k, HX_HI[:, k, :], HX[:, k, :])
            for blk in range(KT):
                ahead(act, Q_XQ + blk // 4, blk % 4)
                copy_out(act, Q_XQ + blk // 4, blk % 4, QX[:, blk, :], XD ** -0.5)

            def xa_exponent(i):
                act.wait_ge(xa_max, i + 1)
                if i >= 2:
                    act.wait_ge(xa_turned, i - 1)
                at = i % 2
                act.activation(APR[at][:, 0:MEM], bank[2 + at][:, 0:MEM], ACT.Exp, bias=NMAX[:, at:at + 1],
                               accum_out=RSUM[:, at:at + 1]).then_inc(xa_exp, 1)

            def xa_copy(i):
                act.wait_ge(xa_turned, i + 1)
                if i >= 2:
                    act.wait_ge(xa_pv, i - 1)
                act.activation(APT[i % 2][:, 0:MEM], bank[4 + i % 2][:, 0:MEM], ACT.Copy).then_inc(xa_copied, 1)

            def xa_round(h):
                act.wait_ge(xa_pv, TT * (h + 1))
                for e in range(2):
                    act.activation(OX_HI[:, 2 * h + e, :], bank[6 + e][:, :], ACT.Copy).then_inc(hi_ready, 1)

            act.sem_inc(t_ready, KT)
            for i in range(XH * TT + 3):
                if i < XH * TT:
                    xa_exponent(i)
                if i >= 3 and (i - 3) % TT == TT - 1:
                    xa_round((i - 3) // TT)
                if 1 <= i <= XH * TT:
                    xa_copy(i - 1)
            for blk in range(KT):
                store_and_square(Q_XO + blk // 4, blk % 4, blk)
            act.wait_ge(ms_ready, 5)
            squares_of_sum(act, 2)
            for k in range(KT):
                round_hi(act, S_HF, k, H_HI[:, k, :], H[:, k, :])

            def ff_block(c, quad, i, s):
                ahead(act, quad, s)
                act.wait_ge(ff_lo, 4 * i + (KT * c + s + 1))
                act.wait_ge(mm_done[s], quad + 1)
                act.activation(RELU[s % 2], bank[s % 2][:, :], ACT.Relu).then_inc(evac_done[s], 1)
                act.drain()
                act.activation(one(F_HI[c % 2], 4 * i + s), RELU[s % 2], ACT.Square).then_inc(ff_hi, 1)

            for step, (which, c) in enumerate(FF_ORDER[:-1]):
                with act.Fori(0, 2) as i:
                    for s in range(4):
                        if which == 1:
                            ff_block(c, i + (Q_FF + 2 * step), i, s)
                        else:
                            ahead(act, i + (Q_FF + 2 * step), s)
            act.wait_ge(ms_ready, 6)
            for blk in range(KT):
                s, quad = blk % 4, Q_L2 - 2 + blk // 4
                if blk < KT - 2:
                    ahead(act, quad, s)
                act.wait_ge(evac_done[s], quad + 1)
                act.activation(SQ[:, blk, :], YF[:, blk, :], ACT.Square).then_inc(sq_ready, 1)
            act.wait_ge(ms_ready, 7)
            squares_of_sum(act, 3)

            with act.Fori(0, LAYERS) as L:
                q0 = act.snap(QL * L + Q_L2)
                stages = act.snap(SL * L + S_L2)
                def layer(ap):
                    return ap[bass.ds(L, 1)].rearrange("a p n -> (a p) n")
                act.wait_ge(x_ready, L * KT + 3 * KT)
                act.dma_start(LVEC[:, :], layer(lvecs)).then_inc(lvec_in, 16)
                for dst, src in ((W2K, cmp_w2k), (W2V, cmp_w2v), (B2V, cmp_b2v), (POS, cmp_pos), (LW[:, 288:544], pool_w)):
                    act.dma_start(dst, layer(src)).then_inc(lw_in, 16)
                act.dma_start(R[:, 24 * T:32 * T], layer(cmp_w1)).then_inc(w1_in, 16)
                weight_hi(act, q0, 0)
                weight_hi(act, q0, 1)
                act.wait_ge(lvec_in, 16 * L + 16)
                for k in range(KT):
                    round_hi(act, stages + S_H, k, H_HI[:, k, :], H[:, k, :])

                def store(quad, s, dst, scale=1.0):
                    ahead(act, quad, s)
                    copy_out(act, quad, s, dst, scale)

                store(q0, 0, RAW[:, 0, :], 64 ** -0.5)
                store(q0, 1, RAW[:, 1, :], 64 ** -0.5)
                store(q0, 2, RAW[:, 2, :])
                store(q0, 3, KCVC)
                store(q0 + 1, 0, VT[0])
                ahead(act, q0 + 1, 1)
                act.wait_ge(mm_done[1], q0 + 2)
                act.activation(FZ, bank[1][:, :], ACT.Identity,
                               bias=LVEC[:, L_FBIAS:L_FBIAS + 1]).then_inc(evac_done[1], 1)
                act.drain()
                act.activation(FL, FZ, ACT.Abs)
                act.drain()
                act.activation(FL, FL, ACT.Exp, scale=-1.0)
                act.drain()
                act.activation(FL, FL, ACT.Ln, bias=1.0)
                store_values(L * 3 + KT, bank[6][:, :], VSW)
                store(q0 + 1, 2, FQ[:, 0, :], 64 ** -0.5)
                act.wait_ge(g_turned, L + 1)
                act.activation(G12[:, :, 0:12], bank[4][:, :].rearrange("p (t g) -> p t g", t=TT)[:, :, 2:14],
                               ACT.Sigmoid).then_inc(f_log, 1)
                store(q0 + 1, 3, FQ[:, 1, :], 64 ** -0.5)
                store(q0 + 2, 0, FK[:, 0, :])
                store(q0 + 2, 1, FK[:, 1, :])
                store(q0 + 2, 2, VT[1])
                store(q0 + 2, 3, VT[0])
                store_values(L * 3 + (KT + 1), bank[7][:, :], FV[:, 0, :])
                for i in range(2):
                    for s in range(4):
                        store(q0 + (3 + i), s, RB[:, 4 * i + s, :])
                        if i == 0 and s == 0:
                            store_values(L * 3 + (KT + 2), bank[6][:, :], FV[:, 1, :])
                    if i == 0:
                        act.wait_ge(hid_mm, L + 1)
                        for c in range(2):
                            op = act.activation(HID[:, 32 * c:32 * c + NC], bank[6][:, NC * c:NC * c + NC], ACT.Silu,
                                                bias=LVEC[:, L_B1 + c:L_B1 + c + 1])
                        op.then_inc(hid_ready, 1)
                act.wait_ge(kv2_mm, L + 1)
                act.activation(VC[0:NC, :], bank[6][0:NC, 128:192], ACT.Copy)
                act.activation(KCR, bank[6][:, 64:64 + NC], ACT.Identity,
                               bias=LVEC[:, L_B2K:L_B2K + 1]).then_inc(kcr_ready, 1)
                act.wait_ge(pool_mm, L + 1)
                for c in range(2):
                    op = act.activation(OBR[:, 2 + c, :], bank[2 + c][:, :], ACT.Copy,
                                        scale=LVEC[:, L_POOL + c:L_POOL + c + 1])
                op.then_inc(pool_out, 1)

                def exponent(i):
                    h, j, kind = STEPS[i]
                    width = NC if kind == "cmp" else (j + 1) * P
                    act.wait_ge(at_max, L * NS + (i + 1))
                    act.wait_ge(at_turned, L * NS + (i + 1))
                    at = i % 2
                    act.activation(APR[at][:, 0:width], bank[2 + at][:, 0:width], ACT.Exp, bias=NMAX[:, at:at + 1],
                                   accum_out=RSUM[:, at:at + 1]).then_inc(at_exp, 1)

                def turned_copy(i):
                    h, j, kind = STEPS[i]
                    act.wait_ge(at_turned, L * NS + (i + 3))
                    act.wait_ge(at_pv, L * NS + (i + 1))
                    if kind == "cmp":
                        act.activation(APT[i % 2][0:NC, 0:P], bank[4 + i % 2][0:NC, 0:P], ACT.Copy).then_inc(at_copied, 1)
                    else:
                        width = (j + 1) * P
                        act.activation(APT[i % 2][:, 0:width], bank[4 + i % 2][:, 0:width], ACT.Copy).then_inc(at_copied, 1)

                def head_out(h):
                    rows = slice(64 * (h % 2), 64 * (h % 2) + 64)
                    act.wait_ge(at_pv, L * NS + (16 * (h + 1) + 2))
                    act.activation(OBR[rows, h // 2, :], bank[6][rows, :], ACT.Copy).then_inc(at_out, 1)
                    act.activation(OBR[rows, 6 + h // 2, :], bank[7][rows, :], ACT.Copy).then_inc(at_out, 1)

                for i in range(NS + 3):
                    if i < NS:
                        exponent(i)
                    for n in [n for n, half in filler(i) if half == 1]:
                        if n == 8:
                            act.wait_ge(conv_out, L + 1)
                        store(q0 + (5 + n // 4), n % 4, U[:, n, :] if n < 8 else ML[n // 4 - 2][:, n % 4, :])
                    if 1 <= i <= NS:
                        turned_copy(i - 1)
                    if i >= 3 and (i - 3) % 16 == 15:
                        head_out((i - 3) // 16)
                act.drain()
                for i in range(2):
                    act.activation(U_[:, 4 * i * T:4 * (i + 1) * T], U_[:, 4 * i * T:4 * (i + 1) * T],
                                   ACT.Silu).then_inc(silu_done, 1)
                for n in range(FILL, 40):
                    s, quad = n % 4, q0 + (5 + n // 4)
                    ahead(act, quad, s)
                    act.wait_ge(mm_done[s], quad + 1)
                    act.activation(ML[n // 4 - 2][:, s, :], bank[s % 2][:, :], ACT.Sigmoid).then_inc(evac_done[s], 1)
                    m = n - FILL
                    for k in (2 * m, 2 * m + 1) if m < 4 else ():
                        round_hi(act, stages + S_OBR, k, OBR_HI[:, k, :], OBR[:, k, :])
                    if m >= 2:
                        group = ML[m - 2]
                        act.activation(group, group, ACT.Sigmoid).then_inc(sig_ready, 1)
                for ob in range(KT + 1):
                    if ob < KT:
                        ahead(act, q0 + (15 + ob // 4), ob % 4)
                    if ob:
                        round_hi(act, stages + S_ACC, ob - 1, ACC_HI[:, ob - 1, :], ACC[:, ob - 1, :])
                act.wait_ge(ms_ready, L + 8)
                for blk in range(KT):
                    s, quad = blk % 4, q0 + (17 + blk // 4)
                    if blk < KT - 2:
                        ahead(act, quad, s)
                    act.wait_ge(evac_done[s], quad + 1)
                    act.activation(SQ[:, blk, :], X[:, blk, :], ACT.Square).then_inc(sq_ready, 1)

        @block.vector
        def _(dve):
            dve.memset(SMALL[:, 0:4], 1.0)
            dve.memset(HALF, -0.5)
            dve.memset(ONE_ROW, 1.0)
            dve.drain()
            dve.sem_inc(bu_used, 1)
            dve.sem_inc(ss_ready, 2)
            dve.sem_inc(y_used, 1)
            dve.sem_inc(ff_lo, 2)
            dve.wait_ge(consts_in, 32)
            dve.sem_inc(const_ready, 1)
            norm_mean(dve, 0)

            dve.tensor_tensor(LAMP[:, 0:1], vec(V_LQ1, 1), vec(V_LK1, 1), ALU.mult)
            dve.tensor_tensor(LAMP[:, 1:2], vec(V_LQ2, 1), vec(V_LK2, 1), ALU.mult).then_inc(lam_prod, 1)
            dve.tensor_scalar(HN08, vec(V_HEADNORM, 1), 1.0 - LAM_INIT, None, ALU.mult)
            norm_split(dve, 0, S_H0, X, H1_HI, H1_LO, X, vec(V_MIX_PRE))
            dve.wait_ge(lam_exp, 1)
            dve.tensor_tensor(NLAM, LAME[:, 1:2], LAME[:, 0:1], ALU.subtract)
            dve.drain()
            dve.tensor_scalar(NLAM, NLAM, LAM_INIT, None, ALU.subtract)

            DT, RE, ARG, ARGC, SN, CS = (PREP[:, i, :] for i in range(1, 7))
            A, B, C, E, F, G, I, J = (PREP[:, i, :] for i in range(8, 16))
            lre, lim = vec(V_LRE, PAIRS), vec(V_LIM, PAIRS)

            def seq(*ops):
                for op in ops:
                    op()
                dve.drain()

            def tt(o, a, b, op):
                return lambda: dve.tensor_tensor(o, a, b, op)

            def ts(o, a, x, y, op0, op1=None):
                if op1 is None:
                    return lambda: dve.tensor_scalar(o, a, x, None, op0)
                return lambda: dve.tensor_scalar(o, a, x, y, op0, op1)

            def stt(o, a, x, b, op0, op1):
                return lambda: dve.scalar_tensor_tensor(o, a, x, b, op0, op1)

            dve.wait_ge(prep_dt, 1)
            dve.tensor_tensor(RE, lre, DT, ALU.mult).then_inc(prep_arg, 1)
            seq(tt(A, lim, DT, ALU.mult))
            turns = 1.5 * 2.0 ** 23
            two_pi = 2 * np.pi
            c1 = 6.28125
            c2 = float(np.float32(np.round((two_pi - c1) * 2.0 ** 22) / 2.0 ** 22))
            c3 = two_pi - c1 - c2
            pi32 = 3.1415925
            seq(ts(B, A, 1 / two_pi, turns, ALU.mult, ALU.add))
            seq(ts(B, B, turns, None, ALU.subtract))
            seq(stt(A, B, -c1, A, ALU.mult, ALU.add))
            seq(stt(A, B, -c2, A, ALU.mult, ALU.add))
            seq(stt(A, B, -c3, A, ALU.mult, ALU.add))
            seq(ts(ARG, A, pi32, -pi32, ALU.min, ALU.max), ts(C, A, np.pi / 2, None, ALU.add))
            seq(ts(E, C, pi32, -two_pi, ALU.is_gt, ALU.mult))
            seq(tt(C, C, E, ALU.add))
            dve.tensor_scalar(ARGC, C, pi32, -pi32, ALU.min, ALU.max).then_inc(prep_arg, 1)
            dve.wait_ge(prep_sin, 1)
            dve.wait_ge(prep_exp, 1)
            for table in (LOT, HIT):
                seq(lambda: dve.memset(table[:, :, 0, 0:1], 1.0), lambda: dve.memset(table[:, :, 1, 0:1], 0.0))
                size, n = table.shape[-1], 1
                while n < size:
                    w = [x.rearrange("p (n a) -> p n a", a=1).to_broadcast([P, PAIRS, n]) for x in (CS, SN)]
                    t = [W.rearrange("p (n a) -> p n a", n=PAIRS)[:, :, 0:n] for W in TMP[0:4]]
                    re, im = table[:, :, 0, 0:n], table[:, :, 1, 0:n]
                    seq(tt(t[0], re, w[0], ALU.mult), tt(t[1], im, w[1], ALU.mult),
                        tt(t[2], im, w[0], ALU.mult), tt(t[3], re, w[1], ALU.mult),
                        tt(E, CS, CS, ALU.mult), tt(F, SN, SN, ALU.mult), tt(G, CS, SN, ALU.mult))
                    if n == 1 and table is LOT:
                        seq(tt(A, RADIUS, CS, ALU.mult), tt(B, RADIUS, SN, ALU.mult))
                    seq(tt(table[:, :, 0, n:2 * n], t[0], t[1], ALU.subtract),
                        tt(table[:, :, 1, n:2 * n], t[2], t[3], ALU.add),
                        tt(CS, E, F, ALU.subtract), ts(SN, G, 2.0, None, ALU.mult))
                    n *= 2
            seq(ts(A, A, 1.0, None, ALU.subtract), tt(C, lre, lre, ALU.mult), tt(E, lim, lim, ALU.mult))
            seq(tt(C, C, E, ALU.add), tt(G, A, lre, ALU.mult), tt(F, B, lim, ALU.mult))
            seq(lambda: dve.reciprocal(C, C), tt(E, G, F, ALU.add), tt(I, B, lre, ALU.mult), tt(J, A, lim, ALU.mult))
            seq(tt(F, I, J, ALU.subtract))
            seq(tt(E, E, C, ALU.mult), tt(F, F, C, ALU.mult))
            dve.wait_ge(ct_in, 16)
            er, ei = [x.rearrange("p (n a) -> p n a", a=1).to_broadcast([P, PAIRS, 32]) for x in (E, F)]
            t = [R3[:, 1024 * i:1024 * i + 1024].rearrange("p (n m) -> p n m", n=PAIRS) for i in range(4)]
            seq(tt(t[0], CT[:, :, 0, :], er, ALU.mult), tt(t[1], CT[:, :, 1, :], ei, ALU.mult),
                tt(t[2], CT[:, :, 0, :], ei, ALU.mult), tt(t[3], CT[:, :, 1, :], er, ALU.mult))
            seq(tt(CT[:, :, 0, :], t[0], t[1], ALU.subtract), stt(CT[:, :, 1, :], t[2], -1.0, t[3], ALU.mult, ALU.subtract))
            dve.sem_inc(prep_done, 1)

            def da_row_max(b, j, c):
                dve.wait_ge(da_scores, 8 * b + 2 * j + c + 1)
                at = 2 * (j % 2) + c
                dve.tensor_reduce(NMAX[:, at:at + 1], bank[5][:, 0:(j + 1) * P], AX.X, ALU.max,
                                  negate=True).then_inc(da_max, 1)

            def da_combine(b, j):
                dve.wait_ge(da_exp, 8 * b + 2 * j + 3)
                o, w = 2 * (j % 2), (j + 1) * P
                dve.reciprocal(RINV[:, 0:2], RSUM[:, o:o + 2])
                dve.drain()
                dve.tensor_scalar(PR[1][:, 0:w], PR[1][:, 0:w], RINV[:, 1:2], NLAM, ALU.mult, ALU.mult)
                dve.drain()
                dve.wait_ge(da_turned, 4 * b + j + 1)
                dve.scalar_tensor_tensor(PC[:, 0:w], PR[0][:, 0:w], RINV[:, 0:1], PR[1][:, 0:w],
                                         ALU.mult, ALU.add).then_inc(da_probs, 1)

            def s5_scan(b, q):
                n = 4 * b + q
                cs, sn = ROT[q % 2]
                rad = PREP[:, 0, n:n + 1] if isinstance(b, int) else PREP[:, 0, bass.ds(n, 1)]
                dve.wait_ge(tab_ready, n + 1)
                dve.wait_ge(bu_ready, n + 1)
                dve.tensor_tensor(TMP[0], bank[2][:, :], cs, ALU.mult)
                dve.tensor_tensor(TMP[1], bank[3][:, :], sn, ALU.mult)
                dve.tensor_tensor(TMP[2], bank[3][:, :], cs, ALU.mult)
                dve.tensor_tensor(TMP[3], bank[2][:, :], sn, ALU.mult).then_inc(bu_used, 1)
                dve.drain()
                dve.tensor_tensor(TMP[0], TMP[0], TMP[1], ALU.add)
                dve.tensor_tensor(TMP[2], TMP[2], TMP[3], ALU.subtract)
                dve.drain()
                dve.tensor_tensor_scan(TMP[1], rad.to_broadcast([P, T]), TMP[0], 0.0, ALU.mult, ALU.add)
                dve.tensor_tensor_scan(TMP[3], rad.to_broadcast([P, T]), TMP[2], 0.0, ALU.mult, ALU.add)
                dve.drain()

            def s5_turn_back(b, q):
                n = 4 * b + q
                cs, sn = ROT[q % 2]
                re, im = SS[q % 2]
                dve.wait_ge(y_done, n + 3)
                dve.tensor_tensor(re, TMP[1], cs, ALU.mult)
                dve.tensor_tensor(TMP[0], TMP[3], sn, ALU.mult)
                dve.tensor_tensor(im, TMP[3], cs, ALU.mult)
                dve.tensor_tensor(TMP[2], TMP[1], sn, ALU.mult)
                dve.drain()
                dve.tensor_tensor(re, re, TMP[0], ALU.subtract)
                dve.tensor_tensor(im, im, TMP[2], ALU.add).then_inc(ss_ready, 1)

            def head_body(b, last):
                for q in range(PPB):
                    da_row_max(b, q, 0)
                    s5_scan(b, q)
                    da_row_max(b, q, 1)
                    s5_turn_back(b, q)
                    da_combine(b, q)
                dve.wait_ge(y_done, 4 * b + 8)
                dve.scalar_tensor_tensor(one(U, b), one(U, b), column(b + V_SSMD), bank[4][:, :],
                                         ALU.mult, ALU.add).then_inc(y_used, 1)

            heads(dve, head_body)

            dve.wait_ge(da_turned, 4 * HEADS + 1)
            dve.drain()
            for k in range(KT):
                dve.wait_ge(t_ready, S_YSG + (k + 1))
                rest_lo(dve, S_YSG, k, YSG_LO[:, k, :], U[:, k, :], YSG_HI[:, k, :])
            dve.drain()
            dve.wait_ge(hms_ready, 1)
            dve.tensor_scalar(HVAR, bank[6][:, 0:32], 1.0 / P, EPS, ALU.mult, ALU.add).then_inc(hvar_ready, 1)

            def glu(blk):
                s = blk % 4
                dve.wait_ge(evac_done[s], Q_GLU + blk // 4 + 1)
                dve.tensor_tensor(U[:, blk, :], PAIR[blk % 2], U[:, blk, :], ALU.mult).then_inc(ys_ready, 1)

            norm_mean(dve, 1, 2)
            for s in range(4):
                for h in (2 * s, 2 * s + 1):
                    dve.wait_ge(hbc_ready, h + 1)
                    dve.scalar_tensor_tensor(YA[:, h, :], YA[:, h, :], HN08, bank[2 + h % 2][:, :],
                                             ALU.mult, ALU.mult).then_inc(t_ready, 1)
                for h in (2 * s, 2 * s + 1):
                    rest_lo(dve, S_YA, h, YA_LO[:, h, :], YA[:, h, :], YA_HI[:, h, :])
                glu(s)
            norm_split(dve, 1, S_MEMN, MEMN, MEMN_HI, MEMN_LO, MEMRAW, vec(V_MEM), MEM)
            for blk in range(4, KT):
                glu(blk)
            dve.drain()
            dve.sem_inc(t_ready, KT)
            for k in range(KT):
                rest_lo(dve, S_YS2, k, YS2_LO[:, k, :], YS2[:, k, :], YS2_HI[:, k, :])
            dve.wait_ge(gates_done, 4)
            for blk in range(KT):
                s = blk % 4
                dve.wait_ge(mm_done[s], Q_DA + blk // 4 + 1)
                dve.tensor_tensor(MG[:, blk, :], RB[:, 8 + blk, :], bank[s % 2][:, :], ALU.mult).then_inc(evac_done[s], 1)
            for blk in range(KT + 1):
                if blk < KT:
                    s = blk % 4
                    dve.wait_ge(mm_done[s], Q_SSM + blk // 4 + 1)
                    dve.tensor_tensor(PAIR[blk % 2], RB[:, blk, :], bank[s % 2][:, :], ALU.mult).then_inc(evac_done[s], 1)
                    dve.drain()
                    dve.tensor_tensor(MG[:, blk, :], MG[:, blk, :], PAIR[blk % 2], ALU.add).then_inc(t_ready, 1)
                if blk:
                    rest_lo(dve, S_MG, blk - 1, MG_LO[:, blk - 1, :], MG[:, blk - 1, :], MG_HI[:, blk - 1, :])
            norm_mean(dve, 2)
            dve.wait_ge(x_again, 16)
            for s in range(4):
                dve.wait_ge(evac_done[s], Q_MIX + 2)
            residual_add(dve, 2, YB, vec(V_MIX_POST))
            norm_mean(dve, 3)
            norm_split(dve, 3, S_HX, HX, HX_HI, HX_LO, X, vec(V_X_PRE))

            def xa_rest(h):
                for e in range(2):
                    rest_lo(dve, S_OX, 2 * h + e, OX_LO[:, 2 * h + e, :], bank[6 + e][:, :], OX_HI[:, 2 * h + e, :])

            for i in range(XH * TT + 1):
                if i >= 7 and (i - 7) % TT == 0:
                    xa_rest((i - 7) // TT)
                if i < XH * TT:
                    at = i % 2
                    dve.wait_ge(xa_scores, i + 1)
                    dve.tensor_reduce(NMAX[:, at:at + 1], bank[2 + at][:, 0:MEM], AX.X, ALU.max,
                                      negate=True).then_inc(xa_max, 1)
                if i:
                    at = (i - 1) % 2
                    dve.wait_ge(xa_exp, i)
                    dve.reciprocal(RINV[:, at:at + 1], RSUM[:, at:at + 1])
                    dve.drain()
                    dve.tensor_scalar(APR[at][:, 0:MEM], APR[at][:, 0:MEM], RINV[:, at:at + 1], None,
                                      ALU.mult).then_inc(xa_probs, 1)
            xa_rest(XH - 1)
            norm_mean(dve, 4)
            for s in range(4):
                dve.wait_ge(evac_done[s], Q_XO + 2)
            residual_add(dve, 4, YB, vec(V_X_POST))
            norm_mean(dve, 5)
            norm_split(dve, 5, S_HF, H, H_HI, H_LO, X, vec(V_FF_PRE))
            for step, (which, c) in enumerate(FF_ORDER):
                with dve.Fori(0, 2) as i:
                    for s in range(4):
                        if which == 1:
                            f_lo = one(F_LO[c % 2], 4 * i + s)
                            f = one(RB[:, 16 * (c % 2):16 * (c % 2) + 8, :], 4 * i + s)
                            dve.wait_ge(ff_hi, 4 * i + (KT * c + s + 1))
                            dve.tensor_tensor(f, RELU[s % 2], RELU[s % 2], ALU.mult)
                            dve.drain()
                            dve.tensor_tensor(f_lo, f, one(F_HI[c % 2], 4 * i + s).bitcast(F32),
                                              ALU.subtract).then_inc(ff_lo, 1)
                        else:
                            y = one(YF, 4 * i + s)
                            dve.drain()
                            dve.wait_ge(mm_done[s], i + (Q_FF + 2 * step + 1))
                            if c == 0:
                                op = dve.tensor_copy(y, bank[s % 2][:, :])
                            else:
                                op = dve.tensor_tensor(y, y, bank[s % 2][:, :], ALU.add)
                            op.then_inc(evac_done[s], 1)
            norm_mean(dve, 6)
            residual_add(dve, 6, YF, vec(V_FF_POST))

            with dve.Fori(0, LAYERS) as L:
                q0 = dve.snap(QL * L + Q_L2)
                stages = dve.snap(SL * L + S_L2)
                norm_mean(dve, L + 7)
                dve.wait_ge(lvec_in, 16 * L + 16)
                norm_split(dve, L + 7, stages + S_H, H, H_HI, H_LO, X, LVEC[:, L_NORM:L_NORM + KT])
                dve.memset(PA[:, 0:16], 0.0)
                dve.memset(PB[:, 0:16], 0.0)
                dve.memset(CP[:, 0:2], 0.0)
                for a in range(2):
                    dve.memset(FLAT[a], 0.0)
                dve.drain()
                dve.wait_ge(evac_done[3], q0 + 1)
                dve.wait_ge(lw_in, 16 * 5 * L + 80)
                kv = KCVC.rearrange("p (m b) -> p b m", b=16)
                for a in range(2):
                    pos = POS[:, 16 * a:16 * a + 16].rearrange("p (l n) -> p l n", n=1).to_broadcast([P, 16, NC])
                    for c in range(2):
                        rows = slice(64 * c, 64 * c + 64)
                        op = dve.tensor_tensor(FLAT[a][rows, :, NC * c:NC * c + NC], kv[rows, :, a:a + NC],
                                               pos[rows, :, :], ALU.add)
                op.then_inc(flat_ready, 1)
                dve.wait_ge(sw_ready, L + 1)
                dve.wait_ge(rope2_in, 16)
                for i in range(3):
                    dve.tensor_tensor(RTMP[:, i, :], RAW[:, i, :], COS, ALU.mult)
                dve.drain()
                for i in range(3):
                    op = dve.tensor_tensor(RAW[:, i, :], bank[(2, 3, 5)[i]][:, :], SIN, ALU.mult)
                op.then_inc(sw_used, 1)
                dve.drain()
                for i in range(2):
                    dve.tensor_tensor(NQ[:, i, :], RTMP[:, i, :], RAW[:, i, :], ALU.add)
                for dst, src in ((KS, 0), (KW, 64)):
                    for half in (0, 64):
                        op = dve.tensor_tensor(dst[half:half + 64, :], RTMP[src:src + 64, 2, :], RAW[src:src + 64, 2, :],
                                               ALU.add)
                op.then_inc(nq_ready, 1)
                dve.wait_ge(f_log, L + 1)
                dve.scalar_tensor_tensor(FZ, FZ, 0.0, FL, ALU.min, ALU.subtract)
                dve.drain()
                dve.tensor_tensor_scan(FL, ones.to_broadcast([P, T]), FZ, 0.0, ALU.mult, ALU.add)
                dve.drain()
                dve.tensor_scalar(FCQ, FL, CON[:, C_FQ:C_FQ + 1], CON[:, C_FK:C_FK + 1], ALU.mult, ALU.add)
                dve.tensor_scalar(FCK, FL, CON[:, C_NFK:C_NFK + 1], CON[:, C_FQ:C_FQ + 1], ALU.mult,
                                  ALU.add)
                dve.tensor_tensor(G12[:, :, 0:NH], G12[:, :, 0:NH],
                                  CON[:, C_VALID:C_VALID + TT].rearrange("p (t g) -> p t g", g=1)
                                  .to_broadcast([P, TT, NH]), ALU.mult)
                dve.drain()
                dve.sem_inc(f_ready, 1)
                for i in range(2):
                    dve.wait_ge(evac_done[i], q0 + 4)
                dve.wait_ge(hid_mm, L + 1)
                for i in range(2):
                    u = PIN[:, i, :]
                    dve.tensor_copy(PA[:, 16:528], u)
                    dve.drain()
                    dve.tensor_tensor(PB[:, 16:528], PA[:, 16:528], PA[:, 15:527], ALU.add)
                    dve.drain()
                    if i == 0:
                        dve.tensor_tensor(PA[64:128, 16:528], PB[64:128, 16:528], PB[64:128, 14:526], ALU.add)
                    else:
                        dve.tensor_tensor(PA[:, 16:528], PB[:, 16:528], PB[:, 14:526], ALU.add)
                        dve.drain()
                        dve.tensor_tensor(PB[:, 16:528], PA[:, 16:528], PA[:, 12:524], ALU.add)
                        dve.drain()
                        dve.tensor_tensor(PA[64:128, 16:528], PB[64:128, 16:528], PB[64:128, 8:520], ALU.add)
                    dve.drain()
                    for rows, s in ((slice(0, 64), PB), (slice(64, 128), PA)):
                        dve.scalar_tensor_tensor(RB[rows, 16 + i, 16:T], s[rows, 32:528], CON[rows, C_W + i:C_W + i + 1],
                                                 u[rows, 16:T], ALU.mult, ALU.subtract)
                        dve.tensor_tensor(s[rows, 16:32], s[rows, 16:32], CON[rows, C_INV + 16 * i:C_INV + 16 * i + 16],
                                          ALU.mult)
                    dve.drain()
                    for rows, s in ((slice(0, 64), PB), (slice(64, 128), PA)):
                        dve.tensor_tensor(RB[rows, 16 + i, 0:16], s[rows, 16:32], u[rows, 0:16], ALU.subtract)
                    dve.drain()
                dve.sem_inc(pooled_ready, 1)
                dve.wait_ge(kcs_mm, L + 1)
                ends = slice(CMP_LEN - 1, T, CMP_STRIDE)
                dve.tensor_tensor(KCT[:, 0:NC], KCR, COS[:, ends], ALU.mult)
                dve.tensor_tensor(KCT[:, 32:32 + NC], bank[6][:, 96:96 + NC], SIN[:, ends], ALU.mult)
                dve.drain()
                dve.tensor_tensor(KC, KCT[:, 0:NC], KCT[:, 32:32 + NC], ALU.add).then_inc(kc_ready, 1)
                def convolve(i):
                    if i == 0:
                        for s in range(4):
                            dve.wait_ge(evac_done[s], q0 + 5)
                    dve.tensor_tensor(CP[:, 2:514], CC[:, i, :], CX[:, i, :], ALU.mult)
                    dve.drain()
                    for tap in range(3):
                        w = LVEC[:, L_CONV + 2 * tap + i:L_CONV + 2 * tap + i + 1]
                        if tap == 0:
                            dve.tensor_scalar(OBR[:, 4 + i, :], CP[:, 0:T], w, None, ALU.mult)
                        else:
                            dve.scalar_tensor_tensor(OBR[:, 4 + i, :], CP[:, tap:tap + T], w, OBR[:, 4 + i, :],
                                                     ALU.mult, ALU.add)
                        dve.drain()
                    dve.tensor_tensor(OBR[:, 4 + i, :], OBR[:, 4 + i, :], CB[:, i, :], ALU.mult)
                    dve.drain()
                    if i == 1:
                        dve.wait_ge(pool_mm, L + 1)
                        dve.sem_inc(conv_out, 1)

                for i in range(NS + 1):
                    if i in (4, 9):
                        convolve((4, 9).index(i))
                    if i < NS:
                        h, j, kind = STEPS[i]
                        width = NC if kind == "cmp" else (j + 1) * P
                        at = i % 2
                        dve.wait_ge(at_scores, L * NS + (i + 1))
                        dve.tensor_reduce(NMAX[:, at:at + 1], bank[2 + at][:, 0:width], AX.X, ALU.max,
                                          negate=True).then_inc(at_max, 1)
                    if i:
                        h, j, kind = STEPS[i - 1]
                        width = NC if kind == "cmp" else (j + 1) * P
                        at = (i - 1) % 2
                        dve.wait_ge(at_exp, L * NS + (i + 2))
                        dve.reciprocal(RINV[:, at:at + 1], RSUM[:, at:at + 1])
                        dve.drain()
                        pr = APR[at][:, 0:width]
                        if kind == "fox":
                            op = dve.tensor_scalar(pr, pr, RINV[:, at:at + 1], None, ALU.mult)
                        else:
                            g = NH * ("cmp", "slc", "win").index(kind) + h
                            op = dve.tensor_scalar(pr, pr, RINV[:, at:at + 1], G12[:, j, g:g + 1], ALU.mult, ALU.mult)
                        op.then_inc(at_probs, 1)
                dve.wait_ge(at_out, L * 8 + 10)
                for k in range(KT + 2):
                    if k < KT:
                        dve.wait_ge(silu_done, L * 2 + (k // 4 + 1))
                        dve.tensor_tensor(OBR[:, k, :], OBR[:, k, :], U[:, k, :], ALU.mult).then_inc(t_ready, 1)
                    if k >= 2:
                        rest_lo(dve, stages + S_OBR, k - 2, OBR_LO[:, k - 2, :], OBR[:, k - 2, :], OBR_HI[:, k - 2, :])
                for ob in range(KT + 1):
                    if ob < KT:
                        s, quad = ob % 4, q0 + (15 + ob // 4)
                        ml = ML[ob]
                        if ob < 6:
                            dve.wait_ge(sig_ready, L * 6 + (ob + 1))
                        else:
                            for i in range(4):
                                dve.wait_ge(evac_done[i], q0 + (8 + ob))
                        dve.wait_ge(mm_done[s], quad + 1)
                        for i in range(NBR):
                            op = dve.tensor_tensor(ml[:, i, :], ml[:, i, :], bank[4 * (ob % 2) + i][:, :], ALU.mult)
                        op.then_inc(evac_done[s], 1)
                        dve.drain()
                        dve.tensor_tensor(ml[:, 0:2, :], ml[:, 0:2, :], ml[:, 2:4, :], ALU.add)
                        dve.drain()
                        dve.tensor_tensor(ACC[:, ob, :], ml[:, 0, :], ml[:, 1, :], ALU.add).then_inc(t_ready, 1)
                    if ob:
                        rest_lo(dve, stages + S_ACC, ob - 1, ACC_LO[:, ob - 1, :], ACC[:, ob - 1, :], ACC_HI[:, ob - 1, :])
                for blk in range(KT):
                    s = blk % 4
                    dve.wait_ge(mm_done[s], q0 + (18 + blk // 4))
                    op = dve.tensor_tensor(X[:, blk, :], X[:, blk, :], bank[s % 2][:, :], ALU.add)
                    op.then_inc(evac_done[s], 1)
                dve.drain()
                dve.sem_inc(x_ready, KT)
            norm_mean(dve, 9)
            dve.wait_ge(bc_ready, 10)
            for k in range(KT):
                dve.scalar_tensor_tensor(H[:, k, :], X[:, k, :], column(V_FINAL + k), bank[7][:, :],
                                         ALU.mult, ALU.mult).then_inc(out_ready, 1)

        @block.gpsimd
        def _(pool):
            pool.wait_ge(x_loaded[3], 16)
            pool.dma_start(CT, c_pad).then_inc(ct_in, 16)
            for q in range(PPB):
                pool.dma_start(BL[q], b_pad[q]).then_inc(bl_full[q], 16)
            for q in range(PPB):
                op = pool.memset(CL[q], 0.0)
            pool.drain()
            pool.sem_inc(cl_zero, 1)
            pool.sem_inc(y_done, 4)
            pool.sem_inc(da_pv, 2)
            pool.sem_inc(at_turned, 2)
            pool.sem_inc(at_pv, 2)
            for s in range(2):
                weight_lo(pool, Q_U, s, W_HEADS)
            pool.wait_ge(const_ready, 1)
            norm_root(pool, 0)
            for s in (2, 3):
                weight_lo(pool, Q_U, s, W_HEADS)
            for quad in (Q_U + 1, Q_HEAD):
                for s in range(4):
                    weight_lo(pool, quad, s, W_HEADS)

            def table(b, q):
                n = 4 * b + q

                def part(tab, c):
                    if isinstance(b, int):
                        return tab[:, n, c, :]
                    return tab[:, bass.ds(n, 1), c, :].rearrange("p a i -> p (a i)")

                hi = [part(HIT, c).rearrange("p (j i) -> p j i", i=1).to_broadcast([P, HI, LO]) for c in range(2)]
                lo = [part(LOT, c).rearrange("p (j i) -> p j i", j=1).to_broadcast([P, HI, LO]) for c in range(2)]
                to = [x.rearrange("p (j i) -> p j i", j=HI) for x in (*ROT[q % 2], *PTMP)]
                pool.wait_ge(ss_ready, n + 1)
                pool.tensor_tensor(to[0], hi[0], lo[0], ALU.mult)
                pool.tensor_tensor(to[2], hi[1], lo[1], ALU.mult)
                pool.tensor_tensor(to[1], hi[1], lo[0], ALU.mult)
                pool.tensor_tensor(to[3], hi[0], lo[1], ALU.mult)
                pool.drain()
                pool.tensor_tensor(to[0], to[0], to[2], ALU.subtract)
                pool.tensor_tensor(to[1], to[1], to[3], ALU.add).then_inc(tab_ready, 1)
                pool.drain()

            def rope_products(hd):
                for s in range(2):
                    pool.wait_ge(evac_done[s], hd + (Q_HEAD + 1))
                for raw, swapped in ((QRAW, QSW), (KRAW, KSW)):
                    pool.tensor_tensor(raw, raw, COS, ALU.mult)
                    pool.tensor_tensor(swapped, swapped, SIN, ALU.mult)

            def rope_sums(hd):
                pool.drain()
                if not isinstance(hd, int):
                    pool.wait_ge(da_scores, 8 * hd)
                pool.tensor_tensor(QH, QRAW, QSW, ALU.add)
                pool.tensor_tensor(KH, KRAW, KSW, ALU.add).then_inc(rope_done, 1)

            def next_input(b, q):
                pool.wait_ge(bu_ready, 4 * b + q + 1)
                src = b_pad[4 * b + q + 4] if isinstance(b, int) else \
                    b_pad[bass.ds(4 * b + q + 4, 1)].rearrange("a p c m -> (a p) c m")
                pool.dma_start(BL[q], src).then_inc(bl_full[q], 16)

            def head_body(b, last):
                table(b, 1)
                if not last:
                    next_input(b, 0)
                table(b, 2)
                if not last:
                    weight_lo(pool, b + (Q_HEAD + 1), 2, W_HEADS)
                    next_input(b, 1)
                    rope_products(b + 1)
                    weight_lo(pool, b + (Q_HEAD + 1), 3, W_HEADS)
                table(b, 3)
                if not last:
                    next_input(b, 2)
                    weight_lo(pool, b + (Q_HEAD + 2), 0, W_HEADS)
                    table(b + 1, 0)
                    next_input(b, 3)
                    weight_lo(pool, b + (Q_HEAD + 2), 1, W_HEADS)
                    rope_sums(b + 1)

            pool.wait_ge(rope1_in, 16)
            rope_products(0)
            rope_sums(0)
            for s in range(2):
                weight_lo(pool, Q_HEAD + 1, s, W_HEADS)
            pool.wait_ge(prep_done, 1)
            table(0, 0)
            heads(pool, head_body)
            pool.wait_ge(ss_ready, PAIRS + 2)
            pool.dma_start(MEMRAW, mem_in).then_inc(mem_loaded, 16)
            pool.wait_ge(da_scores, 8 * HEADS)
            pool.dma_start(TAB[:, :], rope2).then_inc(rope2_in, 16)
            pool.wait_ge(da_pv, 4 * HEADS + 2)
            weight_lo(pool, Q_GB, 2)
            weight_lo(pool, Q_GB, 3)
            weight_lo(pool, Q_GB + 1, 0)
            weight_lo(pool, Q_GB + 1, 1)
            pool.wait_ge(hvar_ready, 1)
            root(pool, HVAR, HR0, HRT, HRS).then_inc(hrs_ready, 1)
            weight_lo(pool, Q_GB + 1, 2)
            norm_root(pool, 1, 2)
            weight_lo(pool, Q_GB + 1, 3)
            weight_lo(pool, Q_GLU, 0)
            weight_lo(pool, Q_GLU, 1)
            for s in range(4):
                pool.wait_ge(mm_done[s], Q_GLU)
            pool.dma_start(X, x_in).then_inc(x_again, 16)
            weight_lo(pool, Q_GLU, 2)
            weight_lo(pool, Q_GLU, 3)

            def weights_lo(first, last):
                with pool.Fori(first, last) as quad:
                    for s in range(4):
                        weight_lo(pool, quad, s)

            def root_within(quad, *norms):
                for s in range(2):
                    weight_lo(pool, quad, s)
                for n in norms:
                    norm_root(pool, n)
                for s in (2, 3):
                    weight_lo(pool, quad, s)

            weights_lo(Q_GLU + 1, Q_KX)
            root_within(Q_KX, 2)
            weights_lo(Q_KX + 1, Q_VX + 1)
            root_within(Q_VX + 1, 3)
            weights_lo(Q_XQ, Q_FF)
            root_within(Q_FF, 4, 5)
            weights_lo(Q_FF + 1, Q_L2)
            norm_root(pool, 6)
            with pool.Fori(0, LAYERS) as L:
                q0 = pool.snap(QL * L + Q_L2)
                norm_root(pool, L + 7)
                for s in range(4):
                    weight_lo(pool, q0, s)
                with pool.Fori(0, QL - 1) as i:
                    quad = pool.snap(q0 + i + 1)
                    for s in range(4):
                        weight_lo(pool, quad, s)
            norm_root(pool, 9)


def tables():
    f = np.float32

    def angles(theta, half, dim):
        inv = (f(theta) ** (-np.arange(half, dtype=f) * f(2.0) / f(dim))).astype(f)
        return (np.arange(T, dtype=f)[None, :] * inv[:, None]).astype(f)

    a1 = angles(10000.0, DH // 2, DH)
    cos1, sin1 = np.cos(a1).astype(f), np.sin(a1).astype(f)
    rope1 = np.concatenate([np.tile(cos1, (4, 1)), np.concatenate([-sin1, sin1] * 2, 0)], 1)
    a2 = angles(500000.0, 8, 16)
    cos2, sin2 = np.cos(a2).astype(f), np.sin(a2).astype(f)
    c = np.concatenate([cos2, cos2, np.ones((48, T), f)], 0)
    s = np.concatenate([-sin2, sin2, np.zeros((48, T), f)], 0)
    rope2 = np.concatenate([np.tile(c, (2, 1)), np.tile(s, (2, 1))], 1)

    con = np.zeros((P, C_END), f)
    con[:, C_ID:C_ID + P] = np.eye(P, dtype=f)
    i, j = np.arange(P)[:, None], np.arange(P)[None, :]
    con[:, C_CAUSAL:C_CAUSAL + P] = np.where(j > i, MASKED, 0)
    con[:, C_CHUNK:C_CHUNK + P] = np.where(j // 64 > i // 64, MASKED, 0)
    for base in (0, 64):
        for d in range(16):
            con[base + d, C_SWAP + base + (d + 8) % 16] = 1
    ends = np.arange(NC) * CMP_STRIDE + CMP_LEN - 1
    for t in range(TT):
        tok = t * P + np.arange(P)
        con[:, C_CMP + 32 * t:C_CMP + 32 * t + NC] = np.where(ends[None, :] <= tok[:, None], 0, MASKED)
        con[:, C_VALID + t] = tok >= ends[0]
    for h in range(4):
        con[32 * h, C_FQ] = 1
        con[32 * h + 1, C_FK] = 1
        con[32 * h + 1, C_NFK] = -1
    for blk in range(2):
        for half in range(2):
            w = (2, 4, 8, 16)[2 * blk + half]
            rows = slice(64 * half, 64 * half + 64)
            con[rows, C_W + blk] = 1 / w
            con[rows, C_INV + 16 * blk:C_INV + 16 * blk + 16] = 1 / np.minimum(np.arange(1, 17), w)
    return rope1.astype(f), rope2.astype(f), con


def stream(w):
    k, n = w.shape
    return w.reshape(k // P, P, n // P, P).transpose(2, 1, 0, 3)


def by_partition(v):
    return v.reshape(-1, P).T


def kernel(x, mem, norm_mix_pre, w_in, b_gate, ssm_lambda_re, ssm_lambda_im, ssm_log_dt,
           ssm_b_re, ssm_b_im, ssm_c_re, ssm_c_im, ssm_d, w_glu, b_glu, w_ssm_proj,
           da_lambda_q1, da_lambda_k1, da_lambda_q2, da_lambda_k2, da_head_norm, w_da_proj,
           w_mix_out, norm_mix_post, norm_x_pre, norm_mem, w_xq, w_xkv, w_xo, norm_x_post,
           norm_ff_pre, w_ff1, w_ff2, norm_ff_post, norm_g_2, w_in_2, fox_f_bias_2, cmp_pos_2,
           cmp_w1_2, cmp_b1_2, cmp_w2_2, cmp_b2_2, pool_w_2, pool_scale_2, conv_w_2, w_branch_2,
           w_out_2, final_norm_g_2):
    import concourse.bacc as bacc
    from concourse.bass_utils import run_bass_kernel_spmd

    f = np.float32
    npa = lambda a: np.asarray(a)
    cat = np.concatenate

    wi = stream(npa(w_in)[0])
    u_blk, q_blk, k_blk, v_blk, ga, gb = (wi[i * 8:(i + 1) * 8] for i in range(6))
    per_head = np.stack([q_blk, k_blk, ga, v_blk], 1).reshape(32, P, KT, P)
    wkv = stream(npa(w_xkv)[0])
    ff1, ff2 = stream(npa(w_ff1)[0]), stream(npa(w_ff2)[0])
    ff = [ff1[KT * c:KT * c + KT] if which == 1 else ff2[:, :, KT * c:KT * c + KT] for which, c in FF_ORDER]
    parts = [u_blk, per_head, gb, stream(npa(w_glu)[0]), stream(npa(w_da_proj)[0]),
             stream(npa(w_ssm_proj)[0]), stream(npa(w_mix_out)[0]), wkv, stream(npa(w_xq)[0]),
             stream(npa(w_xo)[0])] + ff
    kv0, pool0, conv0, fox0, gate0, merge0 = 256, 652, 908, 1676, 2448, 3472
    r = lambda a, n: list(range(a, a + n))
    kvc = lambda i: r(kv0 + 64 * i, 64)
    small = [-1] * P
    for h in range(4):
        small[32 * h] = small[32 * h + 1] = 2444 + h
    for g in range(12):
        small[2 + g] = 640 + g
    cols = (r(0, 256) + kvc(2) + kvc(4) + kvc(0) + kvc(1) + kvc(3) + kvc(5) + small
            + r(fox0, 768) + r(pool0, 256) + r(conv0, 768) + r(gate0, 1024))
    for ob in range(8):
        for i in range(4):
            cols += r(merge0 + i * D + ob * P, P)
    cols = np.array(cols)
    for l in range(LAYERS):
        w = npa(w_in_2)[l]
        w = cat([w, np.zeros((D, 1), w.dtype)], 1)[:, cols]
        parts.append(stream(w))
        parts.append(npa(w_branch_2)[l].reshape(4, 2, P, 8, P).transpose(3, 2, 0, 1, 4).reshape(8, P, KT, P))
        parts.append(stream(npa(w_out_2)[l]))
    weights = np.ascontiguousarray(cat(parts, 0))
    assert weights.shape[0] == 4 * Q_END

    pad64 = lambda v: cat([npa(v)[0], np.zeros(64, f)])[:, None]
    state = lambda a: npa(a)[0].reshape(PAIRS, P).T
    ldt = np.repeat(npa(ssm_log_dt)[0], STATE).reshape(PAIRS, P).T
    vecs = cat([by_partition(npa(norm_mix_pre)[0]), by_partition(npa(b_gate)[0]), by_partition(npa(ssm_d)[0]),
                by_partition(npa(b_glu)[0]), by_partition(npa(norm_mix_post)[0]), by_partition(npa(norm_x_pre)[0]),
                by_partition(npa(norm_mem)[0]), by_partition(npa(norm_x_post)[0]), by_partition(npa(norm_ff_pre)[0]),
                by_partition(npa(norm_ff_post)[0]), npa(da_head_norm)[0][:, None],
                pad64(da_lambda_q1), pad64(da_lambda_k1), pad64(da_lambda_q2), pad64(da_lambda_k2),
                by_partition(npa(final_norm_g_2)), state(ssm_lambda_re), state(ssm_lambda_im), ldt], 1)

    b_pad = np.zeros((PAIRS, P, 2, P), f)
    c_pad = np.zeros((P, PAIRS, 2, 32), f)
    for n in range(PAIRS):
        for g2 in range(2):
            rows = slice(32 * (n % 4) + 16 * g2, 32 * (n % 4) + 16 * g2 + 16)
            st = slice(64 * g2, 64 * g2 + 64)
            for c, (b, cc) in enumerate(((ssm_b_re, ssm_c_re), (ssm_b_im, ssm_c_im))):
                b_pad[n, rows, c, st] = npa(b)[0, 2 * n + g2].T
                c_pad[st, n, c, 16 * g2:16 * g2 + 16] = npa(cc)[0, 2 * n + g2].T

    lv = np.zeros((LAYERS, P, L_END), f)
    pw = np.zeros((LAYERS, P, 2, P), f)
    for l in range(LAYERS):
        lv[l, :, L_NORM:L_NORM + 8] = by_partition(npa(norm_g_2)[l])
        lv[l, :, L_POOL:L_POOL + 2] = by_partition(npa(pool_scale_2)[l])
        for tap in range(3):
            lv[l, :, L_CONV + 2 * tap:L_CONV + 2 * tap + 2] = by_partition(npa(conv_w_2)[l, tap])
        for h in range(4):
            lv[l, 32 * h:32 * h + 2, L_FBIAS] = npa(fox_f_bias_2)[l, h]
        lv[l, :, L_B1:L_B1 + 2] = npa(cmp_b1_2)[l].T
        for half in (0, 64):
            lv[l, half:half + 64, L_B2K] = npa(cmp_b2_2)[l, 0]
        for i in range(4):
            rows = slice(64 * (i % 2), 64 * (i % 2) + 64)
            pw[l, rows, i // 2, rows] = npa(pool_w_2)[l, i]
    cw1 = npa(cmp_w1_2).reshape(LAYERS, 2, CMP_LEN, 64, P).transpose(0, 1, 3, 2, 4).reshape(LAYERS, P, CMP_LEN * P)
    pos = npa(cmp_pos_2).transpose(0, 1, 3, 2).reshape(LAYERS, P, CMP_LEN)
    w2k = cat([npa(cmp_w2_2)[:, 0]] * 2, 2)
    w2v = npa(cmp_w2_2)[:, 1]
    b2v = npa(cmp_b2_2)[:, 1:2]
    rope1, rope2, con = tables()

    feat = lambda a: npa(a)[0].T.reshape(KT, P, -1).transpose(1, 0, 2)
    arrays = {
        "x_in": feat(x), "mem_in": feat(mem), "weights": weights, "vecs": vecs, "lvecs": lv, "consts": con,
        "rope1": rope1, "rope2": rope2, "b_pad": b_pad, "c_pad": c_pad, "cmp_w1": cw1, "cmp_pos": pos,
        "cmp_w2k": w2k, "cmp_w2v": w2v, "cmp_b2v": b2v, "pool_w": pw.reshape(LAYERS, P, 2 * P),
    }
    arrays = {k: np.ascontiguousarray(v) for k, v in arrays.items()}
    nc = bacc.Bacc("TRN2", target_bir_lowering=False, num_devices=1)
    args = {k: nc.dram_tensor(k, v.shape, mybir.dt.from_np(v.dtype), kind="ExternalInput").ap()
            for k, v in arrays.items()}
    out = nc.dram_tensor("out", (P, KT, T), F32, kind="ExternalOutput").ap()
    build(nc, out=out, **args)
    res = run_bass_kernel_spmd(nc, [arrays], core_ids=[0])
    got = res.results[0]["out"]
    return got.transpose(2, 1, 0).reshape(1, T, D)
```
